# Optimizing a Trainium2 kernel written in Bass

```python
import math
import jax, jax.numpy as jnp
from jax import lax
import numpy as np

D_MODEL = 1024
BATCH = 1
SEQ = 1024
DEPTH = 2

CHUNK = 64
N_A_LAYERS = DEPTH // 2
N_B_LAYERS = DEPTH - N_A_LAYERS
SSM_GROUP = 16
N_GROUPS = D_MODEL // SSM_GROUP
SSM_STATE = 64
DT_MIN = 1e-3
DT_MAX = 1e-1
N_HEADS = 8
HEAD_DIM = 64
V_DIM = 2 * HEAD_DIM
ROT_DIM = HEAD_DIM // 4
ROPE_THETA = 500000.0
Q_BLOCK = 128
LAMBDA_INIT_STD = 0.1
FFN_HIDDEN = ((8 * D_MODEL + 3 * 256 - 1) // (3 * 256)) * 256
EPS = 1e-6

kernel_name = "s5_then_shared_kv_diff_attention_trunk"

def rmsnorm(x, g):
    xf = x.astype(jnp.float32)
    xf = xf * lax.rsqrt(jnp.mean(xf * xf, axis=-1, keepdims=True) + EPS)
    return (xf * g.astype(jnp.float32)).astype(x.dtype)

def apply_partial_rope(x, pos):
    half = ROT_DIM // 2
    inv_freq = ROPE_THETA ** (-jnp.arange(half, dtype=jnp.float32) * 2.0 / ROT_DIM)
    ang = pos.astype(jnp.float32)[:, None] * inv_freq[None, :]
    cos = jnp.cos(ang)[None, :, None, :]
    sin = jnp.sin(ang)[None, :, None, :]
    xf = x.astype(jnp.float32)
    x1 = xf[..., :half]
    x2 = xf[..., half:ROT_DIM]
    rest = xf[..., ROT_DIM:]
    return jnp.concatenate([x1 * cos - x2 * sin, x2 * cos + x1 * sin, rest], axis=-1)

def swiglu(hn, w1, w3, w2):
    return (jax.nn.silu(hn @ w1) * (hn @ w3)) @ w2

def _cdiag_combine(e1, e2):
    a1r, a1i, b1r, b1i = e1
    a2r, a2i, b2r, b2i = e2
    return (a2r * a1r - a2i * a1i,
            a2r * a1i + a2i * a1r,
            a2r * b1r - a2i * b1i + b2r,
            a2r * b1i + a2i * b1r + b2i)

def s5_mixer(u, lam_re, lam_im, log_dt, b_re, b_im, c_re, c_im, d_skip, w_glu):
    f32 = jnp.float32
    bsz, L, _ = u.shape
    uf = u.astype(f32)
    lr, li = lam_re.astype(f32), lam_im.astype(f32)
    dt = jnp.exp(log_dt.astype(f32))[:, None]
    mag = jnp.exp(lr * dt)
    abar_re, abar_im = mag * jnp.cos(li * dt), mag * jnp.sin(li * dt)
    nr, ni = abar_re - 1.0, abar_im
    den = lr * lr + li * li
    fr = (nr * lr + ni * li) / den
    fi = (ni * lr - nr * li) / den
    br, bi = b_re.astype(f32), b_im.astype(f32)
    bb_re = fr[..., None] * br - fi[..., None] * bi
    bb_im = fr[..., None] * bi + fi[..., None] * br
    ug = uf.reshape(bsz, L, N_GROUPS, SSM_GROUP)
    bu_re = jnp.einsum('blgc,gpc->blgp', ug, bb_re)
    bu_im = jnp.einsum('blgc,gpc->blgp', ug, bb_im)
    a_re = jnp.broadcast_to(abar_re, bu_re.shape)
    a_im = jnp.broadcast_to(abar_im, bu_im.shape)
    _, _, s_re, s_im = lax.associative_scan(_cdiag_combine, (a_re, a_im, bu_re, bu_im), axis=1)
    y = (jnp.einsum('blgp,gcp->blgc', s_re, c_re.astype(f32))
         - jnp.einsum('blgp,gcp->blgc', s_im, c_im.astype(f32)))
    y = y.reshape(bsz, L, D_MODEL) + d_skip.astype(f32) * uf
    z = jax.nn.gelu(y)
    za, zb = jnp.split(z @ w_glu.astype(f32), 2, axis=-1)
    return (za * jax.nn.sigmoid(zb)).astype(u.dtype)

def shared_kv(h, kv_norm_g, w_kv, pos):
    bsz, L, _ = h.shape
    kv = rmsnorm(h, kv_norm_g) @ w_kv
    hk = N_HEADS * HEAD_DIM
    k1 = kv[..., :hk].reshape(bsz, L, N_HEADS, HEAD_DIM)
    k2 = kv[..., hk:2 * hk].reshape(bsz, L, N_HEADS, HEAD_DIM)
    v = kv[..., 2 * hk:].reshape(bsz, L, N_HEADS, V_DIM).astype(jnp.float32)
    return apply_partial_rope(k1, pos), apply_partial_rope(k2, pos), v

def diff_attention(hn, k1, k2, v, w_q, lq1, lk1, lq2, lk2, subln_g, w_o, lam_init, pos):
    f32 = jnp.float32
    bsz, L, _ = hn.shape
    hq = N_HEADS * HEAD_DIM
    q = hn @ w_q
    q1 = apply_partial_rope(q[..., :hq].reshape(bsz, L, N_HEADS, HEAD_DIM), pos)
    q2 = apply_partial_rope(q[..., hq:].reshape(bsz, L, N_HEADS, HEAD_DIM), pos)
    lam = (jnp.exp(jnp.sum(lq1.astype(f32) * lk1.astype(f32)))
           - jnp.exp(jnp.sum(lq2.astype(f32) * lk2.astype(f32))) + lam_init)
    nblk = L // Q_BLOCK
    q1b = q1.reshape(bsz, nblk, Q_BLOCK, N_HEADS, HEAD_DIM).transpose(1, 0, 2, 3, 4)
    q2b = q2.reshape(bsz, nblk, Q_BLOCK, N_HEADS, HEAD_DIM).transpose(1, 0, 2, 3, 4)
    qpos = pos.reshape(nblk, Q_BLOCK)
    k_chunk = pos // CHUNK
    scale = HEAD_DIM ** -0.5

    def block(args):
        q1c, q2c, qp = args
        mask = (k_chunk[None, :] <= (qp // CHUNK)[:, None])[None, None]
        s1 = jnp.einsum('bqhd,bkhd->bhqk', q1c, k1) * scale
        s2 = jnp.einsum('bqhd,bkhd->bhqk', q2c, k2) * scale
        p1 = jax.nn.softmax(jnp.where(mask, s1, -jnp.inf), axis=-1)
        p2 = jax.nn.softmax(jnp.where(mask, s2, -jnp.inf), axis=-1)
        return jnp.einsum('bhqk,bkhe->bqhe', p1 - lam * p2, v)

    o = lax.map(block, (q1b, q2b, qpos))
    o = o.transpose(1, 0, 2, 3, 4).reshape(bsz, L, N_HEADS, V_DIM)
    o = rmsnorm(o, subln_g) * (1.0 - lam_init)
    return o.reshape(bsz, L, N_HEADS * V_DIM).astype(hn.dtype) @ w_o

def setup_inputs(seed: int = 0) -> dict:
    key = jax.random.key(seed)
    ks = jax.random.split(key, 32)
    f32 = jnp.float32
    D, F, G, P, C = D_MODEL, FFN_HIDDEN, N_GROUPS, SSM_STATE, SSM_GROUP
    nrm = lambda k, shape, s: jax.random.normal(k, shape, f32) * s
    x = jax.random.normal(ks[0], (BATCH, SEQ, D), f32)
    norm_mix_g = 1.0 + nrm(ks[1], (DEPTH, D), 0.02)
    norm_ffn_g = 1.0 + nrm(ks[2], (DEPTH, D), 0.02)
    ffn_w1 = nrm(ks[3], (DEPTH, D, F), D ** -0.5)
    ffn_w3 = nrm(ks[4], (DEPTH, D, F), D ** -0.5)
    ffn_w2 = nrm(ks[5], (DEPTH, F, D), F ** -0.5)
    ssm_lam_re = -0.5 + nrm(ks[6], (N_A_LAYERS, G, P), 0.01)
    ssm_lam_im = math.pi * jnp.arange(P, dtype=f32)[None, None, :] + nrm(ks[7], (N_A_LAYERS, G, P), 0.01)
    ssm_log_dt = jax.random.uniform(ks[8], (N_A_LAYERS, G), f32, math.log(DT_MIN), math.log(DT_MAX))
    ssm_b_re = nrm(ks[9], (N_A_LAYERS, G, P, C), (0.5 / C) ** 0.5)
    ssm_b_im = nrm(ks[10], (N_A_LAYERS, G, P, C), (0.5 / C) ** 0.5)
    ssm_c_re = nrm(ks[11], (N_A_LAYERS, G, C, P), (0.5 / P) ** 0.5)
    ssm_c_im = nrm(ks[12], (N_A_LAYERS, G, C, P), (0.5 / P) ** 0.5)
    ssm_d = nrm(ks[13], (N_A_LAYERS, D), 1.0)
    ssm_w_glu = nrm(ks[14], (N_A_LAYERS, D, 2 * D), D ** -0.5)
    kv_norm_g = 1.0 + nrm(ks[15], (D,), 0.02)
    w_kv = nrm(ks[16], (D, 2 * N_HEADS * HEAD_DIM + N_HEADS * V_DIM), D ** -0.5)
    attn_w_q = nrm(ks[17], (N_B_LAYERS, D, 2 * N_HEADS * HEAD_DIM), D ** -0.5)
    attn_lq1 = nrm(ks[18], (N_B_LAYERS, HEAD_DIM), LAMBDA_INIT_STD)
    attn_lk1 = nrm(ks[19], (N_B_LAYERS, HEAD_DIM), LAMBDA_INIT_STD)
    attn_lq2 = nrm(ks[20], (N_B_LAYERS, HEAD_DIM), LAMBDA_INIT_STD)
    attn_lk2 = nrm(ks[21], (N_B_LAYERS, HEAD_DIM), LAMBDA_INIT_STD)
    attn_subln_g = 1.0 + nrm(ks[22], (N_B_LAYERS, V_DIM), 0.02)
    attn_w_o = nrm(ks[23], (N_B_LAYERS, N_HEADS * V_DIM, D), (N_HEADS * V_DIM) ** -0.5)
    final_norm_g = 1.0 + nrm(ks[24], (D,), 0.02)
    return {"x": x, "norm_mix_g": norm_mix_g, "norm_ffn_g": norm_ffn_g,
            "ffn_w1": ffn_w1, "ffn_w3": ffn_w3, "ffn_w2": ffn_w2,
            "ssm_lam_re": ssm_lam_re, "ssm_lam_im": ssm_lam_im, "ssm_log_dt": ssm_log_dt,
            "ssm_b_re": ssm_b_re, "ssm_b_im": ssm_b_im, "ssm_c_re": ssm_c_re, "ssm_c_im": ssm_c_im,
            "ssm_d": ssm_d, "ssm_w_glu": ssm_w_glu, "kv_norm_g": kv_norm_g, "w_kv": w_kv,
            "attn_w_q": attn_w_q, "attn_lq1": attn_lq1, "attn_lk1": attn_lk1,
            "attn_lq2": attn_lq2, "attn_lk2": attn_lk2, "attn_subln_g": attn_subln_g,
            "attn_w_o": attn_w_o, "final_norm_g": final_norm_g}

def reference(x, norm_mix_g, norm_ffn_g, ffn_w1, ffn_w3, ffn_w2,
              ssm_lam_re, ssm_lam_im, ssm_log_dt, ssm_b_re, ssm_b_im, ssm_c_re, ssm_c_im,
              ssm_d, ssm_w_glu, kv_norm_g, w_kv,
              attn_w_q, attn_lq1, attn_lk1, attn_lq2, attn_lk2, attn_subln_g, attn_w_o,
              final_norm_g):
    L = x.shape[1]
    pos = jnp.arange(L, dtype=jnp.int32)
    h = x
    k1 = k2 = v = None
    for l in range(DEPTH):
        hn = rmsnorm(h, norm_mix_g[l])
        if l < N_A_LAYERS:
            h = h + s5_mixer(hn, ssm_lam_re[l], ssm_lam_im[l], ssm_log_dt[l],
                             ssm_b_re[l], ssm_b_im[l], ssm_c_re[l], ssm_c_im[l],
                             ssm_d[l], ssm_w_glu[l])
        else:
            if l == N_A_LAYERS:
                k1, k2, v = shared_kv(h, kv_norm_g, w_kv, pos)
            j = l - N_A_LAYERS
            lam_init = 0.8 - 0.6 * math.exp(-0.3 * l)
            h = h + diff_attention(hn, k1, k2, v, attn_w_q[j], attn_lq1[j], attn_lk1[j],
                                   attn_lq2[j], attn_lk2[j], attn_subln_g[j], attn_w_o[j],
                                   lam_init, pos)
        h = h + swiglu(rmsnorm(h, norm_ffn_g[l]), ffn_w1[l], ffn_w3[l], ffn_w2[l])
    return rmsnorm(h, final_norm_g)


_drawn_inputs = setup_inputs


def setup_inputs(seed=0):
    import zlib

    import numpy as np

    out = dict(_drawn_inputs(seed))
    spreads = {}
    factors = {'norm_mix_g': 3.602,
     'norm_ffn_g': 2.805,
     'ssm_lam_re': 8.0,
     'ssm_b_re': 3.17,
     'ssm_b_im': 3.132,
     'ssm_c_re': 3.2,
     'ssm_c_im': 3.137,
     'kv_norm_g': 4.379,
     'attn_lq2': 2.748,
     'attn_subln_g': 6.477,
     'final_norm_g': 2.853}
    for name, (base, spread) in spreads.items():
        noise = np.random.default_rng([zlib.crc32(name.encode()), seed]).standard_normal(out[name].shape)
        drawn = base * np.exp(spread * noise) if base else spread * noise
        out[name] = __import__('jax').numpy.asarray(drawn.astype(out[name].dtype))
    for name, factor in factors.items():
        out[name] = (out[name] * factor).astype(out[name].dtype)
    return out
```

```python
import math
from contextlib import ExitStack

import concourse.bass as bass
import numpy as np
from concourse import mybir

F32 = mybir.dt.float32
F32R = mybir.dt.float32r
ALU = mybir.AluOpType
ACT = mybir.ActivationFunctionType
AX = mybir.AxisListType

P = 128
L = 1024
D = 1024
KT = D // P
F = 2816
FP = F // 256
T = 8
NC = L // T
CH = 16
NG = D // CH
NP = NG // 2
HP = NP // 2
R = 8
M = NC // R
NH = 8
VD = 128
EPS = 1e-6
SCALE = 64 ** -0.5
LAM_INIT = 0.8 - 0.6 * math.exp(-0.3)
NEG = -3.0e38
TWO_PI = (6.28125, 0.0019350051879882812, 3.0199159819e-07)
MAGIC = 1.5 * 2 ** 23
PI_F = 3.1415925


def trunk(nc, a, out):
    base = (nc.sbuf_base + 31) // 32 * 32

    def sb(name, shape, kb, dt=F32):
        return nc.alloc_sbuf_tensor_at(name, shape, dt, offset=base + int(kb * 1024))

    ident = sb("ident", [P, P], 0)
    ones = sb("ones", [P, 1], 0.5)
    gains = sb("gains", [P, 5, KT], 0.53125)
    subg = sb("subg", [P, 1], 0.75)
    cos_t = sb("cos_t", [P, KT, 8], 1)
    sin_t = sb("sin_t", [P, KT, 8], 1.25)
    lamv = sb("lamv", [P, 4, 64], 1.5)
    lamp = sb("lamp", [P, 2, 64], 2.5)
    lams = sb("lams", [P, 4], 3)
    ms = sb("ms", [P, 8], 3.03125)
    rt = sb("rt", [P, 8], 3.0625)
    rs = sb("rs", [P, 8], 3.09375)
    mx = sb("mx", [P, 16], 3.125)
    nb = sb("nb", [P, 16], 3.1875)
    es = sb("es", [P, 16], 3.25)
    er = sb("er", [P, 16], 3.3125)
    ec = sb("ec", [P, 8], 3.375)
    h = sb("h", [P, KT, L], 4)
    x_hi = sb("x_hi", [P, KT, L], 36, F32R)
    x_lo = sb("x_lo", [P, KT, L], 68, F32R)
    wa = [sb("wa_hi", [P, KT, 256], 100, F32R), sb("wa_lo", [P, KT, 256], 108, F32R)]
    wb = [sb("wb_hi", [P, KT, 256], 116, F32R), sb("wb_lo", [P, KT, 256], 124, F32R)]
    wc = [sb("wc_hi", [P, 2, D], 132, F32R), sb("wc_lo", [P, 2, D], 140, F32R)]
    raw_a = sb("raw_a", [P, KT, 256], 148)
    raw_b = sb("raw_b", [P, KT, 256], 156)
    raw_c = sb("raw_c", [P, 2, D], 164)
    hid = [sb("hid_hi", [P, 2, L], 172, F32R), sb("hid_lo", [P, 2, L], 180, F32R)]
    tmp = [sb("tmp0", [P, L], 188), sb("tmp1", [P, L], 192), sb("tmp2", [P, L], 196)]
    stg = [sb("stg_a", [P, KT, 256], 172), sb("stg_b", [P, KT, 256], 180)]
    rtmp = [sb(f"rope{n}", [P, KT, 4, 8], 188 + n) for n in range(4)]
    E = [[sb(f"e{s}{q}", [P, L], 100 + 8 * s + 4 * q) for q in range(2)] for s in range(2)]
    kst = sb("kst", [P, 2, L], 116, F32R)
    q_hi = sb("q_hi", [P, 2, L], 124, F32R)
    q_lo = sb("q_lo", [P, 2, L], 132, F32R)
    v_hi = sb("v_hi", [P, KT, VD], 140, F32R)
    v_lo = sb("v_lo", [P, KT, VD], 144, F32R)
    kraw = sb("kraw", [P, KT, 2, 2, 64], 188)
    qraw = sb("qraw", [P, KT, 2, 2, 64], 148)
    vraw = sb("vraw", [P, KT, VD], 156)
    pt_hi = sb("pt_hi", [P, KT, 256], 160, F32R)
    pt_lo = sb("pt_lo", [P, KT, 256], 168, F32R)
    otf = sb("otf", [P, L], 176)
    osq = sb("osq", [P, L], 180)
    onf = sb("onf", [P, L], 184)
    u = sb("u", [P, NG, NC], 172)
    wr = sb("wr", [P, HP, T, CH], 36)
    wi = sb("wi", [P, HP, T, CH], 44)
    cr = sb("cr", [P, HP, T + 1, CH], 52)
    cn = sb("cn", [P, HP, T + 1, CH], 61)
    wt = sb("wt", [P, HP, 2, P], 70)
    gt = sb("gt", [P, 2 * HP, P], 86)
    st = sb("st", [P, HP, 2, NC + 1], 102)
    z = sb("z", [P, 2, T, D // 2], 119)
    w4 = sb("w4", [P, HP, 2, 4, 2 * CH], 135)
    ta = sb("ta", [P, HP, 2, M], 151)
    tb = sb("tb", [P, HP, 2, M], 153)
    b_raw = [sb("b_re", [P, NP, CH], 155), sb("b_im", [P, NP, CH], 157)]
    c_raw = [sb("c_re", [P, NP, CH], 159), sb("c_im", [P, NP, CH], 161)]
    ident4 = sb("ident4", [32, P], 171.5)
    pw_d = sb("pw_d", [P, 2, T + 1, NP], 167)
    pw_a = sb("pw_a", [P, 2, T + 1, NP], 169.25)
    pw_8 = sb("pw_8", [P, 2, R, NP], 204)
    d_two = sb("d_two", [32, NG], 206)
    g_two = sb("g_two", [32, NG], 206.25)
    dd = sb("dd", [32, 2 * HP, 32], 4)
    p1 = sb("p1", [P, HP, T, CH], 8)
    p2 = sb("p2", [P, HP, T, CH], 16)
    bz4 = [sb("bz4_re", [P, HP, 4, 2, CH], 8),
           sb("bz4_im", [P, HP, 4, 2, CH], 16)]
    m1 = sb("m1", [P, HP, T, CH], 24)
    m2 = sb("m2", [P, HP, T, CH], 70)
    part = sb("part", [P, 4, NC], 32)
    ssq = sb("ssq", [P, NC], 34)
    rfull = sb("rfull", [P, NC], 34.5)
    same_j = sb("same_j", [P, P], 35)
    sq = [sb("sq0", [P, 16, NC], 36), sb("sq1", [P, 16, NC], 44)]
    prm = sb("prm", [P, 24, NP], 92)
    g_b = sb("g_b", [P, NP, CH], 96)
    pt4 = [sb(f"pt4_{n}", [P, 4, NP], 102 + n) for n in range(4)]

    scr = nc.dram_tensor("kvq_scratch", [L, 4 * D], F32).ap()

    with ExitStack() as ctx:
        ps = ctx.enter_context(nc.psum_tensor("ps", [P, 8, 512], F32))
        sem = lambda name: ctx.enter_context(nc.semaphore(name))
        consts_in, params_in, h_in = sem("consts_in"), sem("params_in"), sem("h_in")
        bc_in = sem("bc_in")
        u_in = [sem(f"u_in{k}") for k in range(4)]
        sq_done, part_done, ssq_done, rms_pe, rms_ms, rms_rt, rms_rs = map(
            sem, "sq_done part_done ssq_done rms_pe rms_ms rms_rt rms_rs".split())
        u_done, u_pool = sem("u_done"), sem("u_pool")
        dve, act, pool = sem("dve_steps"), sem("act_steps"), sem("pool_steps")
        prm_exp, prm_arg, prm_sin, prm_done = map(sem, "prm_exp prm_arg prm_sin prm_done".split())
        w_hi, w_scaled = sem("w_hi_done"), sem("w_scaled")
        w_tab, c_tab, dd_done = sem("w_tab"), sem("c_tab"), sem("dd_done")
        s5_full, s5_act, s5_dve = sem("s5_full"), sem("s5_act"), sem("s5_dve")
        scan_done, z_hi = sem("scan_done"), sem("z_hi_done")
        a_in, b_in, c_in = sem("a_loaded"), sem("b_loaded"), sem("c_loaded")
        a_rdy, b_rdy, c_rdy = sem("a_split"), sem("b_split"), sem("c_split")
        tile, act_ev, dve_ev = sem("tile_done"), sem("act_evacuated"), sem("dve_evacuated")
        sig_done, h_add = sem("sig_done"), sem("h_added")
        hid_h, hid_l = sem("hid_hi_done"), sem("hid_lo_done")
        nsq, nacc, ncol, nms, nrt, nrs, nbc, nf, nhi, nlo = map(
            sem, "n_sq n_acc n_col n_ms n_rt n_rs n_bcast n_full n_hi n_lo".split())
        roped, stored = sem("roped"), [sem("stored_a"), sem("stored_b")]
        lam_d, lam_e, lam_done = sem("lam_d"), sem("lam_e"), sem("lam_done")
        kq_in, v_in = sem("kq_loaded"), sem("v_loaded")
        kq_tr, kq_hi, kq_lo = sem("kq_transposed"), sem("kq_hi_done"), sem("kq_lo_done")
        vh_done, vl_done = sem("v_hi_done"), sem("v_lo_done")
        sc, masked, mxd, nbd, exd = map(sem, "scores masked max_done negmax exp_done".split())
        er_done, ec_done, e2_done, p_done = map(sem, "er_done ec_done e2_done p_done".split())
        pt_tr, pth, ptz, ptl = map(sem, "pt_transposed pt_hi_done pt_zeroed pt_lo_done".split())
        pv, oc, oq = sem("pv_done"), sem("o_copied"), sem("o_squared")
        ocol, oms, ort, ors, obc, onfd, onh, onl = map(
            sem, "o_col o_ms o_rt o_rs o_bcast o_full o_hi o_lo".split())
        out_done = [sem("out_done0"), sem("out_done1")]

        kinds = []
        for hf in range(2):
            kinds += [(kind, hf, k) for kind in ("wt", "v", "g", "y") for k in range(8)]
        kinds += [("z", 0, k) for k in range(16)]
        by_act = {"wt": True, "g": True, "v": True, "y": True, "z": False}
        number = {key: n for n, key in enumerate(kinds)}

        def evacuated(n):
            mine = by_act[kinds[n][0]]
            return (s5_act if mine else s5_dve), sum(by_act[k[0]] == mine for k in kinds[:n + 1])

        def s5_batches(eng, want, body):
            for n, (kind, hf, k) in enumerate(kinds):
                if (kind, hf) in want:
                    body(n, kind, hf, k)


        N_GLU, N_F0, N_KVQ, N_WO, N_F1 = 0, 4, 4 + FP, 10 + FP, 12 + FP
        FT = 12 * FP
        T_GLU, T_F0, T_KVQ, T_WO, T_F1 = 0, 16, 16 + FT, 28 + FT, 36 + FT
        FA, FD = 2 * FP, 10 * FP
        A_GLU, A_F0, A_KVQ, A_WO, A_F1 = 4, 12, 12 + FA, 24 + FA, 24 + FA
        D_GLU, D_F0, D_KVQ, D_WO, D_F1 = 4, 12, 12 + FD, 12 + FD, 20 + FD

        block = ctx.enter_context(nc.Block())

        @block.sync
        def _(sp):
            for t, name in ((ident, "ident"), (same_j, "same_j"), (ones, "ones"), (gains, "gains"),
                            (ident4, "ident4"), (subg, "subg"), (cos_t, "cos_t"), (sin_t, "sin_t"), (lamv, "lamv")):
                sp.dma_start(t[:], a[name]).then_inc(consts_in, 16)
            sp.dma_start(prm[:, 0:3, :], a["ssm_prm"]).then_inc(params_in, 16)
            for k in range(4):
                sp.dma_start(u[:, 16 * k:16 * k + 16, :], a["x_u"][:, 16 * k:16 * k + 16, :])\
                    .then_inc(u_in[k], 16)
            for t, name in ((b_raw[0], "ssm_b_re"), (b_raw[1], "ssm_b_im"), (c_raw[0], "ssm_c_re"),
                            (c_raw[1], "ssm_c_im"), (g_b, "g_b"), (d_two, "d_two"),
                            (g_two, "g_two")):
                sp.dma_start(t[:], a[name]).then_inc(bc_in, 16)

            def load(t, src, loaded, split, n, first=False):
                if not first:
                    sp.wait_ge(split, 2 * n)
                sp.dma_start(t[:, :, :], src).then_inc(loaded, 16)

            def chunk(name, i):
                return a[name][bass.ds(i, 1), :, :].rearrange("o p c -> p (o c)")\
                    .rearrange("p (k c) -> p k c", c=D if name[:2] == "w2" else 256)

            sp.wait_ge(s5_full, number["y", 1, 7] + 1)
            sp.wait_ge(s5_act, evacuated(number["y", 1, 7])[1])
            load(raw_b, chunk("glu_b", 0), b_in, b_rdy, 0, True)
            sp.wait_ge(s5_full, len(kinds))
            load(raw_a, chunk("glu_a", 0), a_in, a_rdy, 0, True)
            sp.dma_start(h[:, :, :], a["x_t"]).then_inc(h_in, 16)
            with sp.Fori(1, 4) as i:
                load(raw_a, chunk("glu_a", i), a_in, a_rdy, i)
                load(raw_b, chunk("glu_b", i), b_in, b_rdy, i)

            def ffn(layer, n0):
                load(raw_a, chunk(f"w1_{layer}", 0), a_in, a_rdy, n0)
                load(raw_b, chunk(f"w3_{layer}", 0), b_in, b_rdy, n0)
                load(raw_c, chunk(f"w2_{layer}", 0), c_in, c_rdy, layer * FP, layer == 0)
                with sp.Fori(1, FP) as i:
                    load(raw_a, chunk(f"w1_{layer}", i), a_in, a_rdy, i + n0)
                    load(raw_b, chunk(f"w3_{layer}", i), b_in, b_rdy, i + n0)
                    load(raw_c, chunk(f"w2_{layer}", i), c_in, c_rdy, i + layer * FP)

            ffn(0, N_F0)
            load(raw_a, chunk("w_kvq", 0), a_in, a_rdy, N_KVQ)
            load(raw_b, chunk("w_kvq", 1), b_in, b_rdy, N_KVQ)

            def store(c):
                if c // 4 == 1:
                    sp.wait_ge(act_ev, A_KVQ + c + 1)
                else:
                    sp.wait_ge(roped, c + 1 if c < 4 else c - 3)
                sp.dma_start(scr[:, 256 * c:256 * c + 256].rearrange("(k p) c -> p k c", p=P),
                             stg[c % 2][:, :, :]).then_inc(stored[c % 2], 16)

            for i in range(6):
                if i < 5:
                    load(raw_a, chunk("w_kvq", 2 * i + 2), a_in, a_rdy, N_KVQ + i + 1)
                    load(raw_b, chunk("w_kvq", 2 * i + 3), b_in, b_rdy, N_KVQ + i + 1)
                store(2 * i)
                store(2 * i + 1)
            sp.wait_ge(stored[0], 96)
            sp.wait_ge(stored[1], 96)

            def kqv(i, first=False):
                if not first:
                    sp.wait_ge(kq_tr, i * 8)
                for t, c0 in ((kraw, 0), (qraw, 2 * D)):
                    for s, twice in ((0, 0), (0, 1), (1, 0), (1, 1)):
                        sp.dma_start(t[:, :, s, twice, :],
                                     scr[:, bass.ds(i * 64 + (c0 + 512 * s), 64)]
                                     .rearrange("(k p) c -> p k c", p=P)).then_inc(kq_in, 16)
                if not first:
                    sp.wait_ge(vl_done, i)
                sp.dma_start(vraw[:, :, :], scr[:, bass.ds(i * 128 + D, 128)]
                             .rearrange("(k p) c -> p k c", p=P)).then_inc(v_in, 16)

            kqv(0, True)
            with sp.Fori(1, NH) as i:
                kqv(i)
            sp.wait_ge(onl, NH)
            for i in range(2):
                load(raw_a, chunk("w_o", 2 * i), a_in, a_rdy, N_WO + i)
                load(raw_b, chunk("w_o", 2 * i + 1), b_in, b_rdy, N_WO + i)
            ffn(1, N_F1)
            for k in range(KT):
                sp.wait_ge(nf, 24 + k + 1)
                sp.dma_start(out[:, k, :], tmp[k % 2][:, :]).then_inc(out_done[k % 2], 16)
            sp.wait_ge(out_done[0], 16 * KT // 2)
            sp.wait_ge(out_done[1], 16 * KT // 2)

        @block.gpsimd
        def _(pl):
            steps = [0]

            def step(ins):
                steps[0] += 1
                ins.then_inc(pool, 1)
                pl.wait_ge(pool, steps[0])

            pl.wait_ge(rms_rs, 1)
            pl.tensor_tensor(u[:, 44:NG, :], u[:, 44:NG, :],
                             rfull[:, :].unsqueeze(1).to_broadcast([P, NG - 44, NC]), ALU.mult)\
                .then_inc(u_pool, 1)
            pl.wait_ge(bc_in, 112)
            pl.wait_ge(prm_done, 2)
            for hf in range(2):
                half = slice(HP * hf, HP * hf + HP)
                shape = [P, HP, T, CH]
                pr, pi = (pw_a[:, n, 1:T + 1, half].rearrange("p k q -> p q k").unsqueeze(3)
                          .to_broadcast(shape) for n in range(2))
                c_r, c_i = (c_raw[n][:, half, :].unsqueeze(2).to_broadcast(shape) for n in range(2))
                if hf:
                    pl.wait_ge(s5_full, number["y", 0, 7] + 1)
                step(pl.tensor_tensor(p1[:, :, :, :], pr, c_r, ALU.mult))
                step(pl.tensor_tensor(p2[:, :, :, :], pi, c_i, ALU.mult))
                step(pl.tensor_tensor(cr[:, :, 1:T + 1, :], p1[:, :, :, :], p2[:, :, :, :], ALU.subtract))
                step(pl.tensor_tensor(p1[:, :, :, :], pi, c_r, ALU.mult))
                step(pl.tensor_tensor(p2[:, :, :, :], pr, c_i, ALU.mult))
                step(pl.tensor_tensor(p1[:, :, :, :], p1[:, :, :, :], p2[:, :, :, :], ALU.add))
                step(pl.tensor_scalar(cr[:, :, 0, :], c_raw[0][:, half, :], 1.0, None, ALU.mult))
                step(pl.tensor_scalar(cn[:, :, 0, :], c_raw[1][:, half, :], -1.0, None, ALU.mult))
                step(pl.tensor_scalar(cn[:, :, 1:T + 1, :], p1[:, :, :, :], -1.0, None, ALU.mult))
                for n in range(2):
                    b = b_raw[n][:, half, :].unsqueeze(2).to_broadcast([P, HP, 4, CH])
                    pl.tensor_scalar(bz4[n][:, :, :, 0, :], b, 1.0, None, ALU.mult)
                    ins = pl.memset(bz4[n][:, :, :, 1, :], 0.0)
                ins.then_inc(c_tab, 1)

            def split(raw, w, x, loaded, n, ready, used, hi, rows=False, gain=None, sc=None):
                pl.wait_ge(loaded, n * 16 + 16)
                if used is not None:
                    pl.wait_ge(tile, used)
                view = (lambda t: t[:, x:x + 1, :]) if rows else (lambda t: t[:, :, 128 * x:128 * x + 128])
                if gain is not None:
                    g = gains[:, gain, :].unsqueeze(2).to_broadcast([P, KT, 128])
                    pl.tensor_tensor(view(raw), view(raw), g, ALU.mult).then_inc(w_scaled, 1)
                    pl.wait_ge(w_scaled, sc)
                one = ones[:, 0:1].unsqueeze(2).to_broadcast(view(raw).shape)
                pl.tensor_tensor(view(w[0]), view(raw), one, ALU.mult).then_inc(w_hi, 1)
                pl.wait_ge(w_hi, hi)
                pl.tensor_tensor(view(w[1]), view(raw), view(w[0]), ALU.subtract).then_inc(ready, 1)

            def ab(n, free, hi, gain=None, sc=None):
                for k, (raw, w, loaded, ready) in enumerate(
                        ((raw_a, wa, a_in, a_rdy), (raw_b, wb, b_in, b_rdy)) * 2):
                    split(raw, w, k // 2, loaded, n, ready, free[k] if free else None, hi + k,
                          gain=gain, sc=None if gain is None else sc + k)

            ab(N_GLU, None, 1)
            with pl.Fori(1, 4) as i:
                ab(i + N_GLU, [i * 4 + (T_GLU - 3 + k) for k in range(4)], i * 4 + 1)

            def ffn(layer, n0, t0, free, hi0):
                ab(n0, free, hi0)

                def c_chunk(i, hi):
                    for x in range(2):
                        split(raw_c, wc, x, c_in, i + layer * FP, c_rdy, i * 12 + (t0 + 1), hi + x,
                              rows=True)

                with pl.Fori(0, FP - 1) as i:
                    c_chunk(i, i * 6 + (hi0 + 4))
                    ab(i + (n0 + 1), [i * 12 + (t0 + 1 + k) for k in range(4)], i * 6 + (hi0 + 6))
                c_chunk(FP - 1, (FP - 1) * 6 + hi0 + 4)

            ffn(0, N_F0, T_F0, [T_GLU + 13 + k for k in range(4)], 17)
            hi1 = 17 + 6 * FP
            ab(N_KVQ, [T_KVQ - 19, T_KVQ - 10, T_KVQ - 9, T_KVQ - 8], hi1, gain=1, sc=1)
            for i0, i1, gain in ((1, 4, 1), (4, 6, 2)):
                with pl.Fori(i0, i1) as i:
                    ab(i + N_KVQ, [i * 2 + (T_KVQ - 1), i * 2 + T_KVQ] * 2, i * 4 + hi1,
                       gain=gain, sc=i * 4 + 1)

            def head(i):
                pl.wait_ge(v_in, i * 16 + 16)
                if not isinstance(i, int):
                    pl.wait_ge(pv, i * 4)
                pl.tensor_tensor(v_hi[:, :, :], vraw[:, :, :],
                                 ones[:, 0:1].unsqueeze(2).to_broadcast([P, KT, VD]), ALU.mult)\
                    .then_inc(vh_done, 1)
                pl.wait_ge(vh_done, i + 1)
                pl.tensor_tensor(v_lo[:, :, :], vraw[:, :, :], v_hi[:, :, :], ALU.subtract)\
                    .then_inc(vl_done, 1)
                for q in range(8):
                    pl.wait_ge(ec_done, i * 8 + q + 1)
                    e2 = E[1][q % 2][:, 0:(q + 1) * P]
                    pl.tensor_tensor(e2, e2, ec[:, q:q + 1].to_broadcast([P, (q + 1) * P]), ALU.mult)\
                        .then_inc(e2_done, 1)

            head(0)
            with pl.Fori(1, NH) as i:
                head(i)
            hi2 = hi1 + 24
            pl.wait_ge(onl, NH)
            ab(N_WO, None, hi2)
            ab(N_WO + 1, [T_WO + 1, T_WO + 3, T_WO + 2, T_WO + 4], hi2 + 4)
            ffn(1, N_F1, T_F1, [T_WO + 5, T_WO + 7, T_WO + 6, T_WO + 8], hi2 + 8)

        def two(n):
            return ps[:, 2 * n:2 * n + 2, :]

        def wide(t):
            return t.rearrange("p (b c) -> p b c", b=2)

        PT_USES = [(q, k0, min(4, q + 1 - k0)) for q in range(8) for k0 in range(0, q + 1, 4)]

        def pt_of(q):
            return [n for n, use in enumerate(PT_USES) if use[0] == q]

        def h_ready(m, k):
            return ((h_add, KT), (dve_ev, D_KVQ - 8 + k + 1), (dve_ev, D_WO + k + 1),
                    (dve_ev, D_F1 + FD - 8 + k + 1))[m]

        @block.tensor
        def _(pe):
            pe.wait_ge(consts_in, 16 * 9)
            pe.wait_ge(ssq_done, 1)
            pe.matmul(ps[:, 7, 0:NC], same_j[:, :], ssq[:, :], start=True, stop=True).then_inc(rms_pe, 1)

            def batch(n, kind, hf, k):
                b = n % 8
                if n == 7:
                    pe.wait_ge(rms_ms, 1)
                if n >= 8:
                    pe.wait_ge(*evacuated(n - 8))
                if kind == "wt":
                    if k == 0:
                        pe.wait_ge(w_tab, hf + 1)
                    for n4 in range(4):
                        src = (wr, wi)[n4 % 2][:, 2 * k + n4 // 2, :, :].rearrange("p a b -> p (a b)")
                        ins = pe.transpose(ps[:, b, P * n4:P * n4 + P], src, ident[:, :])
                elif kind == "v":
                    if k == 0 and hf == 0:
                        pe.wait_ge(u_done, 1)
                        pe.wait_ge(u_pool, 1)
                    pe.wait_ge(*evacuated(number["wt", hf, k]))
                    for n8 in range(8):
                        q, ri, gp = 2 * k + n8 // 4, n8 // 2 % 2, n8 % 2
                        c0 = 2 * P * (n8 // 4) + P * ri
                        ins = pe.matmul(ps[64 * gp:64 * gp + 64, b, c0:c0 + P],
                                        wt[:, q, ri, 64 * gp:64 * gp + 64],
                                        u[:, 2 * (HP * hf + q) + gp, :], start=True, stop=True)
                elif kind == "g":
                    if k == 0:
                        pe.wait_ge(s5_act, evacuated(number["wt", hf, 0])[1])
                        pe.wait_ge(c_tab, hf + 1)
                        pe.wait_ge(dd_done, hf + 1)
                    rows = slice(64 * (k % 2), 64 * (k % 2) + 64)
                    for n4 in range(4):
                        q, c0 = 4 * (k // 2) + n4, P * n4
                        g = 2 * q + k % 2
                        for ri, c in enumerate((cr, cn)):
                            lhs = w4[rows, q, ri, :, :].rearrange("p a b -> p (a b)")
                            pe.matmul(ps[:, b, c0 + CH:c0 + P], lhs,
                                      c[rows, q, 0:T - 1, :].rearrange("p a b -> p (a b)"),
                                      start=(n4 == 0 and ri == 0), stop=False, skip_group_check=True)
                            lhs = bz4[ri][rows, q, :, :, :].rearrange("p s a b -> p (s a b)")
                            pe.matmul(ps[:, b, c0:c0 + CH], lhs, c[rows, q, 0, :], start=False,
                                      stop=False, skip_group_check=True)
                        ins = pe.matmul(ps[:, b, c0:c0 + 32],
                                        ident4[:, :],
                                        dd[:, g, :], start=False, stop=True, skip_group_check=True)
                elif kind == "y":
                    if k == 0:
                        pe.wait_ge(scan_done, hf + 1)
                    pe.wait_ge(*evacuated(number["g", hf, k]))
                    rows = slice(64 * (k % 2), 64 * (k % 2) + 64)
                    for n4 in range(4):
                        q = 4 * (k // 2) + n4
                        g, o = 2 * q + k % 2, ps[:, b, P * n4:P * n4 + P]
                        pe.matmul(o, u[:, 2 * HP * hf + g, :], gt[:, g, :], start=True, stop=False)
                        for ri, c in enumerate((cr, cn)):
                            ins = pe.matmul(o, st[rows, q, ri, 0:NC],
                                            c[rows, q, 1:T + 1, :].rearrange("p a b -> p (a b)"),
                                            start=False, stop=(ri == 1))
                else:
                    if k == 0:
                        pe.wait_ge(*evacuated(number["y", 1, 7]))
                    for n4 in range(4):
                        j = 4 * (k % 2) + n4
                        ins = pe.transpose(ps[:, b, P * n4:P * n4 + P], z[:, k // 8, j, P * (k // 2 % 4):P * (k // 2 % 4) + P],
                                           ident[:, :])
                ins.then_inc(s5_full, 1)

            s5_batches(pe, [(kind, hf) for kind in ("wt", "v", "g", "y", "z") for hf in range(2)], batch)

            def product(slot, w, wcols, x, ks=range(KT), rows=None):
                for k in ks:
                    if rows is not None:
                        pe.wait_ge(nlo, rows + k + 1)
                    for n, (wn, xn) in enumerate(((0, 0), (0, 1), (1, 0))):
                        for c in range(2):
                            ins = pe.matmul(ps[:, 2 * slot + c, :], w[wn][:, k, wcols],
                                            x[xn][:, k, 512 * c:512 * c + 512],
                                            start=(k == ks[0] and n == 0), stop=(k == ks[-1] and n == 2))
                ins.then_inc(tile, 1)

            xs = (x_hi, x_lo)
            halves = (slice(0, P), slice(P, 2 * P))

            pe.wait_ge(dve_ev, D_GLU)
            pe.wait_ge(act_ev, A_GLU)
            with pe.Fori(0, 4) as i:
                for x in range(2):
                    pe.wait_ge(a_rdy, i * 2 + (2 * N_GLU + x + 1))
                    pe.wait_ge(dve_ev, i * 2 + (D_GLU - 1 + x))
                    product(2 * x, wa, halves[x], xs)
                    pe.wait_ge(b_rdy, i * 2 + (2 * N_GLU + x + 1))
                    pe.wait_ge(act_ev, i * 2 + (A_GLU - 1 + x))
                    product(2 * x + 1, wb, halves[x], xs)

            def columns(m):
                pe.wait_ge(nacc, 7 * m + 7)
                for t in range(KT):
                    ins = pe.matmul(ps[:, 7, t:t + 1], tmp[2][:, P * t:P * t + P], ones[:, :],
                                    start=True, stop=True)
                ins.then_inc(ncol, 1)
                pe.wait_ge(nrs, m + 1)
                spread(ps, 2, rs, nbc)

            def spread(o, b, col, done):
                for t in range(KT):
                    ins = pe.matmul(o[:, b + t // 4, P * (t % 4):P * (t % 4) + P],
                                    col[:, t:t + 1].to_broadcast([P, P]), ident[:, :],
                                    start=True, stop=True)
                ins.then_inc(done, 1)

            def ffn(layer, n0, d0, a0, rows):
                def w1(x, n, **kw):
                    pe.wait_ge(a_rdy, n)
                    product((0, 2)[x], wa, halves[x], xs, **kw)

                def w3(x, n):
                    pe.wait_ge(b_rdy, n)
                    product((1, 3)[x], wb, halves[x], xs)

                def body(i, last):
                    pe.wait_ge(dve_ev, i * 10 + (d0 - 3))
                    w3(0, i * 2 + (2 * n0 + 1))
                    pe.wait_ge(dve_ev, i * 10 + (d0 - 2))
                    w1(1, i * 2 + (2 * n0 + 2))
                    pe.wait_ge(dve_ev, i * 10 + (d0 - 1))
                    w3(1, i * 2 + (2 * n0 + 2))
                    if not last:
                        pe.wait_ge(act_ev, i * 2 + (a0 + 1))
                        pe.wait_ge(dve_ev, i * 10 + d0)
                        w1(0, i * 2 + (2 * n0 + 3))
                    pe.wait_ge(c_rdy, i * 2 + (2 * FP * layer + 2))
                    pe.wait_ge(hid_l, i * 2 + (2 * FP * layer + 2))
                    for n in range(8):
                        if n % 4 == 1 and n < 4:
                            pe.wait_ge(act_ev, i * 2 + (a0 + 2))
                        elif n == 3:
                            if not last:
                                pe.wait_ge(act_ev, i * 2 + (a0 + 3))
                        else:
                            pe.wait_ge(dve_ev, i * 10 + (d0 + (1, 0, 2, 0, 3, 4, 5, 6)[n]))
                        product((1, 2, 3, 0)[n % 4], wc, slice(P * n, P * n + P), hid, range(2))

                w1(0, 2 * n0 + 1, rows=rows)
                with pe.Fori(0, FP - 1) as i:
                    body(i, False)
                body(FP - 1, True)

            columns(0)
            ffn(0, N_F0, D_F0, A_F0, 0)
            columns(1)

            with pe.Fori(0, 6) as i:
                for s, (w, ready) in enumerate(((wa, a_rdy), (wb, b_rdy))):
                    pe.wait_ge(ready, i * 2 + (2 * N_KVQ + 2))
                    pe.wait_ge(act_ev, i * 2 + (A_KVQ - 1 + s))
                    for t in range(KT):
                        for k in range(KT):
                            if t == 0 and s == 0:
                                pe.wait_ge(nlo, KT + k + 1)
                            for n, (wn, xn) in enumerate(((0, 0), (0, 1), (1, 0))):
                                ins = pe.matmul(ps[:, 4 * s + t // 2, 256 * (t % 2):256 * (t % 2) + 256],
                                                xs[xn][:, k, P * t:P * t + P], w[wn][:, k, :],
                                                start=(k == 0 and n == 0), stop=(k == 7 and n == 2))
                    ins.then_inc(tile, 1)

            def turn(i):
                pe.wait_ge(kq_in, i * 128 + 128)
                for v in range(8):
                    src, s, t0 = (kraw, qraw)[v // 4], v // 2 % 2, 4 * (v % 2)
                    if v >= 2:
                        pe.wait_ge(kq_lo, i * 8 + (v - 1))
                    for t in range(4):
                        ins = pe.transpose(ps[:, 4 + v % 2, P * t:P * t + P],
                                           src[:, t0 + t, s, :, :].rearrange("p a b -> p (a b)"),
                                           ident[:, :])
                    ins.then_inc(kq_tr, 1)

            def scores(i, q):
                for s in range(2):
                    if q == 0 and s == 0:
                        pe.wait_ge(kq_lo, i * 8 + 8)
                    if q:
                        pe.wait_ge(exd, i * 16 + (2 * q - 1 + s))
                    ext = (q + 1) * P
                    for c in range(0, ext, 512):
                        n = max(256, min(512, ext - c))
                        for part_, qq in enumerate((q_hi, q_lo)):
                            ins = pe.matmul(ps[:, 2 * s + c // 512, 0:n], qq[:, s, P * q:P * q + P],
                                            kst[:, s, c:c + n], start=(part_ == 0), stop=(part_ == 1))
                    ins.then_inc(sc, 1)

            def turn_p(i, q):
                pe.wait_ge(p_done, i * 8 + (q + 1))
                for n in pt_of(q):
                    _, k0, cnt = PT_USES[n]
                    if n >= 2:
                        pe.wait_ge(ptl, i * 12 + (n - 1))
                    for k in range(cnt):
                        ins = pe.transpose(ps[:, 4 + n % 2, P * k:P * k + P],
                                           E[0][q % 2][:, P * (k0 + k):P * (k0 + k) + P], ident[:, :])
                    ins.then_inc(pt_tr, 1)

            def values(i, b):
                if b == 0:
                    pe.wait_ge(vl_done, i + 1)
                if b >= 2:
                    pe.wait_ge(oq, i * 4 + (b - 1))
                pe.wait_ge(ptl, i * 12 + (pt_of(2 * b + 1)[-1] + 1))
                for k in range(2 * b + 2):
                    for n, (vv, pp) in enumerate(((v_hi, pt_hi), (v_hi, pt_lo), (v_lo, pt_hi))):
                        ins = pe.matmul(ps[:, 6 + b % 2, 0:256], vv[:, k, :], pp[:, k, :],
                                        start=(k == 0 and n == 0), stop=(k == 2 * b + 1 and n == 2))
                ins.then_inc(pv, 1)

            def head(i, last):
                scores(i, 0)
                scores(i, 1)
                turn_p(i, 0)
                for q in range(2, 8):
                    if q % 2 == 0 and q > 2:
                        pass
                    if q % 2 == 0:
                        scores(i, q)
                        turn_p(i, q - 1)
                    else:
                        scores(i, q)
                        values(i, q // 2 - 1)
                        turn_p(i, q - 1)
                turn_p(i, 7)
                values(i, 3)
                if not last:
                    turn(i + 1)
                pe.wait_ge(oq, i * 4 + 4)
                for t in range(KT):
                    ins = pe.matmul(ps[:, 7, t:t + 1], osq[:, P * t:P * t + P], ones[:, :],
                                    start=True, stop=True)
                ins.then_inc(ocol, 1)
                pe.wait_ge(ors, i + 1)
                spread(ps, 6, rs, obc)

            pe.wait_ge(act_ev, A_WO)
            turn(0)
            with pe.Fori(0, NH - 1) as i:
                head(i, False)
            head(NH - 1, True)

            pe.wait_ge(onl, NH)
            for i in range(2):
                for n, (w, ready) in enumerate(((wa, a_rdy), (wa, a_rdy), (wb, b_rdy), (wb, b_rdy))):
                    pe.wait_ge(ready, 2 * (N_WO + i) + n % 2 + 1)
                    if i:
                        pe.wait_ge(dve_ev, D_WO + n + 1)
                    product(n, w, halves[n % 2], xs)
            columns(2)
            ffn(1, N_F1, D_F1, A_F1, 2 * KT)
            pe.wait_ge(nacc, 28)
            for t in range(KT):
                ins = pe.matmul(ps[:, 7, t:t + 1], tmp[2][:, P * t:P * t + P], ones[:, :],
                                start=True, stop=True)
            ins.then_inc(ncol, 1)
            pe.wait_ge(nrs, 4)
            spread(ps, 2, rs, nbc)

        @block.scalar
        def _(ac):
            steps = [0]

            def step(ins):
                steps[0] += 1
                ins.then_inc(act, 1)
                ac.wait_ge(act, steps[0])

            ac.wait_ge(params_in, 16)
            ac.activation(prm[:, 3, :], prm[:, 2, :], ACT.Exp).then_inc(prm_exp, 1)
            ac.wait_ge(prm_arg, 1)
            ac.activation(prm[:, 6, :], prm[:, 4, :], ACT.Exp).then_inc(prm_exp, 1)
            ac.wait_ge(lam_d, 1)
            ac.activation(lams[:, 0:2], lams[:, 0:2], ACT.Exp).then_inc(lam_e, 1)
            ac.wait_ge(prm_arg, 2)
            ac.activation(prm[:, 9, :], prm[:, 8, :], ACT.Sin).then_inc(prm_sin, 1)
            ac.activation(prm[:, 10, :], prm[:, 8, :], ACT.Sin, scale=0.5).then_inc(prm_sin, 1)
            for k in range(4):
                ac.wait_ge(u_in[k], 16)
                if k >= 2:
                    ac.wait_ge(part_done, k - 1)
                ac.activation(sq[k % 2][:, :, :], u[:, 16 * k:16 * k + 16, :], ACT.Square)\
                    .then_inc(sq_done, 1)
            ac.wait_ge(rms_ms, 1)
            ac.activation(rfull[:, :], rfull[:, :], ACT.Sqrt).then_inc(rms_rt, 1)

            def batch(n, kind, hf, k):
                b = n % 8
                if kind == "wt" and k == 0:
                    ac.wait_ge(w_tab, hf + 1)
                    for ri, w in enumerate((wr, wi)):
                        ac.activation(w4[:, :, ri, :, :], w[:, :, T - 2:T, :].rearrange("p q a b -> p q (a b)")
                                      .unsqueeze(2).to_broadcast([P, HP, 4, 2 * CH]), ACT.Copy)
                ac.wait_ge(s5_full, n + 1)
                if kind == "wt":
                    ac.activation(wt[:, 2 * k:2 * k + 2, :, :].rearrange("p q r c -> p (q r c)"),
                                  ps[:, b, :], ACT.Copy).then_inc(s5_act, 1)
                elif kind == "v":
                    ac.activation(st[:, 2 * k:2 * k + 2, :, 1:NC + 1],
                                  ps[:, b, :].rearrange("p (q r c) -> p q r c", q=2, r=2), ACT.Copy)\
                        .then_inc(s5_act, 1)
                elif kind == "g":
                    src = ps[:, b, :].rearrange("p (g c) -> p g c", g=4)
                    g0 = 8 * (k // 2) + k % 2
                    for q in range(4):
                        ins = ac.activation(gt[32 * q:32 * q + 32, g0:g0 + 7:2, 32 * q:P],
                                            src[32 * q:32 * q + 32, :, 0:P - 32 * q], ACT.Copy)
                    ins.then_inc(s5_act, 1)
                elif kind == "y":
                    c0 = 32 * 4 * (k // 2)
                    o = z[:, hf, :, c0:c0 + P].rearrange("p j (s x) -> p s j x", x=32)
                    o = o[:, :, :, CH * (k % 2):CH * (k % 2) + CH]
                    ac.activation(o, ps[:, b, :].rearrange("p (s j x) -> p s j x", s=4, x=CH),
                                  ACT.Gelu_apprx_tanh).then_inc(s5_act, 1)
                else:
                    o = x_hi[:, k // 2, :].rearrange("p (c j) -> p j c", j=T)
                    o = o[:, 4 * (k % 2):4 * (k % 2) + 4, :]
                    ins = ac.activation(o, ps[:, b, :].rearrange("p (j c) -> p j c", j=4), ACT.Copy)
                    ins.then_inc(act_ev, A_GLU) if k == 15 else ins.then_inc(z_hi, 1)

            ac.wait_ge(u_done, 1)
            s5_batches(ac, [(kind, hf) for kind in ("wt", "v", "g", "y", "z") for hf in range(2)], batch)

            def gates(i):
                for x in range(2):
                    ac.wait_ge(tile, i * 4 + (T_GLU + 2 + 2 * x))
                    if not isinstance(i, int):
                        ac.wait_ge(dve_ev, i * 2 + (D_GLU - 1 + x))
                    ac.activation(wide(tmp[x][:, :]), two(1 + 2 * x), ACT.Sigmoid).then_inc(act_ev, 1)

            gates(0)
            with ac.Fori(1, 4) as i:
                gates(i)

            def norm(m):
                for k in range(KT):
                    ac.wait_ge(*h_ready(m, k))
                    if k >= 3:
                        ac.wait_ge(nacc, 7 * m + k - 2)
                    ac.activation((tmp[2] if k == 0 else tmp[1 - k % 2])[:, :], h[:, k, :], ACT.Square)\
                        .then_inc(nsq, 1)
                ac.wait_ge(nms, m + 1)
                ac.activation(rt[:, :], ms[:, :], ACT.Sqrt).then_inc(nrt, 1)
                if m < 3:
                    for k in range(KT):
                        ac.wait_ge(nf, KT * m + k + 1)
                        ac.activation(x_hi[:, k, :], tmp[k % 2][:, :], ACT.Copy).then_inc(nhi, 1)

            def ffn(layer, t0, d0):
                def silu(x, at):
                    ac.wait_ge(tile, at)
                    ac.activation(wide(tmp[x][:, :]), two(2 * x), ACT.Silu).then_inc(act_ev, 1)

                def high(x, n):
                    ac.wait_ge(dve_ev, n)
                    ac.activation(hid[0][:, x, :], tmp[2][:, :], ACT.Copy).then_inc(hid_h, 1)

                def body(i, last):
                    high(0, i * 10 + (d0 + 1))
                    silu(1, i * 12 + (t0 + 3))
                    high(1, i * 10 + (d0 + 2))
                    if not last:
                        silu(0, i * 12 + (t0 + 5))

                silu(0, t0 + 1)
                with ac.Fori(0, FP - 1) as i:
                    body(i, False)
                body(FP - 1, True)

            norm(0)
            ffn(0, T_F0, D_F0)
            norm(1)

            def projected(i):
                for s in range(2):
                    ac.wait_ge(tile, i * 2 + (T_KVQ + 1 + s))
                    if not isinstance(i, int):
                        ac.wait_ge(stored[s], i * 16)
                    ac.activation(stg[s][:, :, :].rearrange("p (b x) c -> p b (x c)", x=2),
                                  ps[:, 4 * s:4 * s + 4, :], ACT.Copy).then_inc(act_ev, 1)

            projected(0)
            with ac.Fori(1, 6) as i:
                projected(i)

            def turned(i):
                for v in range(8):
                    dst, s, c0 = (kst, q_hi)[v // 4], v // 2 % 2, 512 * (v % 2)
                    ac.wait_ge(kq_tr, i * 8 + (v + 1))
                    ac.activation(dst[:, s, c0:c0 + 512], ps[:, 4 + v % 2, :], ACT.Copy).then_inc(kq_hi, 1)

            def exps(i, q):
                for s in range(2):
                    ac.wait_ge(nbd, i * 16 + (2 * q + s + 1))
                    ext = (q + 1) * P
                    ac.activation(E[s][q % 2][:, 0:ext],
                                  ps[:, 2 * s:2 * s + 2, :].rearrange("p b c -> p (b c)")[:, 0:ext],
                                  ACT.Exp, bias=nb[:, 2 * q + s:2 * q + s + 1], scale=SCALE,
                                  accum_out=es[:, 2 * q + s:2 * q + s + 1]).then_inc(exd, 1)

            def turned_p(i, q):
                for n in pt_of(q):
                    _, k0, cnt = PT_USES[n]
                    c0 = P * (q % 2)
                    ac.wait_ge(pt_tr, i * 12 + (n + 1))
                    ac.activation(pt_hi[:, k0:k0 + cnt, c0:c0 + P],
                                  ps[:, 4 + n % 2, 0:P * cnt].rearrange("p (k c) -> p k c", c=P),
                                  ACT.Copy).then_inc(pth, 1)

            def outputs(i, b):
                ac.wait_ge(pv, i * 4 + (b + 1))
                o = ps[:, 6 + b % 2, 0:256]
                ac.activation(otf[:, 256 * b:256 * b + 256], o, ACT.Copy).then_inc(oc, 1)
                ac.activation(osq[:, 256 * b:256 * b + 256], o, ACT.Square).then_inc(oq, 1)

            def head(i, last):
                exps(i, 0)
                exps(i, 1)
                for q in range(2, 8):
                    exps(i, q)
                    turned_p(i, q - 2)
                    if q % 2 == 0 and q >= 4:
                        outputs(i, q // 2 - 2)
                turned_p(i, 6)
                outputs(i, 2)
                turned_p(i, 7)
                outputs(i, 3)
                if not last:
                    turned(i + 1)
                ac.wait_ge(oms, i + 1)
                ac.activation(rt[:, :], ms[:, :], ACT.Sqrt).then_inc(ort, 1)
                ac.wait_ge(onfd, i + 1)
                ac.wait_ge(onfd, 1)
                ac.activation(x_hi[:, i, :] if isinstance(i, int) else
                              x_hi[:, bass.ds(i, 1), :].rearrange("p o c -> p (o c)"),
                              onf[:, :], ACT.Copy).then_inc(onh, 1)

            turned(0)
            with ac.Fori(0, NH - 1) as i:
                head(i, False)
            head(NH - 1, True)
            norm(2)
            ffn(1, T_F1, D_F1)
            norm(3)

        @block.vector
        def _(ve):
            steps = [0]

            def step(ins, wait=True):
                steps[0] += 1
                ins.then_inc(dve, 1)
                if wait:
                    ve.wait_ge(dve, steps[0])

            tt, ts = ve.tensor_tensor, ve.tensor_scalar

            p = lambda n: prm[:, n, :]
            ve.wait_ge(params_in, 16)
            ve.wait_ge(prm_exp, 1)
            step(tt(p(4), p(0), p(3), ALU.mult), False)
            step(tt(p(5), p(1), p(3), ALU.mult))
            ts(p(7), p(5), 1 / (2 * math.pi), MAGIC, ALU.mult, ALU.add).then_inc(prm_arg, 1)
            ve.wait_ge(prm_arg, 1)
            step(ts(p(7), p(7), -MAGIC, None, ALU.add))
            for n, part_pi in enumerate(TWO_PI):
                step(ve.scalar_tensor_tensor(out=p(8), in0=p(7), scalar=-part_pi,
                                             in1=p(5) if n == 0 else p(8), op0=ALU.mult, op1=ALU.add))
            ts(p(8), p(8), PI_F, -PI_F, ALU.min, ALU.max).then_inc(prm_arg, 1)
            step(tt(p(16), p(0), p(0), ALU.mult), False)
            step(tt(p(17), p(1), p(1), ALU.mult))
            step(tt(p(16), p(16), p(17), ALU.add))
            step(ve.reciprocal(p(20), p(16)))
            ve.wait_ge(consts_in, 16 * 9)
            step(tt(lamp[:, :, :], lamv[:, 0:4:2, :], lamv[:, 1:4:2, :], ALU.mult))
            ve.tensor_reduce(lams[:, 0:2], lamp[:, :, :], AX.X, ALU.add).then_inc(lam_d, 1)
            ve.wait_ge(prm_sin, 2)
            ve.wait_ge(prm_exp, 2)
            step(tt(p(11), p(10), p(10), ALU.mult))
            step(ts(p(12), p(11), -2.0, 1.0, ALU.mult, ALU.add))
            step(tt(p(13), p(6), p(12), ALU.mult), False)
            step(tt(p(14), p(6), p(9), ALU.mult))
            step(ts(p(15), p(13), -1.0, None, ALU.add))
            step(tt(p(17), p(15), p(0), ALU.mult), False)
            step(tt(p(18), p(14), p(1), ALU.mult), False)
            step(tt(p(19), p(14), p(0), ALU.mult), False)
            step(tt(p(21), p(15), p(1), ALU.mult))
            step(tt(p(17), p(17), p(18), ALU.add), False)
            step(tt(p(19), p(19), p(21), ALU.subtract))
            step(tt(p(22), p(17), p(20), ALU.mult), False)
            step(tt(p(23), p(19), p(20), ALU.mult))
            ve.wait_ge(lam_e, 1)
            step(tt(lams[:, 2:3], lams[:, 1:2], lams[:, 0:1], ALU.subtract), False)
            step(ts(subg[:, :], subg[:, :], 1 - LAM_INIT, None, ALU.mult))
            ts(lams[:, 3:4], lams[:, 2:3], -LAM_INIT, None, ALU.add).then_inc(lam_done, 1)

            def cmul(out, x, y, n):
                t = [pt4[m][:, 0:n, :] for m in range(4)]
                yr, yi = (v.to_broadcast([P, n, NP]) for v in y)
                step(tt(t[0], x[0], yr, ALU.mult), False)
                step(tt(t[1], x[1], yi, ALU.mult), False)
                step(tt(t[2], x[0], yi, ALU.mult), False)
                step(tt(t[3], x[1], yr, ALU.mult))
                step(tt(out[0], t[0], t[1], ALU.subtract), False)
                step(tt(out[1], t[2], t[3], ALU.add))

            dn = lambda k0, k1: [pw_d[:, r, k0:k1, :] for r in range(2)]
            up = lambda k0, k1: [pw_8[:, r, k0:k1, :] for r in range(2)]
            step(ve.memset(pw_d[:, 0, 8, :], 1.0), False)
            step(ve.memset(pw_d[:, 1, 8, :], 0.0), False)
            step(ve.tensor_copy(pw_d[:, 0, 7, :], p(13)), False)
            step(ve.tensor_copy(pw_d[:, 1, 7, :], p(14)))
            cmul(dn(6, 7), dn(7, 8), dn(7, 8), 1)
            cmul(dn(4, 6), dn(6, 8), dn(6, 7), 2)
            cmul(dn(0, 4), dn(4, 8), dn(4, 5), 4)
            ve.tensor_copy(pw_a[:, :, :, :], pw_d[:, :, ::-1, :]).then_inc(prm_done, 1)
            ve.wait_ge(bc_in, 112)
            for n in range(2):
                step(tt(b_raw[n][:, :, :], b_raw[n][:, :, :], g_b[:, :, :], ALU.mult), n == 1)
            step(tt(d_two[:, :], d_two[:, :], g_two[:, :], ALU.mult))
            f_r, f_i = (p(n).unsqueeze(2).to_broadcast([P, NP, CH]) for n in (22, 23))
            t = [x[:, 4 * n:4 * n + 4, :, :].rearrange("p q k c -> p (q k) c")
                 for n in range(2) for x in (m1, m2)]
            step(tt(t[0], f_r, b_raw[0][:, :, :], ALU.mult), False)
            step(tt(t[1], f_i, b_raw[1][:, :, :], ALU.mult), False)
            step(tt(t[2], f_r, b_raw[1][:, :, :], ALU.mult), False)
            step(tt(t[3], f_i, b_raw[0][:, :, :], ALU.mult))
            step(tt(b_raw[0][:, :, :], t[0], t[1], ALU.subtract), False)
            step(tt(b_raw[1][:, :, :], t[2], t[3], ALU.add))
            step(ve.tensor_copy(up(0, 1)[0], dn(0, 1)[0]), False)
            step(ve.tensor_copy(up(0, 1)[1], dn(0, 1)[1]))
            cmul(up(1, 2), up(0, 1), up(0, 1), 1)
            cmul(up(2, 4), up(0, 2), up(1, 2), 2)
            cmul(up(4, 8), up(0, 4), up(3, 4), 4)

            for k in range(4):
                ve.wait_ge(sq_done, k + 1)
                ve.tensor_reduce(part[:, k, :], sq[k % 2][:, :, :].rearrange("p g c -> p c g"), AX.X,
                                 ALU.add).then_inc(part_done, 1)
            ve.wait_ge(part_done, 4)
            ve.tensor_reduce(ssq[:, :], part[:, :, :].rearrange("p k c -> p c k"), AX.X, ALU.add)\
                .then_inc(ssq_done, 1)
            ve.wait_ge(rms_pe, 1)
            ts(rfull[:, :], ps[:, 7, 0:NC], 1.0 / D, EPS, ALU.mult, ALU.add).then_inc(rms_ms, 1)
            ve.wait_ge(rms_rt, 1)
            ve.reciprocal(rfull[:, :], rfull[:, :]).then_inc(rms_rs, 1)
            ve.memset(gt[:, :, :], 0.0).then_inc(prm_done, 1)
            ve.wait_ge(rms_rs, 1)
            tt(u[:, 0:44, :], u[:, 0:44, :], rfull[:, :].unsqueeze(1).to_broadcast([P, 44, NC]), ALU.mult)\
                .then_inc(u_done, 1)

            for hf in range(2):
                half = slice(HP * hf, HP * hf + HP)
                if hf:
                    ve.wait_ge(s5_full, number["g", 0, 7] + 1)
                shape = [P, HP, T, CH]
                pr, pi = (pw_d[:, n, 1:T + 1, half].rearrange("p k q -> p q k").unsqueeze(3)
                          .to_broadcast(shape) for n in range(2))
                b_r, b_i = (b_raw[n][:, half, :].unsqueeze(2).to_broadcast(shape) for n in range(2))
                step(tt(m1[:, :, :, :], pr, b_r, ALU.mult), False)
                step(tt(m2[:, :, :, :], pi, b_i, ALU.mult))
                step(tt(wr[:, :, :, :], m1[:, :, :, :], m2[:, :, :, :], ALU.subtract))
                step(tt(m1[:, :, :, :], pr, b_i, ALU.mult), False)
                step(tt(m2[:, :, :, :], pi, b_r, ALU.mult))
                tt(wi[:, :, :, :], m1[:, :, :, :], m2[:, :, :, :], ALU.add).then_inc(w_tab, 1)
                tt(dd[:, :, :], ident[0:32, 0:32].unsqueeze(1).to_broadcast([32, 2 * HP, 32]),
                   d_two[:, 2 * HP * hf:2 * HP * hf + 2 * HP].unsqueeze(2).to_broadcast([32, 2 * HP, 32]),
                   ALU.mult).then_inc(dd_done, 1)

                if hf == 0:
                    step(ve.memset(st[:, :, :, 0:1], 0.0))
                ve.wait_ge(*evacuated(number["v", hf, 7]))
                S = st[:, :, :, 1:NC + 1].rearrange("p q i (m r) -> p q i m r", r=R)

                def advance(cur, prev, power, m0, m):
                    a_r, a_i = (pw_8[:, n, power - 1, half] for n in range(2))
                    both = a_r.unsqueeze(2).unsqueeze(3).to_broadcast([P, HP, 2, m])
                    one = a_i.unsqueeze(2).to_broadcast([P, HP, m])
                    x, y = ta[:, :, :, 0:m], tb[:, :, :, 0:m]
                    step(tt(x, prev, both, ALU.mult), False)
                    step(ve.scalar_tensor_tensor(out=y[:, :, 0, :], in0=prev[:, :, 1, :], scalar=-1.0,
                                                 in1=one, op0=ALU.mult, op1=ALU.mult), False)
                    step(tt(y[:, :, 1, :], prev[:, :, 0, :], one, ALU.mult))
                    step(tt(cur, cur, x, ALU.add))
                    step(tt(cur, cur, y, ALU.add))

                for r in range(1, R):
                    advance(S[:, :, :, :, r], S[:, :, :, :, r - 1], 1, 0, M)
                for m in range(1, M):
                    advance(S[:, :, :, m:m + 1, R - 1], S[:, :, :, m - 1:m, R - 1], R, 0, 1)
                for r in range(R - 1):
                    advance(S[:, :, :, 1:M, r], S[:, :, :, 0:M - 1, R - 1], r + 1, 0, M - 1)
                ve.tensor_copy(ta[:, 0, 0, 0:1], ta[:, 0, 0, 0:1]).then_inc(scan_done, 1)
                ve.wait_ge(scan_done, hf + 1)

            for k in range(16):
                n = number["z", 0, k]
                ve.wait_ge(s5_full, n + 1)
                ve.wait_ge(act_ev, A_GLU) if k == 15 else ve.wait_ge(z_hi, k + 1)
                o, i_ = (x[:, k // 2, :].rearrange("p (c j) -> p j c", j=T)
                         [:, 4 * (k % 2):4 * (k % 2) + 4, :] for x in (x_lo, x_hi))
                ins = tt(o, ps[:, n % 8, :].rearrange("p (j c) -> p j c", j=4), i_, ALU.subtract)
                ins.then_inc(dve_ev, D_GLU) if k == 15 else ins.then_inc(s5_dve, 1)

            ve.wait_ge(h_in, 16)
            with ve.Fori(0, 4) as i:
                for x in range(2):
                    ve.wait_ge(tile, i * 4 + (T_GLU + 1 + 2 * x))
                    ve.wait_ge(act_ev, i * 2 + (A_GLU + 1 + x))
                    tt(wide(tmp[2][:, :]), two(2 * x), wide(tmp[x][:, :]), ALU.mult).then_inc(dve_ev, 1)
                    ve.wait_ge(dve_ev, i * 2 + (D_GLU + 1 + x))
                    hk = h[:, bass.ds(i * 2 + x, 1), :].rearrange("p o c -> p (o c)")
                    tt(hk, hk, tmp[2][:, :], ALU.add).then_inc(h_add, 1)
                    ve.wait_ge(h_add, i * 2 + (x + 1))

            def norm(m, gain):
                for k in range(1, KT):
                    ve.wait_ge(nsq, KT * m + k + 1)
                    if k >= 2:
                        ve.wait_ge(nacc, 7 * m + k - 1)
                    tt(tmp[2][:, :], tmp[2][:, :], tmp[1 - k % 2][:, :], ALU.add).then_inc(nacc, 1)
                ve.wait_ge(ncol, m + 1)
                ts(ms[:, :], ps[:, 7, 0:KT], 1.0 / D, EPS, ALU.mult, ALU.add).then_inc(nms, 1)
                ve.wait_ge(nrt, m + 1)
                ve.reciprocal(rs[:, :], rt[:, :]).then_inc(nrs, 1)
                ve.wait_ge(nbc, m + 1)

                def full(k):
                    if m == 3 and k >= 2:
                        ve.wait_ge(out_done[k % 2], 16 * (k // 2))
                    if m < 3 and k >= 2:
                        ve.wait_ge(nlo, KT * m + k - 1)
                    ve.scalar_tensor_tensor(out=wide(tmp[k % 2][:, :]), in0=wide(h[:, k, :]),
                                            scalar=1.0 if gain is None else gains[:, gain, k:k + 1],
                                            in1=two(1), op0=ALU.mult, op1=ALU.mult).then_inc(nf, 1)

                def low(k):
                    ve.wait_ge(nhi, KT * m + k + 1)
                    tt(x_lo[:, k, :], tmp[k % 2][:, :], x_hi[:, k, :], ALU.subtract).then_inc(nlo, 1)

                full(0)
                for k in range(KT):
                    if k + 1 < KT:
                        full(k + 1)
                    if m < 3:
                        low(k)

            def ffn(layer, t0, d0, a0):
                n = 2 * FP * layer

                def body(i, last):
                    for x in range(2):
                        ve.wait_ge(tile, i * 12 + (t0 + 2 + 2 * x))
                        ve.wait_ge(act_ev, i * 2 + (a0 + 1 + x))
                        tt(wide(tmp[2][:, :]), two(1 + 2 * x), wide(tmp[x][:, :]), ALU.mult)\
                            .then_inc(dve_ev, 1)
                        ve.wait_ge(hid_h, i * 2 + (n + 1 + x))
                        tt(hid[1][:, x, :], tmp[2][:, :], hid[0][:, x, :], ALU.subtract).then_inc(hid_l, 1)
                        ve.wait_ge(hid_l, i * 2 + (n + 1 + x))
                    for k in range(KT):
                        ve.wait_ge(tile, i * 12 + (t0 + 6 + k) if not last else i * 12 + (t0 + 5 + k))
                        hk = wide(h[:, k, :])
                        tt(hk, hk, two((1, 2, 3, 0)[k % 4]), ALU.add).then_inc(dve_ev, 1)

                return body

            def run_ffn(layer, t0, d0, a0):
                body = ffn(layer, t0, d0, a0)
                with ve.Fori(0, FP - 1) as i:
                    body(i, False)
                body(FP - 1, True)

            norm(0, 0)
            run_ffn(0, T_F0, D_F0, A_F0)
            norm(1, None)

            for n, c in enumerate((0, 1, 2, 3, 8, 9, 10, 11)):
                ve.wait_ge(act_ev, A_KVQ + c + 1)
                v = stg[c % 2][:, :, :].rearrange("p k (h d) -> p k h d", d=64)
                x1, x2 = v[:, :, :, 0:8], v[:, :, :, 8:16]
                cs, sn = (x[:, :, :].unsqueeze(2).to_broadcast([P, KT, 4, 8]) for x in (cos_t, sin_t))
                t = [x[:, :, :, :] for x in rtmp]
                step(tt(t[0], x1, cs, ALU.mult), False)
                step(tt(t[1], x2, sn, ALU.mult), False)
                step(tt(t[2], x2, cs, ALU.mult), False)
                step(tt(t[3], x1, sn, ALU.mult))
                step(tt(x1, t[0], t[1], ALU.subtract))
                tt(x2, t[2], t[3], ALU.add).then_inc(roped, 1)
                ve.wait_ge(roped, n + 1)

            def turned(i):
                for v in range(8):
                    s, c0 = v // 2 % 2, 512 * (v % 2)
                    ve.wait_ge(kq_hi, i * 8 + (v + 1))
                    if v < 4:
                        lo = kst[64:P, s, c0:c0 + 512]
                        tt(lo, ps[64:P, 4 + v % 2, :], lo, ALU.subtract).then_inc(kq_lo, 1)
                    else:
                        tt(q_lo[:, s, c0:c0 + 512], ps[:, 4 + v % 2, :], q_hi[:, s, c0:c0 + 512],
                           ALU.subtract).then_inc(kq_lo, 1)

            def maxima(i, q):
                for s in range(2):
                    n, ext = 2 * q + s, (q + 1) * P
                    flat = ps[:, 2 * s:2 * s + 2, :].rearrange("p b c -> p (b c)")
                    ve.wait_ge(sc, i * 16 + (n + 1))
                    ve.memset(flat[0:64, ext - 64:ext], NEG).then_inc(masked, 1)
                    ve.wait_ge(masked, i * 16 + (n + 1))
                    ve.tensor_reduce(mx[:, n:n + 1], flat[:, 0:ext], AX.X, ALU.max).then_inc(mxd, 1)
                    ve.wait_ge(mxd, i * 16 + (n + 1))
                    ts(nb[:, n:n + 1], mx[:, n:n + 1], -SCALE, None, ALU.mult).then_inc(nbd, 1)

            def sums(i, q):
                ve.wait_ge(exd, i * 16 + (2 * q + 2))
                ve.reciprocal(er[:, 2 * q:2 * q + 2], es[:, 2 * q:2 * q + 2]).then_inc(er_done, 1)
                ve.wait_ge(er_done, i * 8 + (q + 1))
                ts(ec[:, q:q + 1], er[:, 2 * q + 1:2 * q + 2], lams[:, 3:4], None, ALU.mult)\
                    .then_inc(ec_done, 1)

            def combined(i, q):
                ve.wait_ge(e2_done, i * 8 + (q + 1))
                e1, e2 = (E[s][q % 2][:, 0:(q + 1) * P] for s in range(2))
                ve.scalar_tensor_tensor(out=e1, in0=e1, scalar=er[:, 2 * q:2 * q + 1], in1=e2,
                                        op0=ALU.mult, op1=ALU.add).then_inc(p_done, 1)

            def turned_p(i, q):
                for n in pt_of(q):
                    _, k0, cnt = PT_USES[n]
                    c0 = P * (q % 2)
                    ve.wait_ge(pth, i * 12 + (n + 1))
                    if q % 2 == 0 and k0 == 0:
                        ve.memset(pt_hi[:, q + 1, 0:P].bitcast(F32), 0.0)
                        ve.memset(pt_lo[:, q + 1, 0:P].bitcast(F32), 0.0)
                    tt(pt_lo[:, k0:k0 + cnt, c0:c0 + P],
                       ps[:, 4 + n % 2, 0:P * cnt].rearrange("p (k c) -> p k c", c=P),
                       pt_hi[:, k0:k0 + cnt, c0:c0 + P], ALU.subtract).then_inc(ptl, 1)

            def head(i, last):
                maxima(i, 0)
                for q in range(1, 8):
                    sums(i, q - 1)
                    maxima(i, q)
                    combined(i, q - 1)
                    if q >= 2:
                        turned_p(i, q - 2)
                sums(i, 7)
                combined(i, 7)
                turned_p(i, 6)
                turned_p(i, 7)
                if not last:
                    turned(i + 1)
                ve.wait_ge(ocol, i + 1)
                ts(ms[:, :], ps[:, 7, 0:KT], 1.0 / VD, EPS, ALU.mult, ALU.add).then_inc(oms, 1)
                ve.wait_ge(ort, i + 1)
                ve.reciprocal(rs[:, :], rt[:, :]).then_inc(ors, 1)
                ve.wait_ge(obc, i + 1)
                ve.scalar_tensor_tensor(out=wide(onf[:, :]), in0=wide(otf[:, :]), scalar=subg[:, 0:1],
                                        in1=two(3), op0=ALU.mult, op1=ALU.mult).then_inc(onfd, 1)
                ve.wait_ge(onh, i + 1)
                x1, x2 = ((x[:, i, :] if isinstance(i, int) else
                           x[:, bass.ds(i, 1), :].rearrange("p o c -> p (o c)")) for x in (x_lo, x_hi))
                tt(x1, onf[:, :], x2, ALU.subtract).then_inc(onl, 1)

            ve.wait_ge(lam_done, 1)
            turned(0)
            with ve.Fori(0, NH - 1) as i:
                head(i, False)
            head(NH - 1, True)

            for k in range(KT):
                ve.wait_ge(tile, T_WO + k + 1)
                hk = wide(h[:, k, :])
                tt(hk, hk, two(k % 4), ALU.add).then_inc(dve_ev, 1)
            norm(2, 3)
            run_ffn(1, T_F1, D_F1, A_F1)
            norm(3, 4)


def kernel(**inputs):
    import concourse.bacc as _bacc
    from concourse.bass_utils import run_bass_kernel_spmd as _run

    i = {k: np.asarray(v) for k, v in inputs.items()}

    def states(x):
        return x.reshape(NP, P).T

    def cols(w):
        k, n = w.shape
        return w.reshape(k // P, P, n // 256, 256).transpose(2, 1, 0, 3).reshape(n // 256, P, -1)

    def tiles(g):
        return g.reshape(KT, P).T

    x = i["x"][0]
    lr, li = states(i["ssm_lam_re"][0]), states(i["ssm_lam_im"][0])
    dt = states(np.broadcast_to(i["ssm_log_dt"][0][:, None], (NG, 64)))
    pos = np.arange(L, dtype=np.float32)
    freq = np.float32(500000.0) ** (-np.arange(8, dtype=np.float32) * np.float32(2.0) / np.float32(16))
    ang = (pos[:, None] * freq[None, :]).astype(np.float32)
    by_tile = lambda v: v.reshape(KT, P, 8).transpose(1, 0, 2)
    g_mix = i["norm_mix_g"][0].reshape(NP, 2, 1, CH)
    data = {
        "ident": np.eye(P, dtype=np.float32),
        "ident4": np.tile(np.eye(32, dtype=np.float32), (1, 4)),
        "same_j": np.kron(np.eye(T), np.ones((CH, CH))).astype(np.float32),
        "ones": np.ones((P, 1), np.float32),
        "gains": np.stack([tiles(i["norm_ffn_g"][0]), tiles(i["kv_norm_g"]), tiles(i["norm_mix_g"][1]),
                           tiles(i["norm_ffn_g"][1]), tiles(i["final_norm_g"])], 1),
        "subg": i["attn_subln_g"][0][:, None],
        "cos_t": by_tile(np.cos(ang)), "sin_t": by_tile(np.sin(ang)),
        "lamv": np.broadcast_to(np.stack([i[f"attn_{n}"][0] for n in ("lq1", "lk1", "lq2", "lk2")])[None],
                                (P, 4, 64)),
        "ssm_prm": np.stack([lr, li, dt], 1),
        "x_u": x.reshape(NC, T, NG, CH).transpose(1, 3, 2, 0).reshape(P, NG, NC),
        "x_t": x.T.reshape(KT, P, L).transpose(1, 0, 2),
        "ssm_b_re": i["ssm_b_re"][0].reshape(NP, P, CH).transpose(1, 0, 2),
        "ssm_b_im": i["ssm_b_im"][0].reshape(NP, P, CH).transpose(1, 0, 2),
        "ssm_c_re": i["ssm_c_re"][0].transpose(0, 2, 1).reshape(NP, P, CH).transpose(1, 0, 2),
        "ssm_c_im": i["ssm_c_im"][0].transpose(0, 2, 1).reshape(NP, P, CH).transpose(1, 0, 2),
        "g_b": np.broadcast_to(g_mix, (NP, 2, 64, CH)).reshape(NP, P, CH).transpose(1, 0, 2),
        "d_two": np.concatenate([i["ssm_d"][0].reshape(NG, CH).T] * 2, 0),
        "g_two": np.concatenate([i["norm_mix_g"][0].reshape(NG, CH).T] * 2, 0),
        "glu_a": cols(i["ssm_w_glu"][0][:, :D]), "glu_b": cols(i["ssm_w_glu"][0][:, D:]),
        "w_kvq": cols(np.concatenate([i["w_kv"], i["attn_w_q"][0]], 1)),
        "w_o": cols(i["attn_w_o"][0]),
    }
    for n in range(2):
        data[f"w1_{n}"] = cols(i["ffn_w1"][n])
        data[f"w3_{n}"] = cols(i["ffn_w3"][n])
        data[f"w2_{n}"] = i["ffn_w2"][n].reshape(FP, 2, P, D).transpose(0, 2, 1, 3).reshape(FP, P, 2 * D)

    nc = _bacc.Bacc("TRN2", target_bir_lowering=False, num_devices=1)
    arrays, aps = {}, {}
    for name, v in data.items():
        v = np.ascontiguousarray(v)
        arrays[f"in_{name}"] = v
        aps[name] = nc.dram_tensor(f"in_{name}", v.shape, mybir.dt.from_np(v.dtype), kind="ExternalInput").ap()
    out = nc.dram_tensor("out_t", (P, KT, L), F32, kind="ExternalOutput").ap()
    trunk(nc, aps, out)
    r = _run(nc, [arrays], core_ids=[0])
    return r.results[0]["out_t"].transpose(2, 1, 0).reshape(1, L, D)
```

```python
import math
from contextlib import ExitStack

import concourse.bass as bass
import numpy as np
from concourse import mybir

F32 = mybir.dt.float32
F32R = mybir.dt.float32r
ALU = mybir.AluOpType
ACT = mybir.ActivationFunctionType
AX = mybir.AxisListType

P = 128
L = 1024
D = 1024
KT = D // P
F = 2816
FP = F // 256
T = 8
NC = L // T
CH = 16
NG = D // CH
NP = NG // 2
HP = NP // 2
R = 8
M = NC // R
NH = 8
VD = 128
EPS = 1e-6
SCALE = 64 ** -0.5
LAM_INIT = 0.8 - 0.6 * math.exp(-0.3)
NEG = -3.0e38
TWO_PI = (6.28125, 0.0019350051879882812, 3.0199159819e-07)
MAGIC = 1.5 * 2 ** 23
PI_F = 3.1415925


def trunk(nc, a, out):
    base = (nc.sbuf_base + 31) // 32 * 32

    def sb(name, shape, kb, dt=F32):
        return nc.alloc_sbuf_tensor_at(name, shape, dt, offset=base + int(kb * 1024))

    ident = sb("ident", [P, P], 0)
    ones = sb("ones", [P, 1], 0.5)
    gains = sb("gains", [P, 5, KT], 0.53125)
    subg = sb("subg", [P, 1], 0.75)
    lamv = sb("lamv", [P, 4, 64], 1.5)
    lamp = sb("lamp", [P, 2, 64], 2.5)
    lams = sb("lams", [P, 4], 3)
    ms = sb("ms", [P, 8], 3.03125)
    rt = sb("rt", [P, 8], 3.0625)
    rs = sb("rs", [P, 8], 3.09375)
    mx = sb("mx", [P, 16], 3.125)
    nb = sb("nb", [P, 16], 3.1875)
    es = sb("es", [P, 16], 3.25)
    er = sb("er", [P, 16], 3.3125)
    ec = sb("ec", [P, 8], 3.375)
    h = sb("h", [P, KT, L], 4)
    x_hi = sb("x_hi", [P, KT, L], 36, F32R)
    x_lo = sb("x_lo", [P, KT, L], 68, F32R)
    wa = [sb("wa_hi", [P, KT, 256], 100, F32R), sb("wa_lo", [P, KT, 256], 108, F32R)]
    wb = [sb("wb_hi", [P, KT, 256], 116, F32R), sb("wb_lo", [P, KT, 256], 124, F32R)]
    wc = [sb("wc_hi", [P, 2, D], 132, F32R), sb("wc_lo", [P, 2, D], 140, F32R)]
    raw_a = sb("raw_a", [P, KT, 256], 148)
    raw_b = sb("raw_b", [P, KT, 256], 156)
    raw_c = sb("raw_c", [P, 2, D], 164)
    hid = [sb("hid_hi", [P, 2, L], 172, F32R), sb("hid_lo", [P, 2, L], 180, F32R)]
    tmp = [sb("tmp0", [P, L], 188), sb("tmp1", [P, L], 192), sb("tmp2", [P, L], 196)]
    cos_t = sb("cos_t", [P, L], 132)
    sin_t = sb("sin_t", [P, L], 136)
    xk = [sb("xk0", [P, L], 140), sb("xk1", [P, L], 144)]
    stg = [sb("stg_a", [P, KT, 256], 164), sb("stg_b", [P, KT, 256], 196)]
    rk_hi = [sb("rk_hi0", [P, L], 172, F32R), sb("rk_hi1", [P, L], 176, F32R)]
    rk_lo = [sb("rk_lo0", [P, L], 180, F32R), sb("rk_lo1", [P, L], 184, F32R)]
    rk = [sb("rk0", [P, L], 188), sb("rk1", [P, L], 192)]
    kst = [sb(f"kst{n}", [P, 2, L], kb, F32R) for n, kb in enumerate((148, 100))]
    q_hi = [sb(f"q_hi{n}", [P, 2, L], kb, F32R) for n, kb in enumerate((156, 108))]
    q_lo = [sb(f"q_lo{n}", [P, 2, L], kb, F32R) for n, kb in enumerate((164, 116))]
    v_hi = sb("v_hi", [P, KT, VD], 124, F32R)
    v_lo = sb("v_lo", [P, KT, VD], 128, F32R)
    e1 = [sb("e1_q0", [P, P], 1), sb("e1_q1", [P, 2 * P], 1.5)] \
        + [sb(f"e1_{n}", [P, L], kb) for n, kb in enumerate((132, 136, 140))] * 2
    e2 = [sb(f"e2_{n}", [P, L], kb) for n, kb in enumerate((144, 196))]
    dg = [sb(f"dg{n}", [P, P], 204 + 0.5 * n) for n in range(4)]
    pt_hi = sb("pt_hi", [P, KT, 256], 172, F32R)
    pt_lo = sb("pt_lo", [P, KT, 256], 180, F32R)
    otf = sb("otf", [P, L], 188)
    osq = sb("osq", [P, L], 192)
    onf = osq
    vraw = sb("vraw", [P, KT, VD], 200)
    u = sb("u", [P, NG, NC], 172)
    wr = sb("wr", [P, HP, T, CH], 36)
    wi = sb("wi", [P, HP, T, CH], 44)
    cr = sb("cr", [P, HP, T + 1, CH], 52)
    cn = sb("cn", [P, HP, T + 1, CH], 61)
    wt = sb("wt", [P, HP, 2, P], 70)
    gt = sb("gt", [P, 2 * HP, P], 86)
    st = sb("st", [P, HP, 2, NC + 1], 102)
    z = sb("z", [P, 2, T, D // 2], 119)
    w4 = sb("w4", [P, HP, 2, 4, 2 * CH], 135)
    ta = sb("ta", [P, HP, 2, M], 151)
    tb = sb("tb", [P, HP, 2, M], 153)
    b_raw = [sb("b_re", [P, NP, CH], 155), sb("b_im", [P, NP, CH], 157)]
    c_raw = [sb("c_re", [P, NP, CH], 159), sb("c_im", [P, NP, CH], 161)]
    ident4 = sb("ident4", [32, P], 171.5)
    pw_d = sb("pw_d", [P, 2, T + 1, NP], 167)
    pw_a = sb("pw_a", [P, 2, T + 1, NP], 169.25)
    pw_8 = sb("pw_8", [P, 2, R, NP], 204)
    d_two = sb("d_two", [32, NG], 206)
    g_two = sb("g_two", [32, NG], 206.25)
    dd = sb("dd", [32, 2 * HP, 32], 4)
    p1 = sb("p1", [P, HP, T, CH], 8)
    p2 = sb("p2", [P, HP, T, CH], 16)
    bz4 = [sb("bz4_re", [P, HP, 4, 2, CH], 8),
           sb("bz4_im", [P, HP, 4, 2, CH], 16)]
    m1 = sb("m1", [P, HP, T, CH], 24)
    m2 = sb("m2", [P, HP, T, CH], 70)
    ssq = sb("ssq", [P, NC], 34)
    rfull = sb("rfull", [P, NC], 34.5)
    same_j = sb("same_j", [P, P], 35)
    perm = sb("perm", [P, P], 3.5)
    sq = [sb("sq0", [P, 16, NC], 119), sb("sq1", [P, 16, NC], 127)]
    prm = sb("prm", [P, 24, NP], 92)
    g_b = sb("g_b", [P, NP, CH], 96)
    pt4 = [sb(f"pt4_{n}", [P, 4, NP], 102 + n) for n in range(4)]

    scr_kq = [nc.dram_tensor(name, [2, 2, NH * 64, L], F32).ap() for name in ("k_scratch", "q_scratch")]
    scr_v = nc.dram_tensor("v_scratch", [L, D], F32).ap()

    with ExitStack() as ctx:
        ps = ctx.enter_context(nc.psum_tensor("ps", [P, 8, 512], F32))
        sem = lambda name: ctx.enter_context(nc.semaphore(name))
        consts_in, params_in, h_in = sem("consts_in"), sem("params_in"), sem("h_in")
        bc_in = sem("bc_in")
        u_in = [sem(f"u_in{k}") for k in range(4)]
        sq_done, part_done, rms_pe, rms_ms, rms_rt, rms_rs = map(
            sem, "sq_done part_done rms_pe rms_ms rms_rt rms_rs".split())
        u_done, u_pool = sem("u_done"), sem("u_pool")
        dve, act, pool = sem("dve_steps"), sem("act_steps"), sem("pool_steps")
        prm_exp, prm_arg, prm_sin, prm_done = map(sem, "prm_exp prm_arg prm_sin prm_done".split())
        w_hi, w_scaled = sem("w_hi_done"), sem("w_scaled")
        w_tab, c_tab, dd_done = sem("w_tab"), sem("c_tab"), sem("dd_done")
        s5_full, s5_act, s5_dve = sem("s5_full"), sem("s5_act"), sem("s5_dve")
        scan_done, z_hi = sem("scan_done"), sem("z_hi_done")
        a_in, b_in, c_in = sem("a_loaded"), sem("b_loaded"), sem("c_loaded")
        a_rdy, b_rdy, c_rdy = sem("a_split"), sem("b_split"), sem("c_split")
        tile, act_ev, dve_ev = sem("tile_done"), sem("act_evacuated"), sem("dve_evacuated")
        sig_done, h_add = sem("sig_done"), sem("h_added")
        hid_h, hid_l = sem("hid_hi_done"), sem("hid_lo_done")
        nsq, nacc, ncol, nms, nrt, nrs, nbc, nf, nhi, nlo = map(
            sem, "n_sq n_acc n_col n_ms n_rt n_rs n_bcast n_full n_hi n_lo".split())
        rot_in, rotp, rsum, rhi, rlo = map(sem, "rot_in rot_permuted rot_sum rot_hi rot_lo".split())
        stored, v_stored = [sem("stored_0"), sem("stored_1")], [sem("v_stored_a"), sem("v_stored_b")]
        lam_d, lam_e, lam_done = sem("lam_d"), sem("lam_e"), sem("lam_done")
        kq_in, v_in = [sem("kq_loaded_0"), sem("kq_loaded_1")], sem("v_loaded")
        vh_done, vl_done = sem("v_hi_done"), sem("v_lo_done")
        sc, masked, mxd, nbd, exd = map(sem, "scores masked max_done negmax exp_done".split())
        er_done, ec_done, p_done = map(sem, "er_done ec_done p_done".split())
        pt_tr, pth, ptl = map(sem, "pt_transposed pt_hi_done pt_lo_done".split())
        pv, oc, oq = sem("pv_done"), sem("o_copied"), sem("o_squared")
        ocol, oms, ort, ors, obc, onfd, onh, onl = map(
            sem, "o_col o_ms o_rt o_rs o_bcast o_full o_hi o_lo".split())
        out_done = [sem("out_done0"), sem("out_done1")]

        kinds = []
        for hf in range(2):
            kinds += [(kind, hf, k) for kind in ("wt", "v", "g", "y") for k in range(8)]
        kinds += [("z", 0, k) for k in range(16)]
        by_act = {"wt": True, "g": True, "v": True, "y": True, "z": False}
        number = {key: n for n, key in enumerate(kinds)}

        def evacuated(n):
            mine = by_act[kinds[n][0]]
            return (s5_act if mine else s5_dve), sum(by_act[k[0]] == mine for k in kinds[:n + 1])

        def s5_batches(eng, want, body):
            for n, (kind, hf, k) in enumerate(kinds):
                if (kind, hf) in want:
                    body(n, kind, hf, k)


        N_GLU, N_F0, N_KVQ, N_WO, N_F1 = 0, 4, 4 + FP, 10 + FP, 12 + FP
        FT = 12 * FP
        T_GLU, T_F0, T_KVQ, T_WO, T_F1 = 0, 16, 16 + FT, 40 + FT, 48 + FT
        FA, FD = 2 * FP, 10 * FP
        A_GLU, A_F0, A_KVQ, A_WO, A_F1 = 4, 12, 12 + FA, 32 + FA, 32 + FA
        D_GLU, D_F0, D_KVQ, D_WO, D_F1 = 4, 12, 12 + FD, 28 + FD, 36 + FD

        block = ctx.enter_context(nc.Block())

        @block.sync
        def _(sp):
            for t, name in ((ident, "ident"), (same_j, "same_j"), (ones, "ones"), (gains, "gains"),
                            (ident4, "ident4"), (subg, "subg"), (perm, "perm"), (lamv, "lamv")):
                sp.dma_start(t[:], a[name]).then_inc(consts_in, 16)
            sp.dma_start(prm[:, 0:3, :], a["ssm_prm"]).then_inc(params_in, 16)
            for k in range(4):
                sp.dma_start(u[:, 16 * k:16 * k + 16, :], a["x_u"][:, 16 * k:16 * k + 16, :])\
                    .then_inc(u_in[k], 16)
            for t, name in ((b_raw[0], "ssm_b_re"), (b_raw[1], "ssm_b_im"), (c_raw[0], "ssm_c_re"),
                            (c_raw[1], "ssm_c_im"), (g_b, "g_b"), (d_two, "d_two"),
                            (g_two, "g_two")):
                sp.dma_start(t[:], a[name]).then_inc(bc_in, 16)

            def load(t, src, loaded, split, n, first=False):
                if not first:
                    sp.wait_ge(split, 2 * n)
                sp.dma_start(t[:, :, :], src).then_inc(loaded, 16)

            def chunk(name, i):
                return a[name][bass.ds(i, 1), :, :].rearrange("o p c -> p (o c)")\
                    .rearrange("p (k c) -> p k c", c=D if name[:2] == "w2" else 256)

            sp.wait_ge(s5_full, number["y", 1, 7] + 1)
            sp.wait_ge(s5_act, evacuated(number["y", 1, 7])[1])
            load(raw_b, chunk("glu_b", 0), b_in, b_rdy, 0, True)
            sp.wait_ge(s5_full, len(kinds))
            load(raw_a, chunk("glu_a", 0), a_in, a_rdy, 0, True)
            sp.dma_start(h[:, :, :], a["x_t"]).then_inc(h_in, 16)
            with sp.Fori(1, 4) as i:
                load(raw_a, chunk("glu_a", i), a_in, a_rdy, i)
                load(raw_b, chunk("glu_b", i), b_in, b_rdy, i)

            def ffn(layer, n0):
                load(raw_a, chunk(f"w1_{layer}", 0), a_in, a_rdy, n0)
                load(raw_b, chunk(f"w3_{layer}", 0), b_in, b_rdy, n0)
                load(raw_c, chunk(f"w2_{layer}", 0), c_in, c_rdy, layer * FP, layer == 0)
                with sp.Fori(1, FP) as i:
                    load(raw_a, chunk(f"w1_{layer}", i), a_in, a_rdy, i + n0)
                    load(raw_b, chunk(f"w3_{layer}", i), b_in, b_rdy, i + n0)
                    load(raw_c, chunk(f"w2_{layer}", i), c_in, c_rdy, i + layer * FP)

            ffn(0, N_F0)
            load(raw_a, chunk("w_kvq", 0), a_in, a_rdy, N_KVQ)
            load(raw_b, chunk("w_kvq", 1), b_in, b_rdy, N_KVQ)

            sp.wait_ge(tile, T_KVQ)
            sp.dma_start(cos_t[:, :], a["cos_t"]).then_inc(rot_in, 16)
            sp.dma_start(sin_t[:, :], a["sin_t"]).then_inc(rot_in, 16)

            def store_kq(g, n):
                sp.wait_ge(rlo, 8 * g + n + 1)
                for part_, t in enumerate((rk_hi, rk_lo)):
                    sp.dma_start(scr_kq[g][part_, n // 4, P * (n % 4):P * (n % 4) + P, :],
                                 t[n % 2][:, :].bitcast(F32)).then_inc(stored[n % 2], 16)

            def store_v(c):
                sp.wait_ge(act_ev, A_KVQ + 8 + c + 1)
                sp.dma_start(scr_v[:, 256 * c:256 * c + 256].rearrange("(k p) c -> p k c", p=P),
                             stg[c % 2][:, :, :]).then_inc(v_stored[c % 2], 16)

            for i in range(6):
                if i < 5:
                    load(raw_a, chunk("w_kvq", 2 * i + 2), a_in, a_rdy, N_KVQ + i + 1)
                    load(raw_b, chunk("w_kvq", 2 * i + 3), b_in, b_rdy, N_KVQ + i + 1)
                if i // 2 == 1:
                    store_v(2 * (i - 2))
                    store_v(2 * (i - 2) + 1)
                else:
                    for n in range(4 if i < 5 else 1):
                        store_kq(i // 4, 4 * (i % 2) + n)

            def load_kq(i, n):
                for g, part_, r0, t in ((0, 0, 0, kst), (0, 1, 64, kst), (1, 0, 0, q_hi), (1, 0, 64, q_hi),
                                        (1, 1, 0, q_lo), (1, 1, 64, q_lo)):
                    sp.dma_start(t[n][r0:r0 + 64, :, :].bitcast(F32),
                                 scr_kq[g][part_, :, bass.ds(i * 64, 64), :].rearrange("s d t -> d s t"))\
                        .then_inc(kq_in[n], 16)

            def load_v(i):
                sp.dma_start(vraw[:, :, :], scr_v[:, bass.ds(i * 128, 128)]
                             .rearrange("(k p) c -> p k c", p=P)).then_inc(v_in, 16)

            sp.wait_ge(stored[0], 32 * 7)
            sp.wait_ge(v_stored[0], 32)
            sp.wait_ge(v_stored[1], 32)
            sp.wait_ge(a_rdy, 2 * N_KVQ + 12)
            sp.wait_ge(b_rdy, 2 * N_KVQ + 12)
            load_kq(0, 0)
            load_v(0)
            for n in range(5, 8):
                store_kq(1, n)
            sp.wait_ge(stored[0], 256)
            sp.wait_ge(stored[1], 256)
            sp.wait_ge(tile, T_WO)
            load_kq(1, 1)
            with sp.Fori(0, 3) as j:
                for n in range(2):
                    sp.wait_ge(vl_done, j * 2 + (n + 1))
                    load_v(j * 2 + (n + 1))
                    sp.wait_ge(sc, j * 32 + (16 * n + 16))
                    load_kq(j * 2 + (n + 2), n)
            sp.wait_ge(vl_done, NH - 1)
            load_v(NH - 1)
            sp.wait_ge(sc, 16 * (NH - 1))
            for i in range(2):
                load(raw_a, chunk("w_o", 2 * i), a_in, a_rdy, N_WO + i)
                load(raw_b, chunk("w_o", 2 * i + 1), b_in, b_rdy, N_WO + i)
            ffn(1, N_F1)
            for k in range(KT):
                sp.wait_ge(nf, 24 + k + 1)
                sp.dma_start(out[:, k, :], tmp[k % 2][:, :]).then_inc(out_done[k % 2], 16)
            sp.wait_ge(out_done[0], 16 * KT // 2)
            sp.wait_ge(out_done[1], 16 * KT // 2)

        @block.gpsimd
        def _(pl):
            steps = [0]

            def step(ins):
                steps[0] += 1
                ins.then_inc(pool, 1)
                pl.wait_ge(pool, steps[0])

            pl.wait_ge(bc_in, 112)
            pl.wait_ge(prm_done, 1)
            for hf in range(2):
                half = slice(HP * hf, HP * hf + HP)
                shape = [P, HP, T, CH]
                pr, pi = (pw_a[:, n, 1:T + 1, half].rearrange("p k q -> p q k").unsqueeze(3)
                          .to_broadcast(shape) for n in range(2))
                c_r, c_i = (c_raw[n][:, half, :].unsqueeze(2).to_broadcast(shape) for n in range(2))
                if hf:
                    pl.wait_ge(s5_full, number["y", 0, 7] + 1)
                step(pl.tensor_tensor(p1[:, :, :, :], pr, c_r, ALU.mult))
                step(pl.tensor_tensor(p2[:, :, :, :], pi, c_i, ALU.mult))
                step(pl.tensor_tensor(cr[:, :, 1:T + 1, :], p1[:, :, :, :], p2[:, :, :, :], ALU.subtract))
                step(pl.tensor_tensor(p1[:, :, :, :], pi, c_r, ALU.mult))
                step(pl.tensor_tensor(p2[:, :, :, :], pr, c_i, ALU.mult))
                step(pl.tensor_tensor(p1[:, :, :, :], p1[:, :, :, :], p2[:, :, :, :], ALU.add))
                if hf == 0:
                    pl.wait_ge(rms_rs, 1)
                    pl.tensor_tensor(u[:, 44:NG, :], u[:, 44:NG, :],
                                     rfull[:, :].unsqueeze(1).to_broadcast([P, NG - 44, NC]), ALU.mult)\
                        .then_inc(u_pool, 1)
                    pl.wait_ge(prm_done, 2)
                step(pl.tensor_scalar(cr[:, :, 0, :], c_raw[0][:, half, :], 1.0, None, ALU.mult))
                step(pl.tensor_scalar(cn[:, :, 0, :], c_raw[1][:, half, :], -1.0, None, ALU.mult))
                step(pl.tensor_scalar(cn[:, :, 1:T + 1, :], p1[:, :, :, :], -1.0, None, ALU.mult))
                for n in range(2):
                    b = b_raw[n][:, half, :].unsqueeze(2).to_broadcast([P, HP, 4, CH])
                    pl.tensor_scalar(bz4[n][:, :, :, 0, :], b, 1.0, None, ALU.mult)
                    ins = pl.memset(bz4[n][:, :, :, 1, :], 0.0)
                ins.then_inc(c_tab, 1)

            def split(raw, w, x, loaded, n, ready, used, hi, rows=False):
                pl.wait_ge(loaded, n * 16 + 16)
                if used is not None:
                    pl.wait_ge(tile, used)
                view = (lambda t: t[:, x:x + 1, :]) if rows else (lambda t: t[:, :, 128 * x:128 * x + 128])
                one = ones[:, 0:1].unsqueeze(2).to_broadcast(view(raw).shape)
                pl.tensor_tensor(view(w[0]), view(raw), one, ALU.mult).then_inc(w_hi, 1)
                pl.wait_ge(w_hi, hi)
                pl.tensor_tensor(view(w[1]), view(raw), view(w[0]), ALU.subtract).then_inc(ready, 1)

            def ab(n, free, hi):
                for k, (raw, w, loaded, ready) in enumerate(
                        ((raw_a, wa, a_in, a_rdy), (raw_b, wb, b_in, b_rdy)) * 2):
                    split(raw, w, k // 2, loaded, n, ready, free[k] if free else None, hi + k)

            ab(N_GLU, None, 1)
            with pl.Fori(1, 4) as i:
                ab(i + N_GLU, [i * 4 + (T_GLU - 3 + k) for k in range(4)], i * 4 + 1)

            def ffn(layer, n0, t0, free, hi0):
                ab(n0, free, hi0)

                def c_chunk(i, hi):
                    for x in range(2):
                        split(raw_c, wc, x, c_in, i + layer * FP, c_rdy, i * 12 + (t0 + 1), hi + x,
                              rows=True)

                with pl.Fori(0, FP - 1) as i:
                    c_chunk(i, i * 6 + (hi0 + 4))
                    ab(i + (n0 + 1), [i * 12 + (t0 + 1 + k) for k in range(4)], i * 6 + (hi0 + 6))
                c_chunk(FP - 1, (FP - 1) * 6 + hi0 + 4)

            ffn(0, N_F0, T_F0, [T_GLU + 13 + k for k in range(4)], 17)
            hi1 = 17 + 6 * FP

            def kvq_split(n, free, hi, gain, sc):
                for k, (raw, w, loaded, ready) in enumerate(((raw_a, wa, a_in, a_rdy),
                                                             (raw_b, wb, b_in, b_rdy))):
                    pl.wait_ge(loaded, n * 16 + 16)
                    for x in range(2):
                        v = raw[:, :, 128 * x:128 * x + 128]
                        pl.tensor_tensor(v, v, gains[:, gain, :].unsqueeze(2).to_broadcast([P, KT, 128]),
                                         ALU.mult).then_inc(w_scaled, 1)
                    pl.wait_ge(w_scaled, sc + 2 * k + 1)
                    pl.wait_ge(tile, free[k])
                    for x in range(2):
                        v, w_h, w_l = (t[:, :, 128 * x:128 * x + 128] for t in (raw, *w))
                        pl.tensor_tensor(w_h, v, ones[:, 0:1].unsqueeze(2).to_broadcast([P, KT, 128]),
                                         ALU.mult).then_inc(w_hi, 1)
                        pl.wait_ge(w_hi, hi + 2 * k + x)
                        pl.tensor_tensor(w_l, v, w_h, ALU.subtract).then_inc(ready, 1)

            kvq_split(N_KVQ, [T_KVQ - 9, T_KVQ - 8], hi1, 1, 1)
            for i0, i1, gain in ((1, 4, 1), (4, 6, 2)):
                with pl.Fori(i0, i1) as i:
                    kvq_split(i + N_KVQ, [i * 4 + (T_KVQ - 2), i * 4 + T_KVQ], i * 4 + hi1,
                              gain, i * 4 + 1)

            def split_v(i):
                pl.wait_ge(v_in, i * 16 + 16)
                pl.tensor_tensor(v_hi[:, :, :], vraw[:, :, :],
                                 ones[:, 0:1].unsqueeze(2).to_broadcast([P, KT, VD]), ALU.mult)\
                    .then_inc(vh_done, 1)
                pl.wait_ge(vh_done, i + 1)
                pl.tensor_tensor(v_lo[:, :, :], vraw[:, :, :], v_hi[:, :, :], ALU.subtract)\
                    .then_inc(vl_done, 1)

            def low_x(i):
                pl.wait_ge(onh, i + 1)
                x1, x2 = (x[:, bass.ds(i, 1), :].rearrange("p o c -> p (o c)") for x in (x_lo, x_hi))
                pl.tensor_tensor(x1, onf[:, :], x2, ALU.subtract).then_inc(onl, 1)

            pl.wait_ge(tile, T_WO)
            split_v(0)
            with pl.Fori(1, NH) as i:
                pl.wait_ge(pv, i * 4)
                split_v(i)
                low_x(i - 1)
            hi2 = hi1 + 24
            pl.wait_ge(sc, 16 * NH)
            for x in range(2):
                split(raw_a, wa, x, a_in, N_WO, a_rdy, None, hi2 + x)
            low_x(NH - 1)
            pl.wait_ge(pv, 4 * NH)
            for x in range(2):
                split(raw_b, wb, x, b_in, N_WO, b_rdy, None, hi2 + 2 + x)
            ab(N_WO + 1, [T_WO + 1, T_WO + 3, T_WO + 2, T_WO + 4], hi2 + 4)
            ffn(1, N_F1, T_F1, [T_WO + 5, T_WO + 7, T_WO + 6, T_WO + 8], hi2 + 8)

        def two(n):
            return ps[:, 2 * n:2 * n + 2, :]

        def wide(t):
            return t.rearrange("p (b c) -> p b c", b=2)

        PT_USES = [(q, k0, min(4, q + 1 - k0)) for q in range(8) for k0 in range(0, q + 1, 4)]

        def pt_of(q):
            return [n for n, use in enumerate(PT_USES) if use[0] == q]

        def h_ready(m, k):
            return ((h_add, KT), (dve_ev, D_KVQ - 8 + k + 1), (dve_ev, D_WO + k + 1),
                    (dve_ev, D_F1 + FD - 8 + k + 1))[m]

        @block.tensor
        def _(pe):
            pe.wait_ge(consts_in, 16 * 8)
            for k in range(4):
                pe.wait_ge(sq_done, k + 1)
                for n in range(4):
                    pe.matmul(ps[:, 7, :], same_j[:, :], sq[k % 2][:, 4 * n:4 * n + 4, :],
                              start=(k == 0 and n == 0), stop=(k == 3 and n == 3))\
                        .then_inc(rms_pe if k == 3 and n == 3 else part_done, 1)

            def batch(n, kind, hf, k):
                b = n % 8
                if n == 7:
                    pe.wait_ge(rms_ms, 1)
                if n >= 8:
                    pe.wait_ge(*evacuated(n - 8))
                if kind == "wt":
                    if k == 0:
                        pe.wait_ge(w_tab, hf + 1)
                    for n4 in range(4):
                        src = (wr, wi)[n4 % 2][:, 2 * k + n4 // 2, :, :].rearrange("p a b -> p (a b)")
                        ins = pe.transpose(ps[:, b, P * n4:P * n4 + P], src, ident[:, :])
                elif kind == "v":
                    if k == 0 and hf == 0:
                        pe.wait_ge(u_done, 1)
                        pe.wait_ge(u_pool, 1)
                    pe.wait_ge(*evacuated(number["wt", hf, k]))
                    for n8 in range(8):
                        q, ri, gp = 2 * k + n8 // 4, n8 // 2 % 2, n8 % 2
                        c0 = 2 * P * (n8 // 4) + P * ri
                        ins = pe.matmul(ps[64 * gp:64 * gp + 64, b, c0:c0 + P],
                                        wt[:, q, ri, 64 * gp:64 * gp + 64],
                                        u[:, 2 * (HP * hf + q) + gp, :], start=True, stop=True)
                elif kind == "g":
                    if k == 0:
                        pe.wait_ge(s5_act, evacuated(number["wt", hf, 0])[1])
                        pe.wait_ge(c_tab, hf + 1)
                        pe.wait_ge(dd_done, hf + 1)
                    rows = slice(64 * (k % 2), 64 * (k % 2) + 64)
                    for n4 in range(4):
                        q, c0 = 4 * (k // 2) + n4, P * n4
                        g = 2 * q + k % 2
                        for ri, c in enumerate((cr, cn)):
                            lhs = w4[rows, q, ri, :, :].rearrange("p a b -> p (a b)")
                            pe.matmul(ps[:, b, c0 + CH:c0 + P], lhs,
                                      c[rows, q, 0:T - 1, :].rearrange("p a b -> p (a b)"),
                                      start=(n4 == 0 and ri == 0), stop=False, skip_group_check=True)
                            lhs = bz4[ri][rows, q, :, :, :].rearrange("p s a b -> p (s a b)")
                            pe.matmul(ps[:, b, c0:c0 + CH], lhs, c[rows, q, 0, :], start=False,
                                      stop=False, skip_group_check=True)
                        ins = pe.matmul(ps[:, b, c0:c0 + 32],
                                        ident4[:, :],
                                        dd[:, g, :], start=False, stop=True, skip_group_check=True)
                elif kind == "y":
                    if k == 0:
                        pe.wait_ge(scan_done, hf + 1)
                    pe.wait_ge(*evacuated(number["g", hf, k]))
                    rows = slice(64 * (k % 2), 64 * (k % 2) + 64)
                    for n4 in range(4):
                        q = 4 * (k // 2) + n4
                        g, o = 2 * q + k % 2, ps[:, b, P * n4:P * n4 + P]
                        pe.matmul(o, u[:, 2 * HP * hf + g, :], gt[:, g, :], start=True, stop=False)
                        for ri, c in enumerate((cr, cn)):
                            ins = pe.matmul(o, st[rows, q, ri, 0:NC],
                                            c[rows, q, 1:T + 1, :].rearrange("p a b -> p (a b)"),
                                            start=False, stop=(ri == 1))
                else:
                    if k == 0:
                        pe.wait_ge(*evacuated(number["y", 1, 7]))
                    for n4 in range(4):
                        j = 4 * (k % 2) + n4
                        ins = pe.transpose(ps[:, b, P * n4:P * n4 + P], z[:, k // 8, j, P * (k // 2 % 4):P * (k // 2 % 4) + P],
                                           ident[:, :])
                ins.then_inc(s5_full, 1)

            s5_batches(pe, [(kind, hf) for kind in ("wt", "v", "g", "y", "z") for hf in range(2)], batch)

            def product(slot, w, wcols, x, ks=range(KT)):
                for k in ks:
                    for n, (wn, xn) in enumerate(((0, 0), (0, 1), (1, 0))):
                        for c in range(2):
                            ins = pe.matmul(ps[:, 2 * slot + c, :], w[wn][:, k, wcols],
                                            x[xn][:, k, 512 * c:512 * c + 512],
                                            start=(k == ks[0] and n == 0), stop=(k == ks[-1] and n == 2))
                ins.then_inc(tile, 1)

            def two_products(ws, wcols, rows):
                for k in range(KT):
                    pe.wait_ge(nlo, rows + k + 1)
                    for slot, (w, cols_) in enumerate(zip(ws, wcols)):
                        for n, (wn, xn) in enumerate(((0, 0), (0, 1), (1, 0))):
                            for c in range(2):
                                ins = pe.matmul(ps[:, 2 * slot + c, :], w[wn][:, k, cols_],
                                                xs[xn][:, k, 512 * c:512 * c + 512],
                                                start=(k == 0 and n == 0), stop=(k == KT - 1 and n == 2))
                        if k == KT - 1:
                            ins.then_inc(tile, 1)

            xs = (x_hi, x_lo)
            halves = (slice(0, P), slice(P, 2 * P))

            pe.wait_ge(dve_ev, D_GLU)
            pe.wait_ge(act_ev, A_GLU)
            with pe.Fori(0, 4) as i:
                for x in range(2):
                    pe.wait_ge(a_rdy, i * 2 + (2 * N_GLU + x + 1))
                    pe.wait_ge(dve_ev, i * 2 + (D_GLU - 1 + x))
                    product(2 * x, wa, halves[x], xs)
                    pe.wait_ge(b_rdy, i * 2 + (2 * N_GLU + x + 1))
                    pe.wait_ge(act_ev, i * 2 + (A_GLU - 1 + x))
                    product(2 * x + 1, wb, halves[x], xs)

            def columns(m):
                pe.wait_ge(nacc, 7 * m + 7)
                for t in range(KT):
                    ins = pe.matmul(ps[:, 7, t:t + 1], tmp[2][:, P * t:P * t + P], ones[:, :],
                                    start=True, stop=True)
                ins.then_inc(ncol, 1)
                pe.wait_ge(nrs, m + 1)
                spread(ps, 6, rs, nbc)

            def spread(o, b, col, done):
                for t in range(KT):
                    ins = pe.matmul(o[:, b + t // 4, P * (t % 4):P * (t % 4) + P],
                                    col[:, t:t + 1].to_broadcast([P, P]), ident[:, :],
                                    start=True, stop=True)
                ins.then_inc(done, 1)

            def ffn(layer, n0, d0, a0, rows):
                def w1(x, n):
                    pe.wait_ge(a_rdy, n)
                    product((0, 2)[x], wa, halves[x], xs)

                def w3(x, n):
                    pe.wait_ge(b_rdy, n)
                    product((1, 3)[x], wb, halves[x], xs)

                def body(i, last):
                    pe.wait_ge(dve_ev, i * 10 + (d0 - 2))
                    w1(1, i * 2 + (2 * n0 + 2))
                    pe.wait_ge(dve_ev, i * 10 + (d0 - 1))
                    w3(1, i * 2 + (2 * n0 + 2))
                    if not last:
                        pe.wait_ge(act_ev, i * 2 + (a0 + 1))
                        pe.wait_ge(dve_ev, i * 10 + d0)
                        w1(0, i * 2 + (2 * n0 + 3))
                    pe.wait_ge(c_rdy, i * 2 + (2 * FP * layer + 2))
                    pe.wait_ge(hid_l, i * 2 + (2 * FP * layer + 2))
                    for n in range(8):
                        if n % 4 == 1 and n < 4:
                            pe.wait_ge(act_ev, i * 2 + (a0 + 2))
                        elif n == 3:
                            if not last:
                                pe.wait_ge(act_ev, i * 2 + (a0 + 3))
                        else:
                            pe.wait_ge(dve_ev, i * 10 + (d0 + (1, 0, 2, 0, 3, 4, 5, 6)[n]))
                        product((1, 2, 3, 0)[n % 4], wc, slice(P * n, P * n + P), hid, range(2))
                    if not last:
                        pe.wait_ge(dve_ev, i * 10 + (d0 + 7))
                        w3(0, i * 2 + (2 * n0 + 3))

                pe.wait_ge(a_rdy, 2 * n0 + 1)
                pe.wait_ge(b_rdy, 2 * n0 + 1)
                two_products((wa, wb), (halves[0], halves[0]), rows)
                with pe.Fori(0, FP - 1) as i:
                    body(i, False)
                body(FP - 1, True)

            columns(0)
            ffn(0, N_F0, D_F0, A_F0, 0)
            columns(1)

            def rotated(g, a0):
                def permuted(i, y):
                    pe.wait_ge(act_ev, i * 4 + (a0 + y + 1))
                    pe.wait_ge(dve_ev, i * 4 + (D_KVQ + 8 * g + y - 1))
                    for c in range(2):
                        ins = pe.matmul(ps[:, 4 + 2 * (y % 2) + c, :], perm[:, :],
                                        xk[y % 2][:, 512 * c:512 * c + 512], start=True, stop=True)
                    ins.then_inc(rotp, 1)

                def tiles(i, y0):
                    for y in range(y0, 4):
                        w, ready = ((wa, a_rdy), (wb, b_rdy))[y // 2]
                        pe.wait_ge(ready, i * 2 + (2 * N_KVQ + 8 * g + y % 2 + 1))
                        pe.wait_ge(act_ev, i * 4 + (a0 + y - 1))
                        product(y % 2, w, halves[y % 2], xs)
                        permuted(i, y - 1) if y else None
                    permuted(i, 3)

                if g == 0:
                    pe.wait_ge(a_rdy, 2 * N_KVQ + 2)
                    two_products((wa, wa), halves, KT)
                    permuted(0, 0)
                    tiles(0, 2)
                    tiles(1, 0)
                else:
                    with pe.Fori(0, 2) as i:
                        tiles(i, 0)

            rotated(0, A_KVQ)
            for c in range(4):
                s, (w, ready) = c % 2, ((wa, a_rdy), (wb, b_rdy))[c % 2]
                pe.wait_ge(ready, 2 * N_KVQ + 4 + 2 * (c // 2) + 2)
                pe.wait_ge(dve_ev, D_KVQ + 8)
                pe.wait_ge(act_ev, A_KVQ + 8 + max(0, c - 1))
                for t in range(KT):
                    for k in range(KT):
                        for n, (wn, xn) in enumerate(((0, 0), (0, 1), (1, 0))):
                            ins = pe.matmul(ps[:, 4 * s + t // 2, 256 * (t % 2):256 * (t % 2) + 256],
                                            xs[xn][:, k, P * t:P * t + P], w[wn][:, k, :],
                                            start=(k == 0 and n == 0), stop=(k == 7 and n == 2))
                ins.then_inc(tile, 2)
            rotated(1, A_KVQ + 12)

            def scores(i, q, n):
                for s in range(2):
                    if q:
                        pe.wait_ge(exd, i * 16 + (2 * q - 1 + s))
                    elif isinstance(i, int) and i == 0:
                        pe.wait_ge(dve_ev, D_WO)
                    else:
                        pe.wait_ge(exd, i * 16 + (s - 1))
                    ext = (q + 1) * P
                    for c in range(0, ext, 512):
                        w = max(256, min(512, ext - c))
                        for part_, qq in enumerate((q_hi, q_lo)):
                            ins = pe.matmul(ps[:, 2 * s + c // 512, 0:w], qq[n][:, s, P * q:P * q + P],
                                            kst[n][:, s, c:c + w], start=(part_ == 0), stop=(part_ == 1))
                    ins.then_inc(sc, 1)

            def turn_p(i, q):
                pe.wait_ge(p_done, i * 8 + (q + 1))
                for n in pt_of(q):
                    _, k0, cnt = PT_USES[n]
                    if n >= 2:
                        pe.wait_ge(ptl, i * 12 + (n - 1))
                    elif not (isinstance(i, int) and i == 0):
                        pe.wait_ge(ptl, i * 12 + (n - 1))
                    for k in range(cnt):
                        ins = pe.matmul(ps[:, 4 + n % 2, P * k:P * k + P],
                                        e1[q][:, P * (k0 + k):P * (k0 + k) + P], dg[q % 4][:, :],
                                        start=True, stop=True)
                    ins.then_inc(pt_tr, 1)

            def values(i, b):
                if b == 0:
                    pe.wait_ge(vl_done, i + 1)
                if b >= 2:
                    pe.wait_ge(oq, i * 4 + (b - 1))
                elif not (isinstance(i, int) and i == 0):
                    pe.wait_ge(onfd, i)
                pe.wait_ge(ptl, i * 12 + (pt_of(2 * b + 1)[-1] + 1))
                for k in range(2 * b + 2):
                    for n, (vv, pp) in enumerate(((v_hi, pt_hi), (v_hi, pt_lo), (v_lo, pt_hi))):
                        ins = pe.matmul(ps[:, 6 + b % 2, 0:256], vv[:, k, :], pp[:, k, :],
                                        start=(k == 0 and n == 0), stop=(k == 2 * b + 1 and n == 2))
                ins.then_inc(pv, 1)

            def step(i, q, n, cur, prev):
                if cur:
                    scores(i, q, n)
                if q % 2 == 0 and (cur if q >= 4 else prev):
                    values(i, q // 2 - 2) if q >= 4 else values(i - 1, q // 2 + 2)
                if q == 3 and prev:
                    pe.wait_ge(ors, i)
                    spread(ps, 6, rs, obc)
                if cur if q >= 2 else prev:
                    turn_p(i, q - 2) if q >= 2 else turn_p(i - 1, q + 6)
                if q == 2 and prev:
                    pe.wait_ge(oq, i * 4)
                    for t in range(KT):
                        ins = pe.matmul(ps[:, 7, t:t + 1], osq[:, P * t:P * t + P], ones[:, :],
                                        start=True, stop=True)
                    ins.then_inc(ocol, 1)

            def head(i, n, cur=True, prev=True, start=None):
                if cur:
                    pe.wait_ge(kq_in[n], start)
                for q in range(8 if cur else 4):
                    step(i, q, n, cur, prev)

            pe.wait_ge(act_ev, A_WO)
            head(0, 0, prev=False, start=96)
            with pe.Fori(0, 3) as j:
                head(j * 2 + 1, 1, start=j * 96 + 96)
                head(j * 2 + 2, 0, start=j * 96 + 192)
            head(NH - 1, 1, start=4 * 96)
            head(NH, 0, cur=False)

            pe.wait_ge(onl, NH)
            for i in range(2):
                for n, (w, ready) in enumerate(((wa, a_rdy), (wa, a_rdy), (wb, b_rdy), (wb, b_rdy))):
                    pe.wait_ge(ready, 2 * (N_WO + i) + n % 2 + 1)
                    if i:
                        pe.wait_ge(dve_ev, D_WO + n + 1)
                    product(n, w, halves[n % 2], xs)
            columns(2)
            ffn(1, N_F1, D_F1, A_F1, 2 * KT)
            pe.wait_ge(nacc, 28)
            for t in range(KT):
                ins = pe.matmul(ps[:, 7, t:t + 1], tmp[2][:, P * t:P * t + P], ones[:, :],
                                start=True, stop=True)
            ins.then_inc(ncol, 1)
            pe.wait_ge(nrs, 4)
            spread(ps, 6, rs, nbc)

        @block.scalar
        def _(ac):
            steps = [0]

            def step(ins):
                steps[0] += 1
                ins.then_inc(act, 1)
                ac.wait_ge(act, steps[0])

            ac.wait_ge(params_in, 16)
            ac.activation(prm[:, 3, :], prm[:, 2, :], ACT.Exp).then_inc(prm_exp, 1)
            ac.wait_ge(prm_arg, 1)
            ac.activation(prm[:, 6, :], prm[:, 4, :], ACT.Exp).then_inc(prm_exp, 1)
            ac.wait_ge(lam_d, 1)
            ac.activation(lams[:, 0:2], lams[:, 0:2], ACT.Exp).then_inc(lam_e, 1)
            ac.wait_ge(prm_arg, 2)
            ac.activation(prm[:, 9, :], prm[:, 8, :], ACT.Sin).then_inc(prm_sin, 1)
            ac.activation(prm[:, 10, :], prm[:, 8, :], ACT.Sin, scale=0.5).then_inc(prm_sin, 1)
            for k in range(4):
                ac.wait_ge(u_in[k], 16)
                if k >= 2:
                    ac.wait_ge(part_done, 4 * k - 4)
                ac.activation(sq[k % 2][:, :, :], u[:, 16 * k:16 * k + 16, :], ACT.Square)\
                    .then_inc(sq_done, 1)
            ac.wait_ge(rms_ms, 1)
            ac.activation(rfull[:, :], rfull[:, :], ACT.Sqrt).then_inc(rms_rt, 1)

            def batch(n, kind, hf, k):
                b = n % 8
                if kind == "wt" and k == 0:
                    ac.wait_ge(w_tab, hf + 1)
                    for ri, w in enumerate((wr, wi)):
                        ac.activation(w4[:, :, ri, :, :], w[:, :, T - 2:T, :].rearrange("p q a b -> p q (a b)")
                                      .unsqueeze(2).to_broadcast([P, HP, 4, 2 * CH]), ACT.Copy)
                ac.wait_ge(s5_full, n + 1)
                if kind == "wt":
                    ac.activation(wt[:, 2 * k:2 * k + 2, :, :].rearrange("p q r c -> p (q r c)"),
                                  ps[:, b, :], ACT.Copy).then_inc(s5_act, 1)
                elif kind == "v":
                    ac.activation(st[:, 2 * k:2 * k + 2, :, 1:NC + 1],
                                  ps[:, b, :].rearrange("p (q r c) -> p q r c", q=2, r=2), ACT.Copy)\
                        .then_inc(s5_act, 1)
                elif kind == "g":
                    src = ps[:, b, :].rearrange("p (g c) -> p g c", g=4)
                    g0 = 8 * (k // 2) + k % 2
                    for q in range(4):
                        ins = ac.activation(gt[32 * q:32 * q + 32, g0:g0 + 7:2, 32 * q:P],
                                            src[32 * q:32 * q + 32, :, 0:P - 32 * q], ACT.Copy)
                    ins.then_inc(s5_act, 1)
                elif kind == "y":
                    c0 = 32 * 4 * (k // 2)
                    o = z[:, hf, :, c0:c0 + P].rearrange("p j (s x) -> p s j x", x=32)
                    o = o[:, :, :, CH * (k % 2):CH * (k % 2) + CH]
                    ac.activation(o, ps[:, b, :].rearrange("p (s j x) -> p s j x", s=4, x=CH),
                                  ACT.Gelu_apprx_tanh).then_inc(s5_act, 1)
                else:
                    o = x_hi[:, k // 2, :].rearrange("p (c j) -> p j c", j=T)
                    o = o[:, 4 * (k % 2):4 * (k % 2) + 4, :]
                    ins = ac.activation(o, ps[:, b, :].rearrange("p (j c) -> p j c", j=4), ACT.Copy)
                    ins.then_inc(act_ev, A_GLU) if k == 15 else ins.then_inc(z_hi, 1)

            ac.wait_ge(prm_done, 2)
            ac.activation(gt[:, :, :], ones[:, 0:1].unsqueeze(2).to_broadcast([P, 2 * HP, P]), ACT.Copy,
                          scale=0.0)
            s5_batches(ac, [(kind, hf) for kind in ("wt", "v", "g", "y", "z") for hf in range(2)], batch)

            def gates(i):
                for x in range(2):
                    ac.wait_ge(tile, i * 4 + (T_GLU + 2 + 2 * x))
                    if not isinstance(i, int):
                        ac.wait_ge(dve_ev, i * 2 + (D_GLU - 1 + x))
                    ac.activation(wide(tmp[x][:, :]), two(1 + 2 * x), ACT.Sigmoid).then_inc(act_ev, 1)

            gates(0)
            with ac.Fori(1, 4) as i:
                gates(i)

            def norm(m):
                for k in range(KT):
                    ac.wait_ge(*h_ready(m, k))
                    if k >= 3:
                        ac.wait_ge(nacc, 7 * m + k - 2)
                    ac.activation((tmp[2] if k == 0 else tmp[1 - k % 2])[:, :], h[:, k, :], ACT.Square)\
                        .then_inc(nsq, 1)
                ac.wait_ge(nms, m + 1)
                ac.activation(rt[:, :], ms[:, :], ACT.Sqrt).then_inc(nrt, 1)
                if m < 3:
                    for k in range(KT):
                        ac.wait_ge(nf, KT * m + k + 1)
                        ac.activation(x_hi[:, k, :], tmp[k % 2][:, :], ACT.Copy).then_inc(nhi, 1)

            def ffn(layer, t0, d0):
                def silu(x, at):
                    ac.wait_ge(tile, at)
                    ac.activation(wide(tmp[x][:, :]), two(2 * x), ACT.Silu).then_inc(act_ev, 1)

                def high(x, n):
                    ac.wait_ge(dve_ev, n)
                    ac.activation(hid[0][:, x, :], tmp[2][:, :], ACT.Copy).then_inc(hid_h, 1)

                def body(i, last):
                    high(0, i * 10 + (d0 + 1))
                    silu(1, i * 12 + (t0 + 3))
                    high(1, i * 10 + (d0 + 2))
                    if not last:
                        silu(0, i * 12 + (t0 + 5))

                silu(0, t0 + 1)
                with ac.Fori(0, FP - 1) as i:
                    body(i, False)
                body(FP - 1, True)

            norm(0)
            ffn(0, T_F0, D_F0)
            norm(1)

            def rotated(g, a0, t0):
                def high(n):
                    m = 8 * g + n
                    ac.wait_ge(rsum, m + 1)
                    if m >= 2:
                        ac.wait_ge(stored[n % 2], 32 * (m // 2))
                    ac.activation(rk_hi[n % 2][:, :], rk[n % 2][:, :], ACT.Copy).then_inc(rhi, 1)

                for n in range(8):
                    ac.wait_ge(tile, t0 + n + 1)
                    ac.activation(wide(xk[n % 2][:, :]), two(n % 2), ACT.Copy).then_inc(act_ev, 1)
                    if n:
                        high(n - 1)
                high(7)

            rotated(0, A_KVQ, T_KVQ)
            for c in range(4):
                ac.wait_ge(tile, T_KVQ + 8 + 2 * c + 2)
                if c >= 2:
                    ac.wait_ge(v_stored[c % 2], 16)
                ac.activation(stg[c % 2][:, :, :].rearrange("p (b x) c -> p b (x c)", x=2),
                              ps[:, 4 * (c % 2):4 * (c % 2) + 4, :], ACT.Copy).then_inc(act_ev, 1)
            rotated(1, A_KVQ + 12, T_KVQ + 16)

            def exps(i, q):
                for s, e in enumerate((e1[q], e2[q % 2])):
                    ac.wait_ge(nbd, i * 16 + (2 * q + s + 1))
                    ext = (q + 1) * P
                    ac.activation(e[:, 0:ext],
                                  ps[:, 2 * s:2 * s + 2, :].rearrange("p b c -> p (b c)")[:, 0:ext],
                                  ACT.Exp, bias=nb[:, 2 * q + s:2 * q + s + 1], scale=SCALE,
                                  accum_out=es[:, 2 * q + s:2 * q + s + 1]).then_inc(exd, 1)

            def turned_p(i, q):
                if isinstance(i, int) and i == 0 and q == 0:
                    ac.wait_ge(stored[0], 256)
                    ac.wait_ge(stored[1], 256)
                for n in pt_of(q):
                    _, k0, cnt = PT_USES[n]
                    c0 = P * (q % 2)
                    ac.wait_ge(pt_tr, i * 12 + (n + 1))
                    ac.activation(pt_hi[:, k0:k0 + cnt, c0:c0 + P],
                                  ps[:, 4 + n % 2, 0:P * cnt].rearrange("p (k c) -> p k c", c=P),
                                  ACT.Copy).then_inc(pth, 1)

            def outputs(i, b):
                ac.wait_ge(pv, i * 4 + (b + 1))
                if b == 0 and not (isinstance(i, int) and i == 0):
                    ac.wait_ge(onl, i)
                o = ps[:, 6 + b % 2, 0:256]
                ac.activation(otf[:, 256 * b:256 * b + 256], o, ACT.Copy).then_inc(oc, 1)
                ac.activation(osq[:, 256 * b:256 * b + 256], o, ACT.Square).then_inc(oq, 1)

            def step(i, q, cur, prev):
                if q == 3 and prev:
                    ac.wait_ge(oms, i)
                    ac.activation(rt[:, :], ms[:, :], ACT.Sqrt).then_inc(ort, 1)
                if cur:
                    exps(i, q)
                if q % 2 == 0 and (cur if q >= 4 else prev):
                    outputs(i, q // 2 - 2) if q >= 4 else outputs(i - 1, q // 2 + 2)
                if cur if q >= 2 else prev:
                    turned_p(i, q - 2) if q >= 2 else turned_p(i - 1, q + 6)
                if q == 3 and prev:
                    ac.wait_ge(onfd, i)
                    ac.wait_ge(onfd, 1)
                    ac.activation(x_hi[:, i - 1, :] if isinstance(i, int) else
                                  x_hi[:, bass.ds(i - 1, 1), :].rearrange("p o c -> p (o c)"),
                                  onf[:, :], ACT.Copy).then_inc(onh, 1)

            def head(i, cur=True, prev=True):
                for q in range(8 if cur else 4):
                    step(i, q, cur, prev)

            head(0, prev=False)
            with ac.Fori(1, NH) as i:
                head(i)
            head(NH, cur=False)
            norm(2)
            ffn(1, T_F1, D_F1)
            norm(3)

        @block.vector
        def _(ve):
            steps = [0]

            def step(ins, wait=True):
                steps[0] += 1
                ins.then_inc(dve, 1)
                if wait:
                    ve.wait_ge(dve, steps[0])

            tt, ts = ve.tensor_tensor, ve.tensor_scalar

            p = lambda n: prm[:, n, :]
            ve.wait_ge(params_in, 16)
            ve.wait_ge(prm_exp, 1)
            step(tt(p(4), p(0), p(3), ALU.mult), False)
            step(tt(p(5), p(1), p(3), ALU.mult))
            ts(p(7), p(5), 1 / (2 * math.pi), MAGIC, ALU.mult, ALU.add).then_inc(prm_arg, 1)
            ve.wait_ge(prm_arg, 1)
            step(ts(p(7), p(7), -MAGIC, None, ALU.add))
            for n, part_pi in enumerate(TWO_PI):
                step(ve.scalar_tensor_tensor(out=p(8), in0=p(7), scalar=-part_pi,
                                             in1=p(5) if n == 0 else p(8), op0=ALU.mult, op1=ALU.add))
            ts(p(8), p(8), PI_F, -PI_F, ALU.min, ALU.max).then_inc(prm_arg, 1)
            step(tt(p(16), p(0), p(0), ALU.mult), False)
            step(tt(p(17), p(1), p(1), ALU.mult))
            step(tt(p(16), p(16), p(17), ALU.add))
            step(ve.reciprocal(p(20), p(16)))
            ve.wait_ge(consts_in, 16 * 8)
            step(tt(lamp[:, :, :], lamv[:, 0:4:2, :], lamv[:, 1:4:2, :], ALU.mult))
            ve.tensor_reduce(lams[:, 0:2], lamp[:, :, :], AX.X, ALU.add).then_inc(lam_d, 1)
            ve.wait_ge(prm_sin, 2)
            ve.wait_ge(prm_exp, 2)
            step(tt(p(11), p(10), p(10), ALU.mult))
            step(ts(p(12), p(11), -2.0, 1.0, ALU.mult, ALU.add))
            step(tt(p(13), p(6), p(12), ALU.mult), False)
            step(tt(p(14), p(6), p(9), ALU.mult))
            step(ts(p(15), p(13), -1.0, None, ALU.add))
            step(tt(p(17), p(15), p(0), ALU.mult), False)
            step(tt(p(18), p(14), p(1), ALU.mult), False)
            step(tt(p(19), p(14), p(0), ALU.mult), False)
            step(tt(p(21), p(15), p(1), ALU.mult))
            step(tt(p(17), p(17), p(18), ALU.add), False)
            step(tt(p(19), p(19), p(21), ALU.subtract))
            step(tt(p(22), p(17), p(20), ALU.mult), False)
            step(tt(p(23), p(19), p(20), ALU.mult))
            ve.wait_ge(lam_e, 1)
            step(tt(lams[:, 2:3], lams[:, 1:2], lams[:, 0:1], ALU.subtract), False)
            step(ts(subg[:, :], subg[:, :], 1 - LAM_INIT, None, ALU.mult))
            ts(lams[:, 3:4], lams[:, 2:3], -LAM_INIT, None, ALU.add).then_inc(lam_done, 1)

            def cmul(out, x, y, n):
                t = [pt4[m][:, 0:n, :] for m in range(4)]
                yr, yi = (v.to_broadcast([P, n, NP]) for v in y)
                step(tt(t[0], x[0], yr, ALU.mult), False)
                step(tt(t[1], x[1], yi, ALU.mult), False)
                step(tt(t[2], x[0], yi, ALU.mult), False)
                step(tt(t[3], x[1], yr, ALU.mult))
                step(tt(out[0], t[0], t[1], ALU.subtract), False)
                step(tt(out[1], t[2], t[3], ALU.add))

            dn = lambda k0, k1: [pw_d[:, r, k0:k1, :] for r in range(2)]
            up = lambda k0, k1: [pw_8[:, r, k0:k1, :] for r in range(2)]
            step(ve.memset(pw_d[:, 0, 8, :], 1.0), False)
            step(ve.memset(pw_d[:, 1, 8, :], 0.0), False)
            step(ve.tensor_copy(pw_d[:, 0, 7, :], p(13)), False)
            step(ve.tensor_copy(pw_d[:, 1, 7, :], p(14)))
            cmul(dn(6, 7), dn(7, 8), dn(7, 8), 1)
            cmul(dn(4, 6), dn(6, 8), dn(6, 7), 2)
            cmul(dn(0, 4), dn(4, 8), dn(4, 5), 4)
            ve.tensor_copy(pw_a[:, :, :, :], pw_d[:, :, ::-1, :]).then_inc(prm_done, 1)
            ve.wait_ge(bc_in, 112)
            for n in range(2):
                step(tt(b_raw[n][:, :, :], b_raw[n][:, :, :], g_b[:, :, :], ALU.mult), n == 1)
            step(tt(d_two[:, :], d_two[:, :], g_two[:, :], ALU.mult))
            f_r, f_i = (p(n).unsqueeze(2).to_broadcast([P, NP, CH]) for n in (22, 23))
            t = [x[:, 4 * n:4 * n + 4, :, :].rearrange("p q k c -> p (q k) c")
                 for n in range(2) for x in (m1, m2)]
            step(tt(t[0], f_r, b_raw[0][:, :, :], ALU.mult), False)
            step(tt(t[1], f_i, b_raw[1][:, :, :], ALU.mult), False)
            step(tt(t[2], f_r, b_raw[1][:, :, :], ALU.mult), False)
            step(tt(t[3], f_i, b_raw[0][:, :, :], ALU.mult))
            step(tt(b_raw[0][:, :, :], t[0], t[1], ALU.subtract), False)
            tt(b_raw[1][:, :, :], t[2], t[3], ALU.add).then_inc(prm_done, 1)
            ve.wait_ge(prm_done, 2)
            step(ve.tensor_copy(up(0, 1)[0], dn(0, 1)[0]), False)
            step(ve.tensor_copy(up(0, 1)[1], dn(0, 1)[1]))
            cmul(up(1, 2), up(0, 1), up(0, 1), 1)
            cmul(up(2, 4), up(0, 2), up(1, 2), 2)
            cmul(up(4, 8), up(0, 4), up(3, 4), 4)

            def token_rms():
                ve.wait_ge(rms_pe, 1)
                step(ve.tensor_reduce(ssq[:, :], ps[:, 7, :].rearrange("p (g c) -> p c g", c=NC), AX.X,
                                      ALU.add))
                ts(rfull[:, :], ssq[:, :], 1.0 / D, EPS, ALU.mult, ALU.add).then_inc(rms_ms, 1)
                ve.wait_ge(rms_rt, 1)
                ve.reciprocal(rfull[:, :], rfull[:, :]).then_inc(rms_rs, 1)
                ve.wait_ge(rms_rs, 1)
                tt(u[:, 0:44, :], u[:, 0:44, :], rfull[:, :].unsqueeze(1).to_broadcast([P, 44, NC]),
                   ALU.mult).then_inc(u_done, 1)

            for hf in range(2):
                half = slice(HP * hf, HP * hf + HP)
                if hf:
                    ve.wait_ge(s5_full, number["g", 0, 7] + 1)
                shape = [P, HP, T, CH]
                pr, pi = (pw_d[:, n, 1:T + 1, half].rearrange("p k q -> p q k").unsqueeze(3)
                          .to_broadcast(shape) for n in range(2))
                b_r, b_i = (b_raw[n][:, half, :].unsqueeze(2).to_broadcast(shape) for n in range(2))
                step(tt(m1[:, :, :, :], pr, b_r, ALU.mult), False)
                step(tt(m2[:, :, :, :], pi, b_i, ALU.mult))
                step(tt(wr[:, :, :, :], m1[:, :, :, :], m2[:, :, :, :], ALU.subtract))
                step(tt(m1[:, :, :, :], pr, b_i, ALU.mult), False)
                step(tt(m2[:, :, :, :], pi, b_r, ALU.mult))
                tt(wi[:, :, :, :], m1[:, :, :, :], m2[:, :, :, :], ALU.add).then_inc(w_tab, 1)
                tt(dd[:, :, :], ident[0:32, 0:32].unsqueeze(1).to_broadcast([32, 2 * HP, 32]),
                   d_two[:, 2 * HP * hf:2 * HP * hf + 2 * HP].unsqueeze(2).to_broadcast([32, 2 * HP, 32]),
                   ALU.mult).then_inc(dd_done, 1)
                if hf == 0:
                    token_rms()

                if hf == 0:
                    step(ve.memset(st[:, :, :, 0:1], 0.0))
                ve.wait_ge(*evacuated(number["v", hf, 7]))
                S = st[:, :, :, 1:NC + 1].rearrange("p q i (m r) -> p q i m r", r=R)

                def advance(cur, prev, power, m0, m):
                    a_r, a_i = (pw_8[:, n, power - 1, half] for n in range(2))
                    both = a_r.unsqueeze(2).unsqueeze(3).to_broadcast([P, HP, 2, m])
                    one = a_i.unsqueeze(2).to_broadcast([P, HP, m])
                    x, y = ta[:, :, :, 0:m], tb[:, :, :, 0:m]
                    step(tt(x, prev, both, ALU.mult), False)
                    step(ve.scalar_tensor_tensor(out=y[:, :, 0, :], in0=prev[:, :, 1, :], scalar=-1.0,
                                                 in1=one, op0=ALU.mult, op1=ALU.mult), False)
                    step(tt(y[:, :, 1, :], prev[:, :, 0, :], one, ALU.mult))
                    step(tt(cur, cur, x, ALU.add))
                    step(tt(cur, cur, y, ALU.add))

                for r in range(1, R):
                    advance(S[:, :, :, :, r], S[:, :, :, :, r - 1], 1, 0, M)
                for m in range(1, M):
                    advance(S[:, :, :, m:m + 1, R - 1], S[:, :, :, m - 1:m, R - 1], R, 0, 1)
                for r in range(R - 1):
                    advance(S[:, :, :, 1:M, r], S[:, :, :, 0:M - 1, R - 1], r + 1, 0, M - 1)
                ve.tensor_copy(ta[:, 0, 0, 0:1], ta[:, 0, 0, 0:1]).then_inc(scan_done, 1)
                ve.wait_ge(scan_done, hf + 1)

            for k in range(16):
                n = number["z", 0, k]
                ve.wait_ge(s5_full, n + 1)
                ve.wait_ge(act_ev, A_GLU) if k == 15 else ve.wait_ge(z_hi, k + 1)
                o, i_ = (x[:, k // 2, :].rearrange("p (c j) -> p j c", j=T)
                         [:, 4 * (k % 2):4 * (k % 2) + 4, :] for x in (x_lo, x_hi))
                ins = tt(o, ps[:, n % 8, :].rearrange("p (j c) -> p j c", j=4), i_, ALU.subtract)
                ins.then_inc(dve_ev, D_GLU) if k == 15 else ins.then_inc(s5_dve, 1)

            ve.wait_ge(h_in, 16)
            with ve.Fori(0, 4) as i:
                for x in range(2):
                    ve.wait_ge(tile, i * 4 + (T_GLU + 1 + 2 * x))
                    ve.wait_ge(act_ev, i * 2 + (A_GLU + 1 + x))
                    tt(wide(tmp[2][:, :]), two(2 * x), wide(tmp[x][:, :]), ALU.mult).then_inc(dve_ev, 1)
                    ve.wait_ge(dve_ev, i * 2 + (D_GLU + 1 + x))
                    hk = h[:, bass.ds(i * 2 + x, 1), :].rearrange("p o c -> p (o c)")
                    tt(hk, hk, tmp[2][:, :], ALU.add).then_inc(h_add, 1)
                    ve.wait_ge(h_add, i * 2 + (x + 1))

            def accumulated(m, k):
                ve.wait_ge(nsq, KT * m + k + 1)
                if k >= 2:
                    ve.wait_ge(nacc, 7 * m + k - 1)
                tt(tmp[2][:, :], tmp[2][:, :], tmp[1 - k % 2][:, :], ALU.add).then_inc(nacc, 1)

            def norm(m, gain, k0):
                for k in range(k0, KT):
                    accumulated(m, k)
                ve.wait_ge(ncol, m + 1)
                ts(ms[:, :], ps[:, 7, 0:KT], 1.0 / D, EPS, ALU.mult, ALU.add).then_inc(nms, 1)
                ve.wait_ge(nrt, m + 1)
                ve.reciprocal(rs[:, :], rt[:, :]).then_inc(nrs, 1)
                ve.wait_ge(nbc, m + 1)

                def full(k):
                    if m == 3 and k >= 2:
                        ve.wait_ge(out_done[k % 2], 16 * (k // 2))
                    if m < 3 and k >= 2:
                        ve.wait_ge(nlo, KT * m + k - 1)
                    ve.scalar_tensor_tensor(out=wide(tmp[k % 2][:, :]), in0=wide(h[:, k, :]),
                                            scalar=1.0 if gain is None else gains[:, gain, k:k + 1],
                                            in1=two(3), op0=ALU.mult, op1=ALU.mult).then_inc(nf, 1)

                def low(k):
                    ve.wait_ge(nhi, KT * m + k + 1)
                    tt(x_lo[:, k, :], tmp[k % 2][:, :], x_hi[:, k, :], ALU.subtract).then_inc(nlo, 1)

                full(0)
                for k in range(KT):
                    if k + 1 < KT:
                        full(k + 1)
                    if m < 3:
                        low(k)

            def ffn(layer, t0, d0, a0):
                n = 2 * FP * layer

                def body(i, last):
                    for x in range(2):
                        ve.wait_ge(tile, i * 12 + (t0 + 2 + 2 * x))
                        ve.wait_ge(act_ev, i * 2 + (a0 + 1 + x))
                        tt(wide(tmp[2][:, :]), two(1 + 2 * x), wide(tmp[x][:, :]), ALU.mult)\
                            .then_inc(dve_ev, 1)
                        ve.wait_ge(hid_h, i * 2 + (n + 1 + x))
                        tt(hid[1][:, x, :], tmp[2][:, :], hid[0][:, x, :], ALU.subtract).then_inc(hid_l, 1)
                        ve.wait_ge(hid_l, i * 2 + (n + 1 + x))
                    for k in range(KT):
                        ve.wait_ge(tile, i * 12 + (t0 + 6 + k) if not last else i * 12 + (t0 + 5 + k))
                        hk = wide(h[:, k, :])
                        tt(hk, hk, two((1, 2, 3, 0)[k % 4]), ALU.add).then_inc(dve_ev, 1)
                        if last and k >= 2:
                            accumulated(2 * layer + 1, k - 1)

                return body

            def run_ffn(layer, t0, d0, a0):
                body = ffn(layer, t0, d0, a0)
                with ve.Fori(0, FP - 1) as i:
                    body(i, False)
                body(FP - 1, True)

            norm(0, 0, 1)
            run_ffn(0, T_F0, D_F0, A_F0)
            norm(1, None, KT - 1)

            ve.wait_ge(rot_in, 32)

            def rotated(g, a0):
                def low(n):
                    m = 8 * g + n
                    ve.wait_ge(rhi, m + 1)
                    if m >= 2:
                        ve.wait_ge(stored[n % 2], 32 * (m // 2))
                    tt(rk_lo[n % 2][:, :], rk[n % 2][:, :], rk_hi[n % 2][:, :], ALU.subtract)\
                        .then_inc(rlo, 1)

                for n in range(8):
                    m, x, y = 8 * g + n, xk[n % 2], rk[n % 2]
                    ve.wait_ge(act_ev, a0 + n + 1)
                    if m >= 2:
                        ve.wait_ge(rlo, m - 1)
                    step(tt(y[:, :], x[:, :], cos_t[:, :], ALU.mult))
                    ve.wait_ge(rotp, m + 1)
                    tt(wide(x[:, :]), two(2 + n % 2), wide(sin_t[:, :]), ALU.mult).then_inc(dve_ev, 1)
                    ve.wait_ge(dve_ev, D_KVQ + m + 1)
                    tt(y[:, :], y[:, :], x[:, :], ALU.add).then_inc(rsum, 1)
                    if n:
                        low(n - 1)
                low(7)

            rotated(0, A_KVQ)
            rotated(1, A_KVQ + 12)

            def maxima(i, q):
                for s in range(2):
                    n, ext = 2 * q + s, (q + 1) * P
                    flat = ps[:, 2 * s:2 * s + 2, :].rearrange("p b c -> p (b c)")
                    ve.wait_ge(sc, i * 16 + (n + 1))
                    ve.memset(flat[0:64, ext - 64:ext], NEG).then_inc(masked, 1)
                    ve.wait_ge(masked, i * 16 + (n + 1))
                    ve.tensor_reduce(mx[:, n:n + 1], flat[:, 0:ext], AX.X, ALU.max).then_inc(mxd, 1)
                    ve.wait_ge(mxd, i * 16 + (n + 1))
                    ts(nb[:, n:n + 1], mx[:, n:n + 1], -SCALE, None, ALU.mult).then_inc(nbd, 1)

            def combined(i, q):
                ve.wait_ge(exd, i * 16 + (2 * q + 2))
                ve.reciprocal(er[:, 2 * q:2 * q + 2], es[:, 2 * q:2 * q + 2]).then_inc(er_done, 1)
                ve.wait_ge(er_done, i * 8 + (q + 1))
                ve.scalar_tensor_tensor(out=ec[:, q:q + 1], in0=es[:, 2 * q:2 * q + 1],
                                        scalar=er[:, 2 * q + 1:2 * q + 2], in1=lams[:, 3:4],
                                        op0=ALU.mult, op1=ALU.mult).then_inc(ec_done, 1)
                ts(dg[q % 4][:, :], ident[:, :], er[:, 2 * q:2 * q + 1], None, ALU.mult)
                ve.wait_ge(ec_done, i * 8 + (q + 1))
                p1_, p2_ = (e[:, 0:(q + 1) * P] for e in (e1[q], e2[q % 2]))
                ve.scalar_tensor_tensor(out=p1_, in0=p2_, scalar=ec[:, q:q + 1], in1=p1_,
                                        op0=ALU.mult, op1=ALU.add).then_inc(p_done, 1)

            def turned_p(i, q):
                for n in pt_of(q):
                    _, k0, cnt = PT_USES[n]
                    c0 = P * (q % 2)
                    ve.wait_ge(pth, i * 12 + (n + 1))
                    if q % 2 == 0 and k0 == 0:
                        ve.memset(pt_hi[:, q + 1, 0:P].bitcast(F32), 0.0)
                        ve.memset(pt_lo[:, q + 1, 0:P].bitcast(F32), 0.0)
                    tt(pt_lo[:, k0:k0 + cnt, c0:c0 + P],
                       ps[:, 4 + n % 2, 0:P * cnt].rearrange("p (k c) -> p k c", c=P),
                       pt_hi[:, k0:k0 + cnt, c0:c0 + P], ALU.subtract).then_inc(ptl, 1)

            def step_(i, q, cur, prev):
                if q == 3 and prev:
                    ve.wait_ge(ocol, i)
                    ts(ms[:, :], ps[:, 7, 0:KT], 1.0 / VD, EPS, ALU.mult, ALU.add).then_inc(oms, 1)
                if cur:
                    maxima(i, q)
                if q == 3 and prev:
                    ve.wait_ge(ort, i)
                    ve.reciprocal(rs[:, :], rt[:, :]).then_inc(ors, 1)
                if cur if q else prev:
                    combined(i, q - 1) if q else combined(i - 1, 7)
                if q == 3 and prev:
                    ve.wait_ge(obc, i)
                    ve.scalar_tensor_tensor(out=wide(onf[:, :]), in0=wide(otf[:, :]), scalar=subg[:, 0:1],
                                            in1=two(3), op0=ALU.mult, op1=ALU.mult).then_inc(onfd, 1)
                if cur if q >= 2 else prev:
                    turned_p(i, q - 2) if q >= 2 else turned_p(i - 1, q + 6)

            def head(i, cur=True, prev=True):
                for q in range(8 if cur else 4):
                    step_(i, q, cur, prev)

            ve.wait_ge(lam_done, 1)
            head(0, prev=False)
            with ve.Fori(1, NH) as i:
                head(i)
            head(NH, cur=False)

            for k in range(KT):
                ve.wait_ge(tile, T_WO + k + 1)
                hk = wide(h[:, k, :])
                tt(hk, hk, two(k % 4), ALU.add).then_inc(dve_ev, 1)
                if k >= 2:
                    accumulated(2, k - 1)
            norm(2, 3, KT - 1)
            run_ffn(1, T_F1, D_F1, A_F1)
            norm(3, 4, KT - 1)


def kernel(**inputs):
    import concourse.bacc as _bacc
    from concourse.bass_utils import run_bass_kernel_spmd as _run

    i = {k: np.asarray(v) for k, v in inputs.items()}

    def states(x):
        return x.reshape(NP, P).T

    def cols(w):
        k, n = w.shape
        return w.reshape(k // P, P, n // 256, 256).transpose(2, 1, 0, 3).reshape(n // 256, P, -1)

    def tiles(g):
        return g.reshape(KT, P).T

    x = i["x"][0]
    lr, li = states(i["ssm_lam_re"][0]), states(i["ssm_lam_im"][0])
    dt = states(np.broadcast_to(i["ssm_log_dt"][0][:, None], (NG, 64)))
    pos = np.arange(L, dtype=np.float32)
    freq = np.float32(500000.0) ** (-np.arange(8, dtype=np.float32) * np.float32(2.0) / np.float32(16))
    ang = (freq[:, None] * pos[None, :]).astype(np.float32)
    rest = np.zeros((48, L), np.float32)
    cos_t = np.concatenate([np.cos(ang), np.cos(ang), rest + 1] * 2)
    sin_t = np.concatenate([np.sin(ang), np.sin(ang), rest] * 2)
    perm = np.zeros((P, P), np.float32)
    for d in range(8):
        for r0 in (0, 64):
            perm[r0 + d + 8, r0 + d], perm[r0 + d, r0 + d + 8] = -1, 1
    g_mix = i["norm_mix_g"][0].reshape(NP, 2, 1, CH)
    data = {
        "ident": np.eye(P, dtype=np.float32),
        "ident4": np.tile(np.eye(32, dtype=np.float32), (1, 4)),
        "same_j": np.kron(np.eye(T), np.ones((CH, CH))).astype(np.float32),
        "ones": np.ones((P, 1), np.float32),
        "gains": np.stack([tiles(i["norm_ffn_g"][0]), tiles(i["kv_norm_g"]), tiles(i["norm_mix_g"][1]),
                           tiles(i["norm_ffn_g"][1]), tiles(i["final_norm_g"])], 1),
        "subg": i["attn_subln_g"][0][:, None],
        "cos_t": cos_t, "sin_t": sin_t, "perm": perm,
        "lamv": np.broadcast_to(np.stack([i[f"attn_{n}"][0] for n in ("lq1", "lk1", "lq2", "lk2")])[None],
                                (P, 4, 64)),
        "ssm_prm": np.stack([lr, li, dt], 1),
        "x_u": x.reshape(NC, T, NG, CH).transpose(1, 3, 2, 0).reshape(P, NG, NC),
        "x_t": x.T.reshape(KT, P, L).transpose(1, 0, 2),
        "ssm_b_re": i["ssm_b_re"][0].reshape(NP, P, CH).transpose(1, 0, 2),
        "ssm_b_im": i["ssm_b_im"][0].reshape(NP, P, CH).transpose(1, 0, 2),
        "ssm_c_re": i["ssm_c_re"][0].transpose(0, 2, 1).reshape(NP, P, CH).transpose(1, 0, 2),
        "ssm_c_im": i["ssm_c_im"][0].transpose(0, 2, 1).reshape(NP, P, CH).transpose(1, 0, 2),
        "g_b": np.broadcast_to(g_mix, (NP, 2, 64, CH)).reshape(NP, P, CH).transpose(1, 0, 2),
        "d_two": np.concatenate([i["ssm_d"][0].reshape(NG, CH).T] * 2, 0),
        "g_two": np.concatenate([i["norm_mix_g"][0].reshape(NG, CH).T] * 2, 0),
        "glu_a": cols(i["ssm_w_glu"][0][:, :D]), "glu_b": cols(i["ssm_w_glu"][0][:, D:]),
        "w_kvq": cols(np.concatenate([i["w_kv"], i["attn_w_q"][0]], 1)),
        "w_o": cols(i["attn_w_o"][0]),
    }
    for n in range(2):
        data[f"w1_{n}"] = cols(i["ffn_w1"][n])
        data[f"w3_{n}"] = cols(i["ffn_w3"][n])
        data[f"w2_{n}"] = i["ffn_w2"][n].reshape(FP, 2, P, D).transpose(0, 2, 1, 3).reshape(FP, P, 2 * D)

    nc = _bacc.Bacc("TRN2", target_bir_lowering=False, num_devices=1)
    arrays, aps = {}, {}
    for name, v in data.items():
        v = np.ascontiguousarray(v)
        arrays[f"in_{name}"] = v
        aps[name] = nc.dram_tensor(f"in_{name}", v.shape, mybir.dt.from_np(v.dtype), kind="ExternalInput").ap()
    out = nc.dram_tensor("out_t", (P, KT, L), F32, kind="ExternalOutput").ap()
    trunk(nc, aps, out)
    r = _run(nc, [arrays], core_ids=[0])
    return r.results[0]["out_t"].transpose(2, 1, 0).reshape(1, L, D)
```

```python
import math
from contextlib import ExitStack

import concourse.bass as bass
import numpy as np
from concourse import mybir

F32 = mybir.dt.float32
F32R = mybir.dt.float32r
ALU = mybir.AluOpType
ACT = mybir.ActivationFunctionType
AX = mybir.AxisListType

P = 128
L = 1024
D = 1024
KT = D // P
F = 2816
FP = F // 256
T = 8
NC = L // T
CH = 16
NG = D // CH
NP = NG // 2
HP = NP // 2
HG = 2 * HP
R = 8
M = NC // R
NH = 8
VD = 128
EPS = 1e-6
SCALE = 64 ** -0.5
LAM_INIT = 0.8 - 0.6 * math.exp(-0.3)
NEG = -3.0e38
TWO_PI = (6.28125, 0.0019350051879882812, 3.0199159819e-07)
MAGIC = 1.5 * 2 ** 23
PI_F = 3.1415925


def trunk(nc, a, out):
    base = (nc.sbuf_base + 31) // 32 * 32

    def sb(name, shape, kb, dt=F32):
        return nc.alloc_sbuf_tensor_at(name, shape, dt, offset=base + int(kb * 1024))

    ident = sb("ident", [P, P], 0)
    ones = sb("ones", [P, 1], 0.5)
    gains = sb("gains", [P, 5, KT], 0.53125)
    subg = sb("subg", [P, 1], 0.75)
    sgn = sb("sgn", [P, 1], 0.78125)
    lams = sb("lams", [P, 4], 207)
    ms = sb("ms", [P, 8], 3.03125)
    rt = sb("rt", [P, 8], 3.0625)
    rs = sb("rs", [P, 8], 3.09375)
    mx = sb("mx", [P, 16], 3.125)
    nb = sb("nb", [P, 16], 3.1875)
    es = sb("es", [P, 16], 3.25)
    er = sb("er", [P, 16], 3.3125)
    ec = sb("ec", [P, 8], 3.375)
    h = sb("h", [P, KT, L], 4)
    x_hi = sb("x_hi", [P, KT, L], 36, F32R)
    x_lo = sb("x_lo", [P, KT, L], 68, F32R)
    wa = [sb("wa_hi", [P, KT, 256], 100, F32R), sb("wa_lo", [P, KT, 256], 108, F32R)]
    wb = [sb("wb_hi", [P, KT, 256], 116, F32R), sb("wb_lo", [P, KT, 256], 124, F32R)]
    wc = [sb("wc_hi", [P, 2, D], 132, F32R), sb("wc_lo", [P, 2, D], 140, F32R)]
    raw_a = sb("raw_a", [P, KT, 256], 148)
    raw_b = sb("raw_b", [P, KT, 256], 156)
    raw_c = sb("raw_c", [P, 2, D], 164)
    hid = [sb("hid_hi", [P, 2, L], 172, F32R), sb("hid_lo", [P, 2, L], 180, F32R)]
    tmp = [sb("tmp0", [P, L], 188), sb("tmp1", [P, L], 192), sb("tmp2", [P, L], 196)]
    sg = [sb("sg0", [P, L], 172), sb("sg1", [P, L], 176)]
    glu_v = sb("glu_v", [P, L], 180)
    cos_t = sb("cos_t", [P, L], 132)
    sin_t = sb("sin_t", [P, L], 136)
    xk = [sb("xk0", [P, L], 140), sb("xk1", [P, L], 144)]
    stg = [sb("stg_a", [P, KT, 256], 164), sb("stg_b", [P, KT, 256], 196)]
    rk_hi = [sb("rk_hi0", [P, L], 172, F32R), sb("rk_hi1", [P, L], 176, F32R)]
    rk_lo = [sb("rk_lo0", [P, L], 180, F32R), sb("rk_lo1", [P, L], 184, F32R)]
    rk = [sb("rk0", [P, L], 188), sb("rk1", [P, L], 192)]
    kst = [sb(f"kst{n}", [P, 2, L], kb, F32R) for n, kb in enumerate((148, 100))]
    q_hi = [sb(f"q_hi{n}", [P, 2, L], kb, F32R) for n, kb in enumerate((156, 108))]
    q_lo = [sb(f"q_lo{n}", [P, 2, L], kb, F32R) for n, kb in enumerate((164, 116))]
    v_hi = sb("v_hi", [P, KT, VD], 124, F32R)
    v_lo = sb("v_lo", [P, KT, VD], 128, F32R)
    e1 = [sb("e1_q0", [P, P], 1), sb("e1_q1", [P, 2 * P], 1.5)] \
        + [sb(f"e1_{n}", [P, L], kb) for n, kb in enumerate((132, 136, 140))] * 2
    e2 = [sb(f"e2_{n}", [P, L], kb) for n, kb in enumerate((144, 196))]
    dg = [sb(f"dg{n}", [P, P], 204 + 0.5 * n) for n in range(4)]
    pt_hi = sb("pt_hi", [P, KT, 256], 172, F32R)
    pt_lo = sb("pt_lo", [P, KT, 256], 180, F32R)
    otf = sb("otf", [P, L], 188)
    osq = sb("osq", [P, L], 192)
    onf = osq
    vraw = sb("vraw", [P, KT, VD], 200)
    u = sb("u", [P, NG, NC], 172)
    tw = sb("tw", [P, HG, T, CH], 36)
    tc = sb("tc", [P, HG, T + 1, CH], 52)
    wt = sb("wt", [P, HG, P], 70)
    st_s = sb("st_s", [P, HG, NC], 70)
    gt = sb("gt", [P, 2 * HP, P], 86)
    st = sb("st", [P, HP, 2, NC + 1], 102)
    z = sb("z", [P, 2, T, D // 2], 119)
    w4 = sb("w4", [P, HG, 4, 2 * CH], 135)
    lamv = sb("lamv", [P, 4, 64], 135)
    lamp = sb("lamp", [P, 2, 64], 136)
    ta = sb("ta", [P, HP, 2, M], 151)
    tb = sb("tb", [P, HP, 2, M], 153)
    b_st, b_sw = sb("b_st", [P, NG, CH], 155), sb("b_sw", [P, NG, CH], 159)
    c_st, c_sw = sb("c_st", [P, NG, CH], 163), sb("c_sw", [P, NG, CH], 167)
    ident4 = sb("ident4", [32, P], 206.5)
    pw = [sb("pw_re", [P, T + 1, NG], 1), sb("pw_im", [P, T + 1, NG], 33.5)]
    pw_8 = sb("pw_8", [P, 2, R, NP], 204)
    pw_x = sb("pw_x", [P, 2, 3, NP], 171)
    d_two = sb("d_two", [32, NG], 206)
    g_two = sb("g_two", [32, NG], 206.25)
    dd = sb("dd", [32, HG, 32], 4)
    p1 = sb("p1", [P, HP, T, CH], 8)
    p2 = sb("p2", [P, HP, T, CH], 16)
    bz4 = sb("bz4", [P, HG, 4, 2, CH], 8)
    m1 = sb("m1", [P, HP // 2, T, CH], 24)
    m2 = sb("m2", [P, HP // 2, T, CH], 28)
    pt_x = [sb(f"pt_x{n}", [P, 1, NP], 24 + 0.25 * n) for n in range(4)]
    ssq = sb("ssq", [P, NC], 32)
    rfull = sb("rfull", [P, NC], 32.5)
    same_j = sb("same_j", [P, P], 33)
    perm = sb("perm", [P, P], 3.5)
    sq = [sb("sq0", [P, 16, NC], 119), sb("sq1", [P, 16, NC], 127)]
    prm = sb("prm", [P, 24, NG], 86)
    g_b = sb("g_b", [P, NG, CH], 92)
    bt = [sb(f"bt{n}", [P, NG, CH], 70 + 4 * n) for n in range(4)]
    pt4 = [sb(f"pt4_{n}", [P, 4, NG], 102 + n) for n in range(4)]

    scr_kq = [nc.dram_tensor(name, [2, 2, NH * 64, L], F32).ap() for name in ("k_scratch", "q_scratch")]
    scr_v = nc.dram_tensor("v_scratch", [L, D], F32).ap()

    with ExitStack() as ctx:
        ps = ctx.enter_context(nc.psum_tensor("ps", [P, 8, 512], F32))
        sem = lambda name: ctx.enter_context(nc.semaphore(name))
        consts_in, params_in, h_in = sem("consts_in"), sem("params_in"), sem("h_in")
        bc_in = sem("bc_in")
        u_in = [sem(f"u_in{k}") for k in range(4)]
        sq_done, part_done, rms_pe, rms_ms, rms_rt, rms_rs = map(
            sem, "sq_done part_done rms_pe rms_ms rms_rt rms_rs".split())
        u_done, u_pool = sem("u_done"), sem("u_pool")
        dve, act, pool = sem("dve_steps"), sem("act_steps"), sem("pool_steps")
        prm_exp, prm_arg, prm_sin, prm_done = map(sem, "prm_exp prm_arg prm_sin prm_done".split())
        w_hi, w_scaled = sem("w_hi_done"), sem("w_scaled")
        w_tab, c_pool, c_dve = sem("w_tab"), sem("c_pool"), sem("c_dve")
        dd_done, bz_done, sts_act = map(sem, "dd_done bz_done sts_act".split())
        sts_in = [sem("sts_in0"), sem("sts_in1")]
        s5_full, s5_act, s5_dve = sem("s5_full"), sem("s5_act"), sem("s5_dve")
        scan_done, z_hi = sem("scan_done"), sem("z_hi_done")
        a_in, b_in, c_in = sem("a_loaded"), sem("b_loaded"), sem("c_loaded")
        a_rdy, b_rdy, c_rdy = sem("a_split"), sem("b_split"), sem("c_split")
        tile, act_ev, dve_ev = sem("tile_done"), sem("act_evacuated"), sem("dve_evacuated")
        sig_done, h_add = sem("sig_done"), sem("h_added")
        hid_h, hid_l = sem("hid_hi_done"), sem("hid_lo_done")
        nsq, nacc, ncol, nms, nrt, nrs, nbc, nf, nhi, nlo = map(
            sem, "n_sq n_acc n_col n_ms n_rt n_rs n_bcast n_full n_hi n_lo".split())
        rot_in, rotp, rsum, rhi, rlo = map(sem, "rot_in rot_permuted rot_sum rot_hi rot_lo".split())
        stored, v_stored = [sem("stored_0"), sem("stored_1")], [sem("v_stored_a"), sem("v_stored_b")]
        lam_d, lam_e, lam_done = sem("lam_d"), sem("lam_e"), sem("lam_done")
        kq_in, v_in = [sem("kq_loaded_0"), sem("kq_loaded_1")], sem("v_loaded")
        vh_done, vl_done = sem("v_hi_done"), sem("v_lo_done")
        sc, masked, mxd, nbd, exd = map(sem, "scores masked max_done negmax exp_done".split())
        er_done, ec_done, p_done = map(sem, "er_done ec_done p_done".split())
        pt_tr, pth, ptl = map(sem, "pt_transposed pt_hi_done pt_lo_done".split())
        pv, oc, oq = sem("pv_done"), sem("o_copied"), sem("o_squared")
        ocol, oms, ort, ors, obc, onfd, onh, onl = map(
            sem, "o_col o_ms o_rt o_rs o_bcast o_full o_hi o_lo".split())
        out_done = [sem("out_done0"), sem("out_done1")]

        kinds = []
        for hf in range(2):
            kinds += [(kind, hf, k) for kind in ("wt", "v", "g", "y") for k in range(8)]
        kinds += [("z", 0, k) for k in range(16)]
        by_act = {"wt": True, "g": True, "v": True, "y": True, "z": False}
        number = {key: n for n, key in enumerate(kinds)}

        def evacuated(n):
            mine = by_act[kinds[n][0]]
            return (s5_act if mine else s5_dve), sum(by_act[k[0]] == mine for k in kinds[:n + 1])

        def s5_batches(eng, want, body):
            for n, (kind, hf, k) in enumerate(kinds):
                if (kind, hf) in want:
                    body(n, kind, hf, k)


        N_GLU, N_F0, N_KVQ, N_WO, N_F1 = 0, 4, 4 + FP, 10 + FP, 12 + FP
        FT = 12 * FP
        T_GLU, T_F0, T_KVQ, T_WO, T_F1 = 0, 16, 16 + FT, 40 + FT, 48 + FT
        FA, FD = 2 * FP, 10 * FP
        A_GLU, A_F0, A_KVQ, A_WO, A_F1 = 4, 12, 12 + FA, 32 + FA, 32 + FA
        D_GLU, D_F0, D_KVQ, D_WO, D_F1 = 4, 12, 12 + FD, 28 + FD, 36 + FD

        block = ctx.enter_context(nc.Block())

        @block.sync
        def _(sp):
            for t, name in ((ident, "ident"), (same_j, "same_j"), (ones, "ones"), (gains, "gains"),
                            (ident4, "ident4"), (subg, "subg"), (perm, "perm"), (lamv, "lamv"),
                            (sgn, "sgn")):
                sp.dma_start(t[:], a[name]).then_inc(consts_in, 16)
            sp.dma_start(prm[:, 0:3, :], a["ssm_prm"]).then_inc(params_in, 16)
            for t, name in ((b_st, "ssm_b_st"), (b_sw, "ssm_b_sw"), (c_st, "ssm_c_st"),
                            (c_sw, "ssm_c_sw"), (g_b, "g_b"), (d_two, "d_two"),
                            (g_two, "g_two")):
                sp.dma_start(t[:], a[name]).then_inc(bc_in, 16)
            for k in range(4):
                sp.dma_start(u[:, 16 * k:16 * k + 16, :], a["x_u"][:, 16 * k:16 * k + 16, :])\
                    .then_inc(u_in[k], 16)

            def load(t, src, loaded, split, n, first=False):
                if not first:
                    sp.wait_ge(split, 2 * n)
                sp.dma_start(t[:, :, :], src).then_inc(loaded, 16)

            def chunk(name, i):
                return a[name][bass.ds(i, 1), :, :].rearrange("o p c -> p (o c)")\
                    .rearrange("p (k c) -> p k c", c=D if name[:2] == "w2" else 256)

            for hf in range(2):
                sp.wait_ge(scan_done, hf + 1)
                for x in range(2):
                    g, q = HP * x, HP // 2 * x
                    sp.dma_start(st_s[64:P, g:g + HP:2, :], st[0:64, q:q + HP // 2, 1, 0:NC])\
                        .then_inc(sts_in[x], 16)
                    sp.dma_start(st_s[0:64, g + 1:g + HP:2, :], st[64:P, q:q + HP // 2, 0, 0:NC])\
                        .then_inc(sts_in[x], 16)
            sp.wait_ge(w_tab, 2)
            sp.wait_ge(bz_done, 2)
            sp.wait_ge(c_pool, 2)
            sp.wait_ge(c_dve, 2)
            load(raw_b, chunk("glu_b", 0), b_in, b_rdy, 0, True)
            sp.wait_ge(s5_full, len(kinds))
            load(raw_a, chunk("glu_a", 0), a_in, a_rdy, 0, True)
            sp.dma_start(h[:, :, :], a["x_t"]).then_inc(h_in, 16)
            with sp.Fori(1, 4) as i:
                load(raw_b, chunk("glu_b", i), b_in, b_rdy, i)
                load(raw_a, chunk("glu_a", i), a_in, a_rdy, i)

            def ffn(layer, n0):
                load(raw_a, chunk(f"w1_{layer}", 0), a_in, a_rdy, n0)
                load(raw_b, chunk(f"w3_{layer}", 0), b_in, b_rdy, n0)
                load(raw_c, chunk(f"w2_{layer}", 0), c_in, c_rdy, layer * FP, layer == 0)
                with sp.Fori(1, FP) as i:
                    load(raw_a, chunk(f"w1_{layer}", i), a_in, a_rdy, i + n0)
                    load(raw_b, chunk(f"w3_{layer}", i), b_in, b_rdy, i + n0)
                    load(raw_c, chunk(f"w2_{layer}", i), c_in, c_rdy, i + layer * FP)

            ffn(0, N_F0)
            load(raw_a, chunk("w_kvq", 0), a_in, a_rdy, N_KVQ)
            load(raw_b, chunk("w_kvq", 1), b_in, b_rdy, N_KVQ)

            sp.wait_ge(tile, T_KVQ)
            sp.dma_start(cos_t[:, :], a["cos_t"]).then_inc(rot_in, 16)
            sp.dma_start(sin_t[:, :], a["sin_t"]).then_inc(rot_in, 16)

            def store_kq(g, n):
                sp.wait_ge(rlo, 8 * g + n + 1)
                for part_, t in enumerate((rk_hi, rk_lo)):
                    sp.dma_start(scr_kq[g][part_, n // 4, P * (n % 4):P * (n % 4) + P, :],
                                 t[n % 2][:, :].bitcast(F32)).then_inc(stored[n % 2], 16)

            def store_v(c):
                sp.wait_ge(act_ev, A_KVQ + 8 + c + 1)
                sp.dma_start(scr_v[:, 256 * c:256 * c + 256].rearrange("(k p) c -> p k c", p=P),
                             stg[c % 2][:, :, :]).then_inc(v_stored[c % 2], 16)

            for i in range(6):
                if i < 5:
                    load(raw_a, chunk("w_kvq", 2 * i + 2), a_in, a_rdy, N_KVQ + i + 1)
                    load(raw_b, chunk("w_kvq", 2 * i + 3), b_in, b_rdy, N_KVQ + i + 1)
                if i // 2 == 1:
                    store_v(2 * (i - 2))
                    store_v(2 * (i - 2) + 1)
                else:
                    for n in range(4 if i < 5 else 1):
                        store_kq(i // 4, 4 * (i % 2) + n)

            def load_kq(i, n):
                for g, part_, r0, t in ((0, 0, 0, kst), (0, 1, 64, kst), (1, 0, 0, q_hi), (1, 0, 64, q_hi),
                                        (1, 1, 0, q_lo), (1, 1, 64, q_lo)):
                    sp.dma_start(t[n][r0:r0 + 64, :, :].bitcast(F32),
                                 scr_kq[g][part_, :, bass.ds(i * 64, 64), :].rearrange("s d t -> d s t"))\
                        .then_inc(kq_in[n], 16)

            def load_v(i):
                sp.dma_start(vraw[:, :, :], scr_v[:, bass.ds(i * 128, 128)]
                             .rearrange("(k p) c -> p k c", p=P)).then_inc(v_in, 16)

            sp.wait_ge(stored[0], 32 * 7)
            sp.wait_ge(v_stored[0], 32)
            sp.wait_ge(v_stored[1], 32)
            sp.wait_ge(a_rdy, 2 * N_KVQ + 12)
            sp.wait_ge(b_rdy, 2 * N_KVQ + 12)
            load_kq(0, 0)
            load_v(0)
            for n in range(5, 8):
                store_kq(1, n)
            sp.wait_ge(stored[0], 256)
            sp.wait_ge(stored[1], 256)
            sp.wait_ge(tile, T_WO)
            load_kq(1, 1)
            with sp.Fori(0, 3) as j:
                for n in range(2):
                    sp.wait_ge(vl_done, j * 2 + (n + 1))
                    load_v(j * 2 + (n + 1))
                    sp.wait_ge(sc, j * 32 + (16 * n + 16))
                    load_kq(j * 2 + (n + 2), n)
            sp.wait_ge(vl_done, NH - 1)
            load_v(NH - 1)
            sp.wait_ge(sc, 16 * (NH - 1))
            for i in range(2):
                load(raw_a, chunk("w_o", 2 * i), a_in, a_rdy, N_WO + i)
                load(raw_b, chunk("w_o", 2 * i + 1), b_in, b_rdy, N_WO + i)
            ffn(1, N_F1)
            for k in range(KT):
                sp.wait_ge(nf, 24 + k + 1)
                sp.dma_start(out[:, k, :], tmp[k % 2][:, :]).then_inc(out_done[k % 2], 16)
            sp.wait_ge(out_done[0], 16 * KT // 2)
            sp.wait_ge(out_done[1], 16 * KT // 2)

        @block.gpsimd
        def _(pl):
            steps = [0]

            def step(ins):
                steps[0] += 1
                ins.then_inc(pool, 1)
                pl.wait_ge(pool, steps[0])

            pl.wait_ge(bc_in, 112)
            pl.wait_ge(prm_done, 1)
            for hf in range(2):
                g = slice(HG * hf, HG * hf + HP)
                shape = [P, HP, T, CH]
                pr, pi = (x[:, T - 1::-1, g].rearrange("p k q -> p q k").unsqueeze(3)
                          .to_broadcast(shape) for x in pw)
                c_1, c_2 = (x[:, g, :].unsqueeze(2).to_broadcast(shape) for x in (c_st, c_sw))
                if hf:
                    pl.wait_ge(s5_full, number["y", 0, 7] + 1)
                step(pl.tensor_tensor(p1[:, :, :, :], pr, c_1, ALU.mult))
                step(pl.tensor_tensor(p2[:, :, :, :], pi, c_2, ALU.mult))
                step(pl.tensor_tensor(tc[:, 0:HP, 1:T + 1, :], p1[:, :, :, :], p2[:, :, :, :], ALU.subtract))
                pl.tensor_scalar(tc[:, :, 0, :], c_st[:, HG * hf:HG * hf + HG, :], 1.0, None, ALU.mult)\
                    .then_inc(c_pool, 1)
                if hf == 0:
                    pl.wait_ge(rms_rs, 1)
                    pl.tensor_tensor(u[:, 44:NG, :], u[:, 44:NG, :],
                                     rfull[:, :].unsqueeze(1).to_broadcast([P, NG - 44, NC]), ALU.mult)\
                        .then_inc(u_pool, 1)

            def split(raw, w, x, loaded, n, ready, used, hi, rows=False):
                pl.wait_ge(loaded, n * 16 + 16)
                if used is not None:
                    pl.wait_ge(tile, used)
                view = (lambda t: t[:, x:x + 1, :]) if rows else (lambda t: t[:, :, 128 * x:128 * x + 128])
                one = ones[:, 0:1].unsqueeze(2).to_broadcast(view(raw).shape)
                pl.tensor_tensor(view(w[0]), view(raw), one, ALU.mult).then_inc(w_hi, 1)
                pl.wait_ge(w_hi, hi)
                pl.tensor_tensor(view(w[1]), view(raw), view(w[0]), ALU.subtract).then_inc(ready, 1)

            def ab(n, free, hi, order=(0, 1)):
                streams = (raw_a, wa, a_in, a_rdy), (raw_b, wb, b_in, b_rdy)
                for k, (raw, w, loaded, ready) in enumerate([streams[o] for o in order] * 2):
                    split(raw, w, k // 2, loaded, n, ready, free[k] if free else None, hi + k)

            pl.wait_ge(s5_full, len(kinds))
            ab(N_GLU, None, 1, (1, 0))
            with pl.Fori(1, 4) as i:
                ab(i + N_GLU, [i * 4 + (T_GLU - 3 + k) for k in range(4)], i * 4 + 1, (1, 0))

            def ffn(layer, n0, t0, free, hi0):
                ab(n0, free, hi0)

                def c_chunk(i, hi):
                    for x in range(2):
                        split(raw_c, wc, x, c_in, i + layer * FP, c_rdy, i * 12 + (t0 + 1), hi + x,
                              rows=True)

                with pl.Fori(0, FP - 1) as i:
                    c_chunk(i, i * 6 + (hi0 + 4))
                    ab(i + (n0 + 1), [i * 12 + (t0 + 1 + k) for k in range(4)], i * 6 + (hi0 + 6))
                c_chunk(FP - 1, (FP - 1) * 6 + hi0 + 4)

            ffn(0, N_F0, T_F0, [T_GLU + 13 + k for k in (1, 0, 3, 2)], 17)
            hi1 = 17 + 6 * FP

            def kvq_split(n, free, hi, gain, sc):
                for k, (raw, w, loaded, ready) in enumerate(((raw_a, wa, a_in, a_rdy),
                                                             (raw_b, wb, b_in, b_rdy))):
                    pl.wait_ge(loaded, n * 16 + 16)
                    for x in range(2):
                        v = raw[:, :, 128 * x:128 * x + 128]
                        pl.tensor_tensor(v, v, gains[:, gain, :].unsqueeze(2).to_broadcast([P, KT, 128]),
                                         ALU.mult).then_inc(w_scaled, 1)
                    pl.wait_ge(w_scaled, sc + 2 * k + 1)
                    pl.wait_ge(tile, free[k])
                    for x in range(2):
                        v, w_h, w_l = (t[:, :, 128 * x:128 * x + 128] for t in (raw, *w))
                        pl.tensor_tensor(w_h, v, ones[:, 0:1].unsqueeze(2).to_broadcast([P, KT, 128]),
                                         ALU.mult).then_inc(w_hi, 1)
                        pl.wait_ge(w_hi, hi + 2 * k + x)
                        pl.tensor_tensor(w_l, v, w_h, ALU.subtract).then_inc(ready, 1)

            kvq_split(N_KVQ, [T_KVQ - 9, T_KVQ - 8], hi1, 1, 1)
            for i0, i1, gain in ((1, 4, 1), (4, 6, 2)):
                with pl.Fori(i0, i1) as i:
                    kvq_split(i + N_KVQ, [i * 4 + (T_KVQ - 2), i * 4 + T_KVQ], i * 4 + hi1,
                              gain, i * 4 + 1)

            def split_v(i):
                pl.wait_ge(v_in, i * 16 + 16)
                pl.tensor_tensor(v_hi[:, :, :], vraw[:, :, :],
                                 ones[:, 0:1].unsqueeze(2).to_broadcast([P, KT, VD]), ALU.mult)\
                    .then_inc(vh_done, 1)
                pl.wait_ge(vh_done, i + 1)
                pl.tensor_tensor(v_lo[:, :, :], vraw[:, :, :], v_hi[:, :, :], ALU.subtract)\
                    .then_inc(vl_done, 1)

            def low_x(i):
                pl.wait_ge(onh, i + 1)
                x1, x2 = (x[:, bass.ds(i, 1), :].rearrange("p o c -> p (o c)") for x in (x_lo, x_hi))
                pl.tensor_tensor(x1, onf[:, :], x2, ALU.subtract).then_inc(onl, 1)

            pl.wait_ge(tile, T_WO)
            split_v(0)
            with pl.Fori(1, NH) as i:
                pl.wait_ge(pv, i * 4)
                split_v(i)
                low_x(i - 1)
            hi2 = hi1 + 24
            pl.wait_ge(sc, 16 * NH)
            for x in range(2):
                split(raw_a, wa, x, a_in, N_WO, a_rdy, None, hi2 + x)
            low_x(NH - 1)
            pl.wait_ge(pv, 4 * NH)
            for x in range(2):
                split(raw_b, wb, x, b_in, N_WO, b_rdy, None, hi2 + 2 + x)
            ab(N_WO + 1, [T_WO + 1, T_WO + 3, T_WO + 2, T_WO + 4], hi2 + 4)
            ffn(1, N_F1, T_F1, [T_WO + 5, T_WO + 7, T_WO + 6, T_WO + 8], hi2 + 8)

        def two(n):
            return ps[:, 2 * n:2 * n + 2, :]

        def wide(t):
            return t.rearrange("p (b c) -> p b c", b=2)

        def bank(q, s):
            return 2 * s + (q % 2 if q < 4 else 0)

        PT_USES = [(q, k0, min(4, q + 1 - k0)) for q in range(8) for k0 in range(0, q + 1, 4)]

        def pt_of(q):
            return [n for n, use in enumerate(PT_USES) if use[0] == q]

        def h_ready(m, k):
            return ((h_add, k + 1), (dve_ev, D_KVQ - 8 + k + 1), (dve_ev, D_WO + k + 1),
                    (dve_ev, D_F1 + FD - 8 + k + 1))[m]

        @block.tensor
        def _(pe):
            pe.wait_ge(consts_in, 16 * 9)
            for k in range(4):
                pe.wait_ge(sq_done, k + 1)
                for n in range(4):
                    pe.matmul(ps[:, 7, :], same_j[:, :], sq[k % 2][:, 4 * n:4 * n + 4, :],
                              start=(k == 0 and n == 0), stop=(k == 3 and n == 3))\
                        .then_inc(rms_pe if k == 3 and n == 3 else part_done, 1)

            def batch(n, kind, hf, k):
                b = n % 8
                if n == 7:
                    pe.wait_ge(rms_ms, 1)
                if n >= 8:
                    pe.wait_ge(*evacuated(n - 8))
                if kind == "wt":
                    if k == 0:
                        pe.wait_ge(w_tab, hf + 1)
                    for n4 in range(4):
                        src = tw[:, 4 * k + n4, :, :].rearrange("p a b -> p (a b)")
                        ins = pe.transpose(ps[:, b, P * n4:P * n4 + P], src, ident[:, :])
                elif kind == "v":
                    if k == 0 and hf == 0:
                        pe.wait_ge(u_done, 1)
                        pe.wait_ge(u_pool, 1)
                    pe.wait_ge(*evacuated(number["wt", hf, k]))
                    for n8 in range(8):
                        q, ri, gp = 2 * k + n8 // 4, n8 // 2 % 2, n8 % 2
                        c0 = 2 * P * (n8 // 4) + P * ri
                        ins = pe.matmul(ps[64 * gp:64 * gp + 64, b, c0:c0 + P],
                                        wt[:, 2 * q + gp, 64 * ri:64 * ri + 64],
                                        u[:, 2 * (HP * hf + q) + gp, :], start=True, stop=True)
                elif kind == "g":
                    if k == 0:
                        pe.wait_ge(c_pool, hf + 1)
                        pe.wait_ge(c_dve, hf + 1)
                        pe.wait_ge(bz_done, hf + 1)
                        pe.wait_ge(dd_done, hf + 1)
                    pe.matmul(ps[:, b, :].rearrange("p (g c) -> p g c", c=P)[:, :, 0:32], ident4[:, :],
                              dd[:, 4 * k:4 * k + 4, :], start=True, stop=False, skip_group_check=True)
                    for n4 in range(4):
                        g, c0 = 4 * k + n4, P * n4
                        pe.matmul(ps[:, b, c0 + CH:c0 + P], w4[:, g, :, :].rearrange("p a b -> p (a b)"),
                                  tc[:, g, 0:T - 1, :].rearrange("p a b -> p (a b)"),
                                  start=False, stop=False, skip_group_check=True)
                        ins = pe.matmul(ps[:, b, c0:c0 + CH], bz4[:, g, :, :, :].rearrange("p s a b -> p (s a b)"),
                                        tc[:, g, 0, :], start=False, stop=True, skip_group_check=True)
                elif kind == "y":
                    if k == 0:
                        pe.wait_ge(sts_act, hf + 1)
                    if k % 4 == 0:
                        pe.wait_ge(sts_in[k // 4], 32 * hf + 32)
                    pe.wait_ge(*evacuated(number["g", hf, k]))
                    for n4 in range(4):
                        g, o = 4 * k + n4, ps[:, b, P * n4:P * n4 + P]
                        pe.matmul(o, u[:, HG * hf + g, :], gt[:, g, :], start=True, stop=False)
                        ins = pe.matmul(o, st_s[:, g, :], tc[:, g, 1:T + 1, :].rearrange("p a b -> p (a b)"),
                                        start=False, stop=True)
                else:
                    if k == 0:
                        pe.wait_ge(*evacuated(number["y", 1, 7]))
                    for n4 in range(4):
                        j = 4 * (k % 2) + n4
                        ins = pe.transpose(ps[:, b, P * n4:P * n4 + P], z[:, k // 8, j, P * (k // 2 % 4):P * (k // 2 % 4) + P],
                                           ident[:, :])
                ins.then_inc(s5_full, 1)

            s5_batches(pe, [(kind, hf) for kind in ("wt", "v", "g", "y", "z") for hf in range(2)], batch)

            def product(slot, w, wcols, x, ks=range(KT)):
                for k in ks:
                    for n, (wn, xn) in enumerate(((0, 0), (0, 1), (1, 0))):
                        for c in range(2):
                            ins = pe.matmul(ps[:, 2 * slot + c, :], w[wn][:, k, wcols],
                                            x[xn][:, k, 512 * c:512 * c + 512],
                                            start=(k == ks[0] and n == 0), stop=(k == ks[-1] and n == 2))
                ins.then_inc(tile, 1)

            def part_product(slot, w, wcols, x, k):
                for n, (wn, xn) in enumerate(((0, 0), (0, 1), (1, 0))):
                    for c in range(2):
                        ins = pe.matmul(ps[:, 2 * slot + c, :], w[wn][:, k, wcols],
                                        x[xn][:, k, 512 * c:512 * c + 512],
                                        start=(k == 0 and n == 0), stop=(k == 1 and n == 2))
                return ins

            def two_products(ws, wcols, rows):
                for k in range(KT):
                    pe.wait_ge(nlo, rows + k + 1)
                    for slot, (w, cols_) in enumerate(zip(ws, wcols)):
                        for n, (wn, xn) in enumerate(((0, 0), (0, 1), (1, 0))):
                            for c in range(2):
                                ins = pe.matmul(ps[:, 2 * slot + c, :], w[wn][:, k, cols_],
                                                xs[xn][:, k, 512 * c:512 * c + 512],
                                                start=(k == 0 and n == 0), stop=(k == KT - 1 and n == 2))
                        if k == KT - 1:
                            ins.then_inc(tile, 1)

            xs = (x_hi, x_lo)
            halves = (slice(0, P), slice(P, 2 * P))

            pe.wait_ge(dve_ev, D_GLU)
            pe.wait_ge(act_ev, A_GLU)
            with pe.Fori(0, 4) as i:
                for x in range(2):
                    pe.wait_ge(b_rdy, i * 2 + (2 * N_GLU + x + 1))
                    pe.wait_ge(act_ev, i * 2 + (A_GLU - 1 + x))
                    product(2 * x + 1, wb, halves[x], xs)
                    pe.wait_ge(a_rdy, i * 2 + (2 * N_GLU + x + 1))
                    pe.wait_ge(dve_ev, i * 2 + (D_GLU - 1 + x))
                    product(2 * x, wa, halves[x], xs)

            def columns(m):
                pe.wait_ge(nacc, 7 * m + 7)
                for t in range(KT):
                    ins = pe.matmul(ps[:, 7, t:t + 1], tmp[2][:, P * t:P * t + P], ones[:, :],
                                    start=True, stop=True)
                ins.then_inc(ncol, 1)
                pe.wait_ge(nrs, m + 1)
                spread(ps, 6, rs, nbc)

            def spread(o, b, col, done):
                for t in range(KT):
                    ins = pe.matmul(o[:, b + t // 4, P * (t % 4):P * (t % 4) + P],
                                    col[:, t:t + 1].to_broadcast([P, P]), ident[:, :],
                                    start=True, stop=True)
                ins.then_inc(done, 1)

            def ffn(layer, n0, d0, a0, rows):
                def w1(x, n):
                    pe.wait_ge(a_rdy, n)
                    product((0, 2)[x], wa, halves[x], xs)

                def w3(x, n):
                    pe.wait_ge(b_rdy, n)
                    product((1, 3)[x], wb, halves[x], xs)

                def body(i, last):
                    pe.wait_ge(dve_ev, i * 10 + (d0 - 2))
                    w1(1, i * 2 + (2 * n0 + 2))
                    pe.wait_ge(dve_ev, i * 10 + (d0 - 1))
                    w3(1, i * 2 + (2 * n0 + 2))
                    if not last:
                        pe.wait_ge(act_ev, i * 2 + (a0 + 1))
                        pe.wait_ge(dve_ev, i * 10 + d0)
                        w1(0, i * 2 + (2 * n0 + 3))
                    pe.wait_ge(c_rdy, i * 2 + (2 * FP * layer + 2))
                    if last:
                        pe.wait_ge(hid_l, 2 * FP * (layer + 1) - 1)
                        pe.wait_ge(dve_ev, 10 * FP - 10 + d0 + 1)
                        part_product(1, wc, slice(0, P), hid, 0)
                        pe.wait_ge(act_ev, 2 * FP - 2 + a0 + 2)
                        part_product(2, wc, slice(P, 2 * P), hid, 0)
                        pe.wait_ge(hid_l, 2 * FP * (layer + 1))
                        part_product(1, wc, slice(0, P), hid, 1).then_inc(tile, 1)
                        part_product(2, wc, slice(P, 2 * P), hid, 1).then_inc(tile, 1)
                    else:
                        pe.wait_ge(hid_l, i * 2 + (2 * FP * layer + 2))
                    for n in range(2 if last else 0, 8):
                        if n % 4 == 1 and n < 4:
                            pe.wait_ge(act_ev, i * 2 + (a0 + 2))
                        elif n == 3:
                            if not last:
                                pe.wait_ge(act_ev, i * 2 + (a0 + 3))
                        else:
                            pe.wait_ge(dve_ev, i * 10 + (d0 + (1, 0, 2, 0, 3, 4, 5, 6)[n]))
                        product((1, 2, 3, 0)[n % 4], wc, slice(P * n, P * n + P), hid, range(2))
                    if not last:
                        pe.wait_ge(dve_ev, i * 10 + (d0 + 7))
                        w3(0, i * 2 + (2 * n0 + 3))

                pe.wait_ge(a_rdy, 2 * n0 + 1)
                pe.wait_ge(b_rdy, 2 * n0 + 1)
                two_products((wa, wb), (halves[0], halves[0]), rows)
                with pe.Fori(0, FP - 1) as i:
                    body(i, False)
                body(FP - 1, True)

            columns(0)
            ffn(0, N_F0, D_F0, A_F0, 0)
            columns(1)

            def rotated(g, a0):
                def permuted(i, y):
                    pe.wait_ge(act_ev, i * 4 + (a0 + y + 1))
                    pe.wait_ge(dve_ev, i * 4 + (D_KVQ + 8 * g + y - 1))
                    for c in range(2):
                        ins = pe.matmul(ps[:, 4 + 2 * (y % 2) + c, :], perm[:, :],
                                        xk[y % 2][:, 512 * c:512 * c + 512], start=True, stop=True)
                    ins.then_inc(rotp, 1)

                def tiles(i, y0):
                    for y in range(y0, 4):
                        w, ready = ((wa, a_rdy), (wb, b_rdy))[y // 2]
                        pe.wait_ge(ready, i * 2 + (2 * N_KVQ + 8 * g + y % 2 + 1))
                        pe.wait_ge(act_ev, i * 4 + (a0 + y - 1))
                        product(y % 2, w, halves[y % 2], xs)
                        permuted(i, y - 1) if y else None
                    permuted(i, 3)

                if g == 0:
                    pe.wait_ge(a_rdy, 2 * N_KVQ + 2)
                    two_products((wa, wa), halves, KT)
                    permuted(0, 0)
                    tiles(0, 2)
                    tiles(1, 0)
                else:
                    with pe.Fori(0, 2) as i:
                        tiles(i, 0)

            rotated(0, A_KVQ)
            for c in range(4):
                s, (w, ready) = c % 2, ((wa, a_rdy), (wb, b_rdy))[c % 2]
                pe.wait_ge(ready, 2 * N_KVQ + 4 + 2 * (c // 2) + 2)
                pe.wait_ge(dve_ev, D_KVQ + 8)
                pe.wait_ge(act_ev, A_KVQ + 8 + max(0, c - 1))
                for t in range(KT):
                    for k in range(KT):
                        for n, (wn, xn) in enumerate(((0, 0), (0, 1), (1, 0))):
                            ins = pe.matmul(ps[:, 4 * s + t // 2, 256 * (t % 2):256 * (t % 2) + 256],
                                            xs[xn][:, k, P * t:P * t + P], w[wn][:, k, :],
                                            start=(k == 0 and n == 0), stop=(k == 7 and n == 2))
                ins.then_inc(tile, 2)
            rotated(1, A_KVQ + 12)

            def scores(i, q, n):
                for s in range(2):
                    if q in (2, 3):
                        pe.wait_ge(exd, i * 16 + (2 * q - 3 + s))
                    elif q >= 4:
                        pe.wait_ge(exd, i * 16 + (2 * q - 1 + s))
                    elif q == 0 and isinstance(i, int) and i == 0:
                        pe.wait_ge(dve_ev, D_WO)
                    elif q == 0:
                        pe.wait_ge(exd, i * 16 + (s - 1))
                    ext = (q + 1) * P
                    for c in range(0, ext, 512):
                        w = max(256, min(512, ext - c))
                        for part_, qq in enumerate((q_hi, q_lo)):
                            ins = pe.matmul(ps[:, bank(q, s) + c // 512, 0:w], qq[n][:, s, P * q:P * q + P],
                                            kst[n][:, s, c:c + w], start=(part_ == 0), stop=(part_ == 1))
                    ins.then_inc(sc, 1)

            def turn_p(i, q):
                pe.wait_ge(p_done, i * 8 + (q + 1))
                for n in pt_of(q):
                    _, k0, cnt = PT_USES[n]
                    if n >= 2:
                        pe.wait_ge(ptl, i * 12 + (n - 1))
                    elif not (isinstance(i, int) and i == 0):
                        pe.wait_ge(ptl, i * 12 + (n - 1))
                    for k in range(cnt):
                        ins = pe.matmul(ps[:, 4 + n % 2, P * k:P * k + P],
                                        e1[q][:, P * (k0 + k):P * (k0 + k) + P], dg[q % 4][:, :],
                                        start=True, stop=True)
                    ins.then_inc(pt_tr, 1)

            def values(i, b):
                if b == 0:
                    pe.wait_ge(vl_done, i + 1)
                if b >= 2:
                    pe.wait_ge(oq, i * 4 + (b - 1))
                elif not (isinstance(i, int) and i == 0):
                    pe.wait_ge(onfd, i)
                pe.wait_ge(ptl, i * 12 + (pt_of(2 * b + 1)[-1] + 1))
                for k in range(2 * b + 2):
                    for n, (vv, pp) in enumerate(((v_hi, pt_hi), (v_hi, pt_lo), (v_lo, pt_hi))):
                        ins = pe.matmul(ps[:, 6 + b % 2, 0:256], vv[:, k, :], pp[:, k, :],
                                        start=(k == 0 and n == 0), stop=(k == 2 * b + 1 and n == 2))
                ins.then_inc(pv, 1)

            def step(i, q, n, cur, prev):
                if cur:
                    scores(i, q, n)
                if q % 2 == 0 and (cur if q >= 4 else prev):
                    values(i, q // 2 - 2) if q >= 4 else values(i - 1, q // 2 + 2)
                if cur if q >= 2 else prev:
                    turn_p(i, q - 2) if q >= 2 else turn_p(i - 1, q + 6)
                if q == 3 and prev:
                    pe.wait_ge(ors, i)
                    spread(ps, 6, rs, obc)
                if q == 2 and prev:
                    pe.wait_ge(oq, i * 4)
                    for t in range(KT):
                        ins = pe.matmul(ps[:, 7, t:t + 1], osq[:, P * t:P * t + P], ones[:, :],
                                        start=True, stop=True)
                    ins.then_inc(ocol, 1)

            def head(i, n, cur=True, prev=True, start=None):
                if cur:
                    pe.wait_ge(kq_in[n], start)
                for q in range(8 if cur else 4):
                    step(i, q, n, cur, prev)

            pe.wait_ge(act_ev, A_WO)
            head(0, 0, prev=False, start=96)
            with pe.Fori(0, 3) as j:
                head(j * 2 + 1, 1, start=j * 96 + 96)
                head(j * 2 + 2, 0, start=j * 96 + 192)
            head(NH - 1, 1, start=4 * 96)
            head(NH, 0, cur=False)

            pe.wait_ge(onl, NH)
            for i in range(2):
                for n, (w, ready) in enumerate(((wa, a_rdy), (wa, a_rdy), (wb, b_rdy), (wb, b_rdy))):
                    pe.wait_ge(ready, 2 * (N_WO + i) + n % 2 + 1)
                    if i:
                        pe.wait_ge(dve_ev, D_WO + n + 1)
                    product(n, w, halves[n % 2], xs)
            columns(2)
            ffn(1, N_F1, D_F1, A_F1, 2 * KT)
            pe.wait_ge(nacc, 28)
            for t in range(KT):
                ins = pe.matmul(ps[:, 7, t:t + 1], tmp[2][:, P * t:P * t + P], ones[:, :],
                                start=True, stop=True)
            ins.then_inc(ncol, 1)
            pe.wait_ge(nrs, 4)
            spread(ps, 6, rs, nbc)

        @block.scalar
        def _(ac):
            steps = [0]

            def step(ins):
                steps[0] += 1
                ins.then_inc(act, 1)
                ac.wait_ge(act, steps[0])

            ac.wait_ge(params_in, 16)
            ac.activation(prm[:, 3, :], prm[:, 2, :], ACT.Exp).then_inc(prm_exp, 1)
            ac.wait_ge(prm_arg, 1)
            ac.activation(prm[:, 6, :], prm[:, 4, :], ACT.Exp).then_inc(prm_exp, 1)
            ac.wait_ge(lam_d, 1)
            ac.activation(lams[:, 0:2], lams[:, 0:2], ACT.Exp).then_inc(lam_e, 1)
            ac.wait_ge(prm_arg, 2)
            ac.activation(prm[:, 9, :], prm[:, 8, :], ACT.Sin).then_inc(prm_sin, 1)
            ac.activation(prm[:, 10, :], prm[:, 8, :], ACT.Sin, scale=0.5).then_inc(prm_sin, 1)
            for k in range(4):
                ac.wait_ge(u_in[k], 16)
                if k >= 2:
                    ac.wait_ge(part_done, 4 * k - 4)
                ac.activation(sq[k % 2][:, :, :], u[:, 16 * k:16 * k + 16, :], ACT.Square)\
                    .then_inc(sq_done, 1)
            ac.wait_ge(prm_done, 2)
            ac.activation(gt[:, :, :], ones[:, 0:1].unsqueeze(2).to_broadcast([P, HG, P]), ACT.Copy,
                          scale=0.0)
            ac.wait_ge(rms_ms, 1)
            ac.activation(rfull[:, :], rfull[:, :], ACT.Sqrt).then_inc(rms_rt, 1)

            def batch(n, kind, hf, k):
                b = n % 8
                if kind == "wt" and k == 0:
                    ac.wait_ge(w_tab, hf + 1)
                    ac.activation(w4[:, :, :, :], tw[:, :, T - 2:T, :].rearrange("p q a b -> p q (a b)")
                                  .unsqueeze(2).to_broadcast([P, HG, 4, 2 * CH]), ACT.Copy)
                if kind == "g" and k == 0:
                    ac.wait_ge(c_pool, hf + 1)
                    b_ = b_st[:, HG * hf:HG * hf + HG, :].unsqueeze(2).to_broadcast([P, HG, 4, CH])
                    ac.activation(bz4[:, :, :, 0, :], b_, ACT.Copy)
                    ac.activation(bz4[:, :, :, 1, :], b_, ACT.Copy, scale=0.0).then_inc(bz_done, 1)
                if kind == "y" and k == 0:
                    ac.wait_ge(scan_done, hf + 1)
                    for r in range(2):
                        ins = ac.activation(st_s[64 * r:64 * r + 64, r:HG:2, :],
                                            st[64 * r:64 * r + 64, :, r, 0:NC], ACT.Copy)
                    ins.then_inc(sts_act, 1)
                ac.wait_ge(s5_full, n + 1)
                if kind == "wt":
                    ac.activation(wt[:, 4 * k:4 * k + 4, :].rearrange("p g c -> p (g c)"),
                                  ps[:, b, :], ACT.Copy).then_inc(s5_act, 1)
                elif kind == "v":
                    ac.activation(st[:, 2 * k:2 * k + 2, :, 1:NC + 1],
                                  ps[:, b, :].rearrange("p (q r c) -> p q r c", q=2, r=2), ACT.Copy)\
                        .then_inc(s5_act, 1)
                elif kind == "g":
                    src = ps[:, b, :].rearrange("p (g c) -> p g c", g=4)
                    for q in range(4):
                        ins = ac.activation(gt[32 * q:32 * q + 32, 4 * k:4 * k + 4, 32 * q:P],
                                            src[32 * q:32 * q + 32, :, 0:P - 32 * q], ACT.Copy)
                    ins.then_inc(s5_act, 1)
                elif kind == "y":
                    o = z[:, hf, :, 64 * k:64 * k + 64].rearrange("p j (s x) -> p s j x", x=CH)
                    ac.activation(o, ps[:, b, :].rearrange("p (s j x) -> p s j x", s=4, x=CH),
                                  ACT.Gelu_apprx_tanh).then_inc(s5_act, 1)
                else:
                    o = x_hi[:, k // 2, :].rearrange("p (c j) -> p j c", j=T)
                    o = o[:, 4 * (k % 2):4 * (k % 2) + 4, :]
                    ins = ac.activation(o, ps[:, b, :].rearrange("p (j c) -> p j c", j=4), ACT.Copy)
                    ins.then_inc(act_ev, A_GLU) if k == 15 else ins.then_inc(z_hi, 1)

            s5_batches(ac, [(kind, hf) for kind in ("wt", "v", "g", "y", "z") for hf in range(2)], batch)

            def gates(i):
                for x in range(2):
                    ac.wait_ge(tile, i * 4 + (T_GLU + 1 + 2 * x))
                    if not isinstance(i, int):
                        ac.wait_ge(dve_ev, i * 2 + (D_GLU - 1 + x))
                    ac.activation(wide(sg[x][:, :]), two(1 + 2 * x), ACT.Sigmoid).then_inc(act_ev, 1)

            gates(0)
            with ac.Fori(1, 4) as i:
                gates(i)

            def norm(m):
                for k in range(KT):
                    ac.wait_ge(*h_ready(m, k))
                    if k >= 3:
                        ac.wait_ge(nacc, 7 * m + k - 2)
                    ac.activation((tmp[2] if k == 0 else tmp[1 - k % 2])[:, :], h[:, k, :], ACT.Square)\
                        .then_inc(nsq, 1)
                ac.wait_ge(nms, m + 1)
                ac.activation(rt[:, :], ms[:, :], ACT.Sqrt).then_inc(nrt, 1)
                if m < 3:
                    for k in range(KT):
                        ac.wait_ge(nf, KT * m + k + 1)
                        ac.activation(x_hi[:, k, :], tmp[k % 2][:, :], ACT.Copy).then_inc(nhi, 1)

            def ffn(layer, t0, d0):
                def silu(x, at):
                    ac.wait_ge(tile, at)
                    ac.activation(wide(tmp[x][:, :]), two(2 * x), ACT.Silu).then_inc(act_ev, 1)

                def high(x, n):
                    ac.wait_ge(dve_ev, n)
                    ac.activation(hid[0][:, x, :], tmp[2][:, :], ACT.Copy).then_inc(hid_h, 1)

                def body(i, last):
                    high(0, i * 10 + (d0 + 1))
                    silu(1, i * 12 + (t0 + 3))
                    high(1, i * 10 + (d0 + 2))
                    if not last:
                        silu(0, i * 12 + (t0 + 5))

                silu(0, t0 + 1)
                with ac.Fori(0, FP - 1) as i:
                    body(i, False)
                body(FP - 1, True)

            norm(0)
            ffn(0, T_F0, D_F0)
            norm(1)

            def rotated(g, a0, t0):
                def high(n):
                    m = 8 * g + n
                    ac.wait_ge(rsum, m + 1)
                    if m >= 2:
                        ac.wait_ge(stored[n % 2], 32 * (m // 2))
                    ac.activation(rk_hi[n % 2][:, :], rk[n % 2][:, :], ACT.Copy).then_inc(rhi, 1)

                for n in range(8):
                    ac.wait_ge(tile, t0 + n + 1)
                    ac.activation(wide(xk[n % 2][:, :]), two(n % 2), ACT.Copy).then_inc(act_ev, 1)
                    if n:
                        high(n - 1)
                high(7)

            rotated(0, A_KVQ, T_KVQ)
            for c in range(4):
                ac.wait_ge(tile, T_KVQ + 8 + 2 * c + 2)
                if c >= 2:
                    ac.wait_ge(v_stored[c % 2], 16)
                ac.activation(stg[c % 2][:, :, :].rearrange("p (b x) c -> p b (x c)", x=2),
                              ps[:, 4 * (c % 2):4 * (c % 2) + 4, :], ACT.Copy).then_inc(act_ev, 1)
            rotated(1, A_KVQ + 12, T_KVQ + 16)

            def exps(i, q):
                for s, e in enumerate((e1[q], e2[q % 2])):
                    ac.wait_ge(nbd, i * 16 + (2 * q + s + 1))
                    ext = (q + 1) * P
                    ac.activation(e[:, 0:ext],
                                  ps[:, bank(q, s):2 * s + 2, :].rearrange("p b c -> p (b c)")[:, 0:ext],
                                  ACT.Exp, bias=nb[:, 2 * q + s:2 * q + s + 1], scale=SCALE,
                                  accum_out=es[:, 2 * q + s:2 * q + s + 1]).then_inc(exd, 1)

            def turned_p(i, q):
                if isinstance(i, int) and i == 0 and q == 0:
                    ac.wait_ge(stored[0], 256)
                    ac.wait_ge(stored[1], 256)
                for n in pt_of(q):
                    _, k0, cnt = PT_USES[n]
                    c0 = P * (q % 2)
                    ac.wait_ge(pt_tr, i * 12 + (n + 1))
                    ac.activation(pt_hi[:, k0:k0 + cnt, c0:c0 + P],
                                  ps[:, 4 + n % 2, 0:P * cnt].rearrange("p (k c) -> p k c", c=P),
                                  ACT.Copy).then_inc(pth, 1)

            def outputs(i, b):
                ac.wait_ge(pv, i * 4 + (b + 1))
                if b == 0 and not (isinstance(i, int) and i == 0):
                    ac.wait_ge(onl, i)
                o = ps[:, 6 + b % 2, 0:256]
                ac.activation(otf[:, 256 * b:256 * b + 256], o, ACT.Copy).then_inc(oc, 1)
                ac.activation(osq[:, 256 * b:256 * b + 256], o, ACT.Square).then_inc(oq, 1)

            def step(i, q, cur, prev):
                if q == 3 and prev:
                    ac.wait_ge(oms, i)
                    ac.activation(rt[:, :], ms[:, :], ACT.Sqrt).then_inc(ort, 1)
                if cur:
                    exps(i, q)
                if q % 2 == 0 and (cur if q >= 4 else prev):
                    outputs(i, q // 2 - 2) if q >= 4 else outputs(i - 1, q // 2 + 2)
                if cur if q >= 2 else prev:
                    turned_p(i, q - 2) if q >= 2 else turned_p(i - 1, q + 6)
                if q == 3 and prev:
                    ac.wait_ge(onfd, i)
                    ac.wait_ge(onfd, 1)
                    ac.activation(x_hi[:, i - 1, :] if isinstance(i, int) else
                                  x_hi[:, bass.ds(i - 1, 1), :].rearrange("p o c -> p (o c)"),
                                  onf[:, :], ACT.Copy).then_inc(onh, 1)

            def head(i, cur=True, prev=True):
                for q in range(8 if cur else 4):
                    step(i, q, cur, prev)

            head(0, prev=False)
            with ac.Fori(1, NH) as i:
                head(i)
            head(NH, cur=False)
            norm(2)
            ffn(1, T_F1, D_F1)
            norm(3)

        @block.vector
        def _(ve):
            steps = [0]

            def step(ins, wait=True):
                steps[0] += 1
                ins.then_inc(dve, 1)
                if wait:
                    ve.wait_ge(dve, steps[0])

            tt, ts = ve.tensor_tensor, ve.tensor_scalar

            p = lambda n: prm[:, n, :]
            ve.wait_ge(params_in, 16)
            ve.wait_ge(prm_exp, 1)
            step(tt(p(4), p(0), p(3), ALU.mult), False)
            step(tt(p(5), p(1), p(3), ALU.mult))
            ts(p(7), p(5), 1 / (2 * math.pi), MAGIC, ALU.mult, ALU.add).then_inc(prm_arg, 1)
            ve.wait_ge(prm_arg, 1)
            step(ts(p(7), p(7), -MAGIC, None, ALU.add))
            for n, part_pi in enumerate(TWO_PI):
                step(ve.scalar_tensor_tensor(out=p(8), in0=p(7), scalar=-part_pi,
                                             in1=p(5) if n == 0 else p(8), op0=ALU.mult, op1=ALU.add))
            ts(p(8), p(8), PI_F, -PI_F, ALU.min, ALU.max).then_inc(prm_arg, 1)
            step(tt(p(16), p(0), p(0), ALU.mult), False)
            step(tt(p(17), p(1), p(1), ALU.mult))
            step(tt(p(16), p(16), p(17), ALU.add))
            step(ve.reciprocal(p(20), p(16)))
            ve.wait_ge(consts_in, 16 * 9)
            step(tt(lamp[:, :, :], lamv[:, 0:4:2, :], lamv[:, 1:4:2, :], ALU.mult))
            ve.tensor_reduce(lams[:, 0:2], lamp[:, :, :], AX.X, ALU.add).then_inc(lam_d, 1)
            ve.wait_ge(prm_sin, 2)
            ve.wait_ge(prm_exp, 2)
            step(tt(p(11), p(10), p(10), ALU.mult))
            step(ts(p(12), p(11), -2.0, 1.0, ALU.mult, ALU.add))
            step(tt(p(13), p(6), p(12), ALU.mult), False)
            step(tt(p(14), p(6), p(9), ALU.mult))
            step(ts(p(15), p(13), -1.0, None, ALU.add))
            step(tt(p(17), p(15), p(0), ALU.mult), False)
            step(tt(p(18), p(14), p(1), ALU.mult), False)
            step(tt(p(19), p(14), p(0), ALU.mult), False)
            step(tt(p(21), p(15), p(1), ALU.mult))
            step(tt(p(17), p(17), p(18), ALU.add), False)
            step(tt(p(19), p(19), p(21), ALU.subtract))
            step(tt(p(22), p(17), p(20), ALU.mult), False)
            step(tt(p(23), p(19), p(20), ALU.mult))
            step(ts(p(16), p(22), sgn[:, 0:1], -1.0, ALU.mult, ALU.mult), False)
            step(ts(p(17), p(23), sgn[:, 0:1], -1.0, ALU.mult, ALU.mult))
            ve.wait_ge(lam_e, 1)
            step(tt(lams[:, 2:3], lams[:, 1:2], lams[:, 0:1], ALU.subtract), False)
            step(ts(subg[:, :], subg[:, :], 1 - LAM_INIT, None, ALU.mult))
            ts(lams[:, 3:4], lams[:, 2:3], -LAM_INIT, None, ALU.add).then_inc(lam_done, 1)

            def cmul(out, x, y, n, width, temps=pt4):
                t = [temps[m][:, 0:n, 0:width] for m in range(4)]
                yr, yi = (v.to_broadcast([P, n, width]) for v in y)
                step(tt(t[0], x[0], yr, ALU.mult), False)
                step(tt(t[1], x[1], yi, ALU.mult), False)
                step(tt(t[2], x[0], yi, ALU.mult), False)
                step(tt(t[3], x[1], yr, ALU.mult))
                step(tt(out[0], t[0], t[1], ALU.subtract), False)
                step(tt(out[1], t[2], t[3], ALU.add))

            dn = lambda k0, k1: [pw[r][:, k0:k1, :] for r in range(2)]
            up = lambda k0, k1: [pw_8[:, r, k0:k1, :] for r in range(2)]
            step(ve.memset(pw[0][:, 8, :], 1.0), False)
            step(ve.memset(pw[1][:, 8, :], 0.0), False)
            step(ve.tensor_copy(pw[0][:, 7, :], p(13)), False)
            step(ve.tensor_copy(pw[1][:, 7, :], p(14)))
            cmul(dn(6, 7), dn(7, 8), dn(7, 8), 1, NG)
            cmul(dn(4, 6), dn(6, 8), dn(6, 7), 2, NG)
            cmul(dn(0, 4), dn(4, 8), dn(4, 5), 4, NG)
            ve.wait_ge(bc_in, 112)
            ts(c_st[:, :, :], c_st[:, :, :], sgn[:, 0:1], None, ALU.mult).then_inc(prm_done, 1)
            step(tt(b_st[:, :, :], b_st[:, :, :], g_b[:, :, :], ALU.mult), False)
            step(tt(b_sw[:, :, :], b_sw[:, :, :], g_b[:, :, :], ALU.mult))
            step(tt(d_two[:, :], d_two[:, :], g_two[:, :], ALU.mult))
            f_r, f_i, f_rs, f_is = (p(n).unsqueeze(2).to_broadcast([P, NG, CH]) for n in (22, 23, 16, 17))
            step(tt(bt[0][:, :, :], f_r, b_st[:, :, :], ALU.mult), False)
            step(tt(bt[1][:, :, :], f_is, b_sw[:, :, :], ALU.mult), False)
            step(tt(bt[2][:, :, :], f_rs, b_sw[:, :, :], ALU.mult), False)
            step(tt(bt[3][:, :, :], f_i, b_st[:, :, :], ALU.mult))
            step(tt(b_st[:, :, :], bt[0][:, :, :], bt[1][:, :, :], ALU.add), False)
            tt(b_sw[:, :, :], bt[2][:, :, :], bt[3][:, :, :], ALU.subtract).then_inc(prm_done, 1)
            ve.wait_ge(prm_done, 2)
            for r_ in range(2):
                for n in range(2):
                    step(ve.tensor_copy(pw_8[64 * n:64 * n + 64, r_, 0, :], pw[r_][64 * n:64 * n + 64, 0, n:NG:2]),
                         r_ == n == 1)
            cmul(up(1, 2), up(0, 1), up(0, 1), 1, NP)
            cmul(up(2, 4), up(0, 2), up(1, 2), 2, NP)
            cmul(up(4, 8), up(0, 4), up(3, 4), 4, NP)

            def token_rms():
                ve.wait_ge(rms_pe, 1)
                step(ve.tensor_reduce(ssq[:, :], ps[:, 7, :].rearrange("p (g c) -> p c g", c=NC), AX.X,
                                      ALU.add))
                ts(rfull[:, :], ssq[:, :], 1.0 / D, EPS, ALU.mult, ALU.add).then_inc(rms_ms, 1)
                ve.wait_ge(rms_rt, 1)
                ve.reciprocal(rfull[:, :], rfull[:, :]).then_inc(rms_rs, 1)
                ve.wait_ge(rms_rs, 1)
                tt(u[:, 0:44, :], u[:, 0:44, :], rfull[:, :].unsqueeze(1).to_broadcast([P, 44, NC]),
                   ALU.mult).then_inc(u_done, 1)

            for hf in range(2):
                half = slice(HP * hf, HP * hf + HP)
                shape = [P, HP // 2, T, CH]
                if hf:
                    ve.wait_ge(*evacuated(number["wt", 0, 7]))
                for g0 in range(0, HG, HP // 2):
                    g = slice(HG * hf + g0, HG * hf + g0 + HP // 2)
                    pr, pi = (x[:, 1:T + 1, g].rearrange("p k q -> p q k").unsqueeze(3)
                              .to_broadcast(shape) for x in pw)
                    b_1, b_2 = (x[:, g, :].unsqueeze(2).to_broadcast(shape) for x in (b_st, b_sw))
                    step(tt(m1[:, :, :, :], pr, b_1, ALU.mult), False)
                    step(tt(m2[:, :, :, :], pi, b_2, ALU.mult))
                    ins = tt(tw[:, g0:g0 + HP // 2, :, :], m1[:, :, :, :], m2[:, :, :, :], ALU.add)
                    if g0 + HP // 2 < HG:
                        step(ins)
                ins.then_inc(w_tab, 1)
                ve.wait_ge(w_tab, hf + 1)
                if hf == 0:
                    token_rms()
                else:
                    ve.wait_ge(s5_full, number["g", 0, 7] + 1)
                tt(dd[:, :, :], ident[0:32, 0:32].unsqueeze(1).to_broadcast([32, HG, 32]),
                   d_two[:, HG * hf:HG * hf + HG].unsqueeze(2).to_broadcast([32, HG, 32]),
                   ALU.mult).then_inc(dd_done, 1)
                if hf == 0:
                    far = lambda n: [pw_x[:, r, n:n + 1, :] for r in range(2)]
                    cmul(far(0), up(7, 8), up(7, 8), 1, NP, pt_x)
                    cmul(far(1), far(0), far(0), 1, NP, pt_x)
                    cmul(far(2), far(1), far(1), 1, NP, pt_x)
                if hf:
                    ve.wait_ge(s5_full, number["y", 0, 7] + 1)
                for g0 in range(HP, HG, HP // 2):
                    g = slice(HG * hf + g0, HG * hf + g0 + HP // 2)
                    pr, pi = (x[:, T - 1::-1, g].rearrange("p k q -> p q k").unsqueeze(3)
                              .to_broadcast(shape) for x in pw)
                    c_1, c_2 = (x[:, g, :].unsqueeze(2).to_broadcast(shape) for x in (c_st, c_sw))
                    step(tt(m1[:, :, :, :], pr, c_1, ALU.mult), False)
                    step(tt(m2[:, :, :, :], pi, c_2, ALU.mult))
                    ins = tt(tc[:, g0:g0 + HP // 2, 1:T + 1, :], m1[:, :, :, :], m2[:, :, :, :], ALU.subtract)
                    if g0 + HP // 2 < HG:
                        step(ins)
                ins.then_inc(c_dve, 1)

                if hf == 0:
                    step(ve.memset(st[:, :, :, 0:1], 0.0))
                ve.wait_ge(*evacuated(number["v", hf, 7]))
                S = st[:, :, :, 1:NC + 1].rearrange("p q i (m r) -> p q i m r", r=R)

                def advance(cur, prev, power, m0, m):
                    a_r, a_i = ((pw_8[:, n, power - 1, half] if power <= R else
                                 pw_x[:, n, {16: 0, 32: 1, 64: 2}[power], half]) for n in range(2))
                    both = a_r.unsqueeze(2).unsqueeze(3).to_broadcast([P, HP, 2, m])
                    one = a_i.unsqueeze(2).to_broadcast([P, HP, m])
                    x, y = ta[:, :, :, 0:m], tb[:, :, :, 0:m]
                    step(tt(x, prev, both, ALU.mult), False)
                    step(ve.scalar_tensor_tensor(out=y[:, :, 0, :], in0=prev[:, :, 1, :], scalar=-1.0,
                                                 in1=one, op0=ALU.mult, op1=ALU.mult), False)
                    step(tt(y[:, :, 1, :], prev[:, :, 0, :], one, ALU.mult))
                    step(tt(cur, cur, x, ALU.add))
                    step(tt(cur, cur, y, ALU.add))

                for r in range(1, R):
                    advance(S[:, :, :, :, r], S[:, :, :, :, r - 1], 1, 0, M)
                for d in (1, 2, 4, 8):
                    advance(S[:, :, :, d:M, R - 1], S[:, :, :, 0:M - d, R - 1], R * d, 0, M - d)
                for r in range(R - 1):
                    advance(S[:, :, :, 1:M, r], S[:, :, :, 0:M - 1, R - 1], r + 1, 0, M - 1)
                ve.tensor_copy(ta[:, 0, 0, 0:1], ta[:, 0, 0, 0:1]).then_inc(scan_done, 1)
                ve.wait_ge(scan_done, hf + 1)

            for k in range(16):
                n = number["z", 0, k]
                ve.wait_ge(s5_full, n + 1)
                ve.wait_ge(act_ev, A_GLU) if k == 15 else ve.wait_ge(z_hi, k + 1)
                o, i_ = (x[:, k // 2, :].rearrange("p (c j) -> p j c", j=T)
                         [:, 4 * (k % 2):4 * (k % 2) + 4, :] for x in (x_lo, x_hi))
                ins = tt(o, ps[:, n % 8, :].rearrange("p (j c) -> p j c", j=4), i_, ALU.subtract)
                ins.then_inc(dve_ev, D_GLU) if k == 15 else ins.then_inc(s5_dve, 1)

            ve.wait_ge(h_in, 16)
            def accumulated(m, k):
                ve.wait_ge(nsq, KT * m + k + 1)
                if k >= 2:
                    ve.wait_ge(nacc, 7 * m + k - 1)
                tt(tmp[2][:, :], tmp[2][:, :], tmp[1 - k % 2][:, :], ALU.add).then_inc(nacc, 1)

            def glu(i, x):
                ve.wait_ge(tile, i * 4 + (T_GLU + 2 + 2 * x))
                ve.wait_ge(act_ev, i * 2 + (A_GLU + 1 + x))
                tt(wide(glu_v[:, :]), two(2 * x), wide(sg[x][:, :]), ALU.mult).then_inc(dve_ev, 1)
                ve.wait_ge(dve_ev, i * 2 + (D_GLU + 1 + x))
                hk = h[:, bass.ds(i * 2 + x, 1), :].rearrange("p o c -> p (o c)")
                tt(hk, hk, glu_v[:, :], ALU.add).then_inc(h_add, 1)
                ve.wait_ge(h_add, i * 2 + (x + 1))

            with ve.Fori(0, 3) as i:
                for x in range(2):
                    glu(i, x)
            glu(3, 0)
            for k in range(1, KT - 1):
                accumulated(0, k)
            glu(3, 1)

            def norm(m, gain, k0):
                for k in range(k0, KT):
                    accumulated(m, k)
                ve.wait_ge(ncol, m + 1)
                ts(ms[:, :], ps[:, 7, 0:KT], 1.0 / D, EPS, ALU.mult, ALU.add).then_inc(nms, 1)
                ve.wait_ge(nrt, m + 1)
                ve.reciprocal(rs[:, :], rt[:, :]).then_inc(nrs, 1)
                ve.wait_ge(nbc, m + 1)

                def full(k):
                    if m == 3 and k >= 2:
                        ve.wait_ge(out_done[k % 2], 16 * (k // 2))
                    if m < 3 and k >= 2:
                        ve.wait_ge(nlo, KT * m + k - 1)
                    ve.scalar_tensor_tensor(out=wide(tmp[k % 2][:, :]), in0=wide(h[:, k, :]),
                                            scalar=1.0 if gain is None else gains[:, gain, k:k + 1],
                                            in1=two(3), op0=ALU.mult, op1=ALU.mult).then_inc(nf, 1)

                def low(k):
                    ve.wait_ge(nhi, KT * m + k + 1)
                    tt(x_lo[:, k, :], tmp[k % 2][:, :], x_hi[:, k, :], ALU.subtract).then_inc(nlo, 1)

                full(0)
                for k in range(KT):
                    if k + 1 < KT:
                        full(k + 1)
                    if m < 3:
                        low(k)

            def ffn(layer, t0, d0, a0):
                n = 2 * FP * layer

                def body(i, last):
                    for x in range(2):
                        ve.wait_ge(tile, i * 12 + (t0 + 2 + 2 * x))
                        ve.wait_ge(act_ev, i * 2 + (a0 + 1 + x))
                        tt(wide(tmp[2][:, :]), two(1 + 2 * x), wide(tmp[x][:, :]), ALU.mult)\
                            .then_inc(dve_ev, 1)
                        ve.wait_ge(hid_h, i * 2 + (n + 1 + x))
                        tt(hid[1][:, x, :], tmp[2][:, :], hid[0][:, x, :], ALU.subtract).then_inc(hid_l, 1)
                        ve.wait_ge(hid_l, i * 2 + (n + 1 + x))
                    for k in range(KT):
                        ve.wait_ge(tile, i * 12 + (t0 + 6 + k) if not last else i * 12 + (t0 + 5 + k))
                        hk = wide(h[:, k, :])
                        tt(hk, hk, two((1, 2, 3, 0)[k % 4]), ALU.add).then_inc(dve_ev, 1)
                        if last and k >= 2:
                            accumulated(2 * layer + 1, k - 1)

                return body

            def run_ffn(layer, t0, d0, a0):
                body = ffn(layer, t0, d0, a0)
                with ve.Fori(0, FP - 1) as i:
                    body(i, False)
                body(FP - 1, True)

            norm(0, 0, KT - 1)
            run_ffn(0, T_F0, D_F0, A_F0)
            norm(1, None, KT - 1)

            ve.wait_ge(rot_in, 32)

            def rotated(g, a0):
                def low(n):
                    m = 8 * g + n
                    ve.wait_ge(rhi, m + 1)
                    if m >= 2:
                        ve.wait_ge(stored[n % 2], 32 * (m // 2))
                    tt(rk_lo[n % 2][:, :], rk[n % 2][:, :], rk_hi[n % 2][:, :], ALU.subtract)\
                        .then_inc(rlo, 1)

                for n in range(8):
                    m, x, y = 8 * g + n, xk[n % 2], rk[n % 2]
                    ve.wait_ge(act_ev, a0 + n + 1)
                    if m >= 2:
                        ve.wait_ge(rlo, m - 1)
                    step(tt(y[:, :], x[:, :], cos_t[:, :], ALU.mult))
                    ve.wait_ge(rotp, m + 1)
                    tt(wide(x[:, :]), two(2 + n % 2), wide(sin_t[:, :]), ALU.mult).then_inc(dve_ev, 1)
                    ve.wait_ge(dve_ev, D_KVQ + m + 1)
                    tt(y[:, :], y[:, :], x[:, :], ALU.add).then_inc(rsum, 1)
                    if n:
                        low(n - 1)
                low(7)

            rotated(0, A_KVQ)
            rotated(1, A_KVQ + 12)

            def maxima(i, q):
                for s in range(2):
                    n, ext = 2 * q + s, (q + 1) * P
                    flat = ps[:, bank(q, s):2 * s + 2, :].rearrange("p b c -> p (b c)")
                    ve.wait_ge(sc, i * 16 + (n + 1))
                    ve.memset(flat[0:64, ext - 64:ext], NEG).then_inc(masked, 1)
                    ve.wait_ge(masked, i * 16 + (n + 1))
                    ve.tensor_reduce(mx[:, n:n + 1], flat[:, 0:ext], AX.X, ALU.max).then_inc(mxd, 1)
                    ve.wait_ge(mxd, i * 16 + (n + 1))
                    ts(nb[:, n:n + 1], mx[:, n:n + 1], -SCALE, None, ALU.mult).then_inc(nbd, 1)

            def combined(i, q):
                ve.wait_ge(exd, i * 16 + (2 * q + 2))
                ve.reciprocal(er[:, 2 * q:2 * q + 2], es[:, 2 * q:2 * q + 2]).then_inc(er_done, 1)
                ve.wait_ge(er_done, i * 8 + (q + 1))
                ve.scalar_tensor_tensor(out=ec[:, q:q + 1], in0=es[:, 2 * q:2 * q + 1],
                                        scalar=er[:, 2 * q + 1:2 * q + 2], in1=lams[:, 3:4],
                                        op0=ALU.mult, op1=ALU.mult).then_inc(ec_done, 1)
                ts(dg[q % 4][:, :], ident[:, :], er[:, 2 * q:2 * q + 1], None, ALU.mult)
                ve.wait_ge(ec_done, i * 8 + (q + 1))
                p1_, p2_ = (e[:, 0:(q + 1) * P] for e in (e1[q], e2[q % 2]))
                ve.scalar_tensor_tensor(out=p1_, in0=p2_, scalar=ec[:, q:q + 1], in1=p1_,
                                        op0=ALU.mult, op1=ALU.add).then_inc(p_done, 1)

            def turned_p(i, q):
                for n in pt_of(q):
                    _, k0, cnt = PT_USES[n]
                    c0 = P * (q % 2)
                    ve.wait_ge(pth, i * 12 + (n + 1))
                    if q % 2 == 0 and k0 == 0:
                        ve.memset(pt_hi[:, q + 1, 0:P].bitcast(F32), 0.0)
                        ve.memset(pt_lo[:, q + 1, 0:P].bitcast(F32), 0.0)
                    tt(pt_lo[:, k0:k0 + cnt, c0:c0 + P],
                       ps[:, 4 + n % 2, 0:P * cnt].rearrange("p (k c) -> p k c", c=P),
                       pt_hi[:, k0:k0 + cnt, c0:c0 + P], ALU.subtract).then_inc(ptl, 1)

            def step_(i, q, cur, prev):
                if q == 3 and prev:
                    ve.wait_ge(ocol, i)
                    ts(ms[:, :], ps[:, 7, 0:KT], 1.0 / VD, EPS, ALU.mult, ALU.add).then_inc(oms, 1)
                if q == 3 and prev:
                    ve.wait_ge(ort, i)
                    ve.reciprocal(rs[:, :], rt[:, :]).then_inc(ors, 1)
                if cur:
                    maxima(i, q)
                if cur if q else prev:
                    combined(i, q - 1) if q else combined(i - 1, 7)
                if cur if q >= 2 else prev:
                    turned_p(i, q - 2) if q >= 2 else turned_p(i - 1, q + 6)
                if q == 3 and prev:
                    ve.wait_ge(obc, i)
                    ve.scalar_tensor_tensor(out=wide(onf[:, :]), in0=wide(otf[:, :]), scalar=subg[:, 0:1],
                                            in1=two(3), op0=ALU.mult, op1=ALU.mult).then_inc(onfd, 1)

            def head(i, cur=True, prev=True):
                for q in range(8 if cur else 4):
                    step_(i, q, cur, prev)

            ve.wait_ge(lam_done, 1)
            head(0, prev=False)
            with ve.Fori(1, NH) as i:
                head(i)
            head(NH, cur=False)

            for k in range(KT):
                ve.wait_ge(tile, T_WO + k + 1)
                hk = wide(h[:, k, :])
                tt(hk, hk, two(k % 4), ALU.add).then_inc(dve_ev, 1)
                if k >= 2:
                    accumulated(2, k - 1)
            norm(2, 3, KT - 1)
            run_ffn(1, T_F1, D_F1, A_F1)
            norm(3, 4, KT - 1)


def kernel(**inputs):
    import concourse.bacc as _bacc
    from concourse.bass_utils import run_bass_kernel_spmd as _run

    i = {k: np.asarray(v) for k, v in inputs.items()}

    def states(x):
        return np.concatenate([x.T] * 2, 0)

    def cols(w):
        k, n = w.shape
        return w.reshape(k // P, P, n // 256, 256).transpose(2, 1, 0, 3).reshape(n // 256, P, -1)

    def tiles(g):
        return g.reshape(KT, P).T

    x = i["x"][0]
    lr, li = states(i["ssm_lam_re"][0]), states(i["ssm_lam_im"][0])
    dt = states(np.broadcast_to(i["ssm_log_dt"][0][:, None], (NG, 64)))
    b_re, b_im = (i[f"ssm_b_{n}"][0].transpose(1, 0, 2) for n in ("re", "im"))
    c_re, c_im = (i[f"ssm_c_{n}"][0].transpose(2, 0, 1) for n in ("re", "im"))
    pos = np.arange(L, dtype=np.float32)
    freq = np.float32(500000.0) ** (-np.arange(8, dtype=np.float32) * np.float32(2.0) / np.float32(16))
    ang = (freq[:, None] * pos[None, :]).astype(np.float32)
    rest = np.zeros((48, L), np.float32)
    cos_t = np.concatenate([np.cos(ang), np.cos(ang), rest + 1] * 2)
    sin_t = np.concatenate([np.sin(ang), np.sin(ang), rest] * 2)
    perm = np.zeros((P, P), np.float32)
    for d in range(8):
        for r0 in (0, 64):
            perm[r0 + d + 8, r0 + d], perm[r0 + d, r0 + d + 8] = -1, 1
    data = {
        "ident": np.eye(P, dtype=np.float32),
        "ident4": np.tile(np.eye(32, dtype=np.float32), (1, 4)),
        "same_j": np.kron(np.eye(T), np.ones((CH, CH))).astype(np.float32),
        "ones": np.ones((P, 1), np.float32),
        "gains": np.stack([tiles(i["norm_ffn_g"][0]), tiles(i["kv_norm_g"]), tiles(i["norm_mix_g"][1]),
                           tiles(i["norm_ffn_g"][1]), tiles(i["final_norm_g"])], 1),
        "subg": i["attn_subln_g"][0][:, None],
        "cos_t": cos_t, "sin_t": sin_t, "perm": perm,
        "lamv": np.broadcast_to(np.stack([i[f"attn_{n}"][0] for n in ("lq1", "lk1", "lq2", "lk2")])[None],
                                (P, 4, 64)),
        "ssm_prm": np.stack([lr, li, dt], 1),
        "x_u": x.reshape(NC, T, NG, CH).transpose(1, 3, 2, 0).reshape(P, NG, NC),
        "x_t": x.T.reshape(KT, P, L).transpose(1, 0, 2),
        "ssm_b_st": np.concatenate([b_re, b_im]), "ssm_b_sw": np.concatenate([b_im, b_re]),
        "ssm_c_st": np.concatenate([c_re, c_im]), "ssm_c_sw": np.concatenate([c_im, c_re]),
        "g_b": np.broadcast_to(i["norm_mix_g"][0].reshape(1, NG, CH), (P, NG, CH)),
        "sgn": np.concatenate([np.ones((64, 1), np.float32), -np.ones((64, 1), np.float32)]),
        "d_two": np.concatenate([i["ssm_d"][0].reshape(NG, CH).T] * 2, 0),
        "g_two": np.concatenate([i["norm_mix_g"][0].reshape(NG, CH).T] * 2, 0),
        "glu_a": cols(i["ssm_w_glu"][0][:, :D]), "glu_b": cols(i["ssm_w_glu"][0][:, D:]),
        "w_kvq": cols(np.concatenate([i["w_kv"], i["attn_w_q"][0]], 1)),
        "w_o": cols(i["attn_w_o"][0]),
    }
    for n in range(2):
        data[f"w1_{n}"] = cols(i["ffn_w1"][n])
        data[f"w3_{n}"] = cols(i["ffn_w3"][n])
        data[f"w2_{n}"] = i["ffn_w2"][n].reshape(FP, 2, P, D).transpose(0, 2, 1, 3).reshape(FP, P, 2 * D)

    nc = _bacc.Bacc("TRN2", target_bir_lowering=False, num_devices=1)
    arrays, aps = {}, {}
    for name, v in data.items():
        v = np.ascontiguousarray(v)
        arrays[f"in_{name}"] = v
        aps[name] = nc.dram_tensor(f"in_{name}", v.shape, mybir.dt.from_np(v.dtype), kind="ExternalInput").ap()
    out = nc.dram_tensor("out_t", (P, KT, L), F32, kind="ExternalOutput").ap()
    trunk(nc, aps, out)
    r = _run(nc, [arrays], core_ids=[0])
    return r.results[0]["out_t"].transpose(2, 1, 0).reshape(1, L, D)
```
